# Optimizing a Trainium2 kernel written in Bass

```python
import math
import jax, jax.numpy as jnp
from jax import lax
import numpy as np

D_MODEL = 2048
BATCH = 1
SEQ = 512
DEPTH = 1

N_MIXERS = 3
HEAD_DIM = 64
N_HEADS = D_MODEL // HEAD_DIM
BRANCH = N_HEADS * HEAD_DIM
N_KV_A = N_HEADS // 8
KV_A = N_KV_A * HEAD_DIM
WINDOW = 128
BLOCK = 128
NORM_EPS = 1e-6
NEG = -1e30

A_COLS = BRANCH + 2 * KV_A + BRANCH
B_COLS = 4 * BRANCH
C_COLS = 4 * BRANCH + N_HEADS


def _n_layers_of(kind):
    return sum(1 for i in range(DEPTH) if i % N_MIXERS == kind)

def _alibi_slopes(n):
    return jnp.asarray(2.0 ** (-8.0 * np.arange(1, n + 1, dtype=np.float32) / n), dtype=jnp.float32)

def rmsnorm(x, g):
    xf = x.astype(jnp.float32)
    r = lax.rsqrt(jnp.mean(xf * xf, axis=-1, keepdims=True) + NORM_EPS)
    return (xf * r * g.astype(jnp.float32)).astype(x.dtype)

def swa_sink_mixer(h, w_in, sinks):
    B, S, _ = h.shape
    nb = S // BLOCK
    G = N_HEADS // N_KV_A
    q, k, v, z = jnp.split(h @ w_in, [BRANCH, BRANCH + KV_A, BRANCH + 2 * KV_A], axis=-1)
    q = q.reshape(B, nb, BLOCK, N_KV_A, G, HEAD_DIM).astype(jnp.float32)
    k = k.reshape(B, nb, BLOCK, N_KV_A, HEAD_DIM).astype(jnp.float32)
    v = v.reshape(B, nb, BLOCK, N_KV_A, HEAD_DIM).astype(jnp.float32)

    def band(a):
        prev = jnp.concatenate([jnp.zeros_like(a[:, :1]), a[:, :-1]], axis=1)
        return jnp.concatenate([prev, a], axis=2)

    kb, vb = band(k), band(v)
    scores = jnp.einsum('bnqhgd,bnkhd->bnhgqk', q, kb) * (HEAD_DIM ** -0.5)
    qi = jnp.arange(BLOCK)[:, None]
    kj = jnp.arange(2 * BLOCK)[None, :]
    dist = (qi + BLOCK - kj).astype(jnp.float32)
    s_pos = jnp.arange(nb)[:, None, None] * BLOCK - BLOCK + kj[None]
    valid = (dist >= 0) & (dist < WINDOW) & (s_pos >= 0)
    slopes = _alibi_slopes(N_HEADS).reshape(N_KV_A, G)
    scores = scores - slopes[:, :, None, None] * dist
    scores = jnp.where(valid[None, :, None, None], scores, NEG)
    sink = sinks.astype(jnp.float32).reshape(N_KV_A, G)
    sink_col = jnp.broadcast_to(sink[None, None, :, :, None, None], scores.shape[:-1] + (1,))
    p = jax.nn.softmax(jnp.concatenate([scores, sink_col], axis=-1), axis=-1)[..., :-1]
    o = jnp.einsum('bnhgqk,bnkhd->bnqhgd', p, vb).reshape(B, S, BRANCH)
    return o, z

def stick_breaking_mixer(h, w_in):
    B, S, _ = h.shape
    nb = S // BLOCK
    q, k, v, z = jnp.split(h @ w_in, 4, axis=-1)
    q = q.reshape(B, nb, BLOCK, N_HEADS, HEAD_DIM).transpose(1, 0, 3, 2, 4).astype(jnp.float32)
    k = k.reshape(B, S, N_HEADS, HEAD_DIM).astype(jnp.float32)
    v = v.reshape(B, S, N_HEADS, HEAD_DIM).astype(jnp.float32)
    s_pos = jnp.arange(S)
    scale = HEAD_DIM ** -0.5

    def block(args):
        qb, n = args
        t_pos = n * BLOCK + jnp.arange(BLOCK)
        logits = jnp.einsum('bhqd,bshd->bhqs', qb, k) * scale
        before = s_pos[None, :] < t_pos[:, None]
        log_fail = jnp.where(before, jax.nn.log_sigmoid(-logits), 0.0)
        incl = lax.cumsum(log_fail, axis=3, reverse=True)
        suffix = jnp.concatenate([incl[..., 1:], jnp.zeros_like(incl[..., :1])], axis=-1)
        a = jnp.where(before, jnp.exp(jax.nn.log_sigmoid(logits) + suffix), 0.0)
        return jnp.einsum('bhqs,bshd->bqhd', a, v)

    o = lax.map(block, (q, jnp.arange(nb)))
    o = o.transpose(1, 0, 2, 3, 4).reshape(B, S, BRANCH)
    return o, z

def forgetting_mixer(h, w_in, b_f):
    B, S, _ = h.shape
    nb = S // BLOCK
    q, k, v, z, f_logit = jnp.split(h @ w_in, [BRANCH, 2 * BRANCH, 3 * BRANCH, 4 * BRANCH], axis=-1)
    log_f = jax.nn.log_sigmoid(f_logit.astype(jnp.float32) + b_f.astype(jnp.float32))
    cum = lax.cumsum(log_f, axis=1).transpose(0, 2, 1)
    q = q.reshape(B, nb, BLOCK, N_HEADS, HEAD_DIM).transpose(1, 0, 3, 2, 4).astype(jnp.float32)
    cq = cum.reshape(B, N_HEADS, nb, BLOCK).transpose(2, 0, 1, 3)
    k = k.reshape(B, S, N_HEADS, HEAD_DIM).astype(jnp.float32)
    v = v.reshape(B, S, N_HEADS, HEAD_DIM).astype(jnp.float32)
    s_pos = jnp.arange(S)
    scale = HEAD_DIM ** -0.5

    def block(args):
        qb, cqb, n = args
        t_pos = n * BLOCK + jnp.arange(BLOCK)
        logits = jnp.einsum('bhqd,bshd->bhqs', qb, k) * scale + cqb[..., :, None] - cum[:, :, None, :]
        causal = s_pos[None, :] <= t_pos[:, None]
        p = jax.nn.softmax(jnp.where(causal, logits, NEG), axis=-1)
        return jnp.einsum('bhqs,bshd->bqhd', p, v)

    o = lax.map(block, (q, cq, jnp.arange(nb)))
    o = o.transpose(1, 0, 2, 3, 4).reshape(B, S, BRANCH)
    return o, z

def first_inputs(seed: int = 0) -> dict:
    key = jax.random.key(seed)
    ks = jax.random.split(key, 12)
    n_a, n_b, n_c = _n_layers_of(0), _n_layers_of(1), _n_layers_of(2)
    f32 = jnp.float32
    nrm = jax.random.normal
    return {
        "x": nrm(ks[0], (BATCH, SEQ, D_MODEL), f32),
        "g_pre": 1.0 + 0.02 * nrm(ks[1], (DEPTH, D_MODEL), f32),
        "g_post": 1.0 + 0.02 * nrm(ks[2], (DEPTH, D_MODEL), f32),
        "w_in_a": nrm(ks[3], (n_a, D_MODEL, A_COLS), f32) * D_MODEL ** -0.5,
        "w_out_a": nrm(ks[4], (n_a, BRANCH, D_MODEL), f32) * BRANCH ** -0.5,
        "sinks_a": 0.5 * nrm(ks[5], (n_a, N_HEADS), f32),
        "w_in_b": nrm(ks[6], (n_b, D_MODEL, B_COLS), f32) * D_MODEL ** -0.5,
        "w_out_b": nrm(ks[7], (n_b, BRANCH, D_MODEL), f32) * BRANCH ** -0.5,
        "w_in_c": nrm(ks[8], (n_c, D_MODEL, C_COLS), f32) * D_MODEL ** -0.5,
        "b_f_c": 1.0 + 5.0 * jax.random.uniform(ks[9], (n_c, N_HEADS), f32),
        "w_out_c": nrm(ks[10], (n_c, BRANCH, D_MODEL), f32) * BRANCH ** -0.5,
    }

def first_block(x, g_pre, g_post, w_in_a, w_out_a, sinks_a, w_in_b, w_out_b, w_in_c, b_f_c, w_out_c):
    for i in range(DEPTH):
        kind, j = i % N_MIXERS, i // N_MIXERS
        h = rmsnorm(x, g_pre[i])
        if kind == 0:
            o, z = swa_sink_mixer(h, w_in_a[j], sinks_a[j])
            w_out = w_out_a[j]
        elif kind == 1:
            o, z = stick_breaking_mixer(h, w_in_b[j])
            w_out = w_out_b[j]
        else:
            o, z = forgetting_mixer(h, w_in_c[j], b_f_c[j])
            w_out = w_out_c[j]
        y = (o.astype(z.dtype) * jax.nn.silu(z)) @ w_out
        x = x + rmsnorm(y, g_post[i])
    return x


DEPTH_2 = 2

MEM_TOKENS = 256
EPS = 1e-6
ROPE_THETA = 10000.0
Q_BLOCK = 128
MLA_HEADS = D_MODEL // 256
QK_NOPE_DIM = 128
QK_ROPE_DIM = 64
QK_HEAD_DIM = QK_NOPE_DIM + QK_ROPE_DIM
V_HEAD_DIM = 128
Q_LORA_RANK = D_MODEL // 4
KV_LORA_RANK = D_MODEL // 8
MLA_WIDTH = MLA_HEADS * V_HEAD_DIM
CONV_WIDTH = D_MODEL // 4
CONV_K = 3
MEM_HEADS = 4
MEM_HEAD_DIM = D_MODEL // 16
MEM_WIDTH = MEM_HEADS * MEM_HEAD_DIM
MIX_WIDTH = MLA_WIDTH + CONV_WIDTH + MEM_WIDTH
IN_SPLITS = (Q_LORA_RANK, KV_LORA_RANK, QK_ROPE_DIM, CONV_WIDTH, CONV_WIDTH, CONV_WIDTH, MEM_WIDTH, MIX_WIDTH)
IN_COLS = Q_LORA_RANK + KV_LORA_RANK + QK_ROPE_DIM + 3 * CONV_WIDTH + MEM_WIDTH + MIX_WIDTH


def rmsnorm_2(x, g):
    x32 = x.astype(jnp.float32)
    y = x32 * lax.rsqrt(jnp.mean(x32 * x32, axis=-1, keepdims=True) + EPS)
    return (y * g.astype(jnp.float32)).astype(x.dtype)

def rope_tables(positions):
    inv_freq = 1.0 / (ROPE_THETA ** (jnp.arange(0, QK_ROPE_DIM, 2, dtype=jnp.float32) / QK_ROPE_DIM))
    ang = positions.astype(jnp.float32)[..., None] * inv_freq
    return jnp.cos(ang), jnp.sin(ang)

def apply_rope(x, cos, sin):
    half = x.shape[-1] // 2
    x32 = x.astype(jnp.float32)
    x1, x2 = x32[..., :half], x32[..., half:]
    return jnp.concatenate([x1 * cos - x2 * sin, x2 * cos + x1 * sin], axis=-1).astype(x.dtype)

def split_cols(z):
    idx = list(np.cumsum(IN_SPLITS)[:-1])
    return jnp.split(z, idx, axis=-1)

def mla_attention(q, k, v):
    b, s, h, dq = q.shape
    nb = s // Q_BLOCK
    scale = QK_HEAD_DIM ** -0.5
    qb = q.reshape(b, nb, Q_BLOCK, h, dq).transpose(1, 0, 2, 3, 4)

    def block(qi):
        sc = jnp.einsum('bqhd,bkhd->bhqk', qi, k).astype(jnp.float32) * scale
        p = jax.nn.softmax(sc, axis=-1).astype(v.dtype)
        return jnp.einsum('bhqk,bkhd->bqhd', p, v)

    o = lax.map(block, qb)
    return o.transpose(1, 0, 2, 3, 4).reshape(b, s, h * V_HEAD_DIM)

def short_gated_conv(gb, gc, xin, w):
    u = gc * xin
    up = jnp.pad(u, ((0, 0), (1, 1), (0, 0)))
    conv = up[:, :-2] * w[0] + up[:, 1:-1] * w[1] + up[:, 2:] * w[2]
    return gb * conv

def memory_attention(q, mem_n, w_mk, w_mv):
    b, m, _ = mem_n.shape
    mk = (mem_n @ w_mk).reshape(b, m, MEM_HEADS, MEM_HEAD_DIM)
    mv = (mem_n @ w_mv).reshape(b, m, MEM_HEADS, MEM_HEAD_DIM)
    sc = jnp.einsum('bshd,bmhd->bhsm', q, mk).astype(jnp.float32) * (MEM_HEAD_DIM ** -0.5)
    p = jax.nn.softmax(sc, axis=-1).astype(mv.dtype)
    o = jnp.einsum('bhsm,bmhd->bshd', p, mv)
    return o.reshape(b, q.shape[1], MEM_WIDTH)

def second_inputs(seed: int = 0) -> dict:
    key = jax.random.key(seed)
    ks = jax.random.split(key, 16)
    f32 = jnp.float32

    def w(k, shape, fan_in):
        return jax.random.normal(k, shape, f32) * (fan_in ** -0.5)

    def gain(k, shape):
        return 1.0 + 0.02 * jax.random.normal(k, shape, f32)

    x = jax.random.normal(ks[0], (BATCH, SEQ, D_MODEL), f32)
    mem = jax.random.normal(ks[1], (BATCH, MEM_TOKENS, D_MODEL), f32)
    offset = jax.random.randint(ks[2], (BATCH, 1), 0, 4096, dtype=jnp.int32)
    positions = (offset + jnp.arange(SEQ, dtype=jnp.int32)[None, :]).astype(jnp.int32)
    return {
        "x": x,
        "mem": mem,
        "positions": positions,
        "pre_norm_g": gain(ks[3], (DEPTH_2, D_MODEL)),
        "w_in": w(ks[4], (DEPTH_2, D_MODEL, IN_COLS), D_MODEL),
        "q_norm_g": gain(ks[5], (DEPTH_2, Q_LORA_RANK)),
        "w_uq": w(ks[6], (DEPTH_2, Q_LORA_RANK, MLA_HEADS * QK_HEAD_DIM), Q_LORA_RANK),
        "kv_norm_g": gain(ks[7], (DEPTH_2, KV_LORA_RANK)),
        "w_ukv": w(ks[8], (DEPTH_2, KV_LORA_RANK, MLA_HEADS * (QK_NOPE_DIM + V_HEAD_DIM)), KV_LORA_RANK),
        "conv_w": w(ks[9], (DEPTH_2, CONV_K, CONV_WIDTH), CONV_K),
        "mem_norm_g": gain(ks[10], (DEPTH_2, D_MODEL)),
        "w_mk": w(ks[11], (DEPTH_2, D_MODEL, MEM_WIDTH), D_MODEL),
        "w_mv": w(ks[12], (DEPTH_2, D_MODEL, MEM_WIDTH), D_MODEL),
        "w_o": w(ks[13], (DEPTH_2, MIX_WIDTH, D_MODEL), MIX_WIDTH),
        "post_norm_g": gain(ks[14], (DEPTH_2, D_MODEL)),
    }

def second_block(x, mem, positions, pre_norm_g, w_in, q_norm_g, w_uq, kv_norm_g, w_ukv, conv_w,
              mem_norm_g, w_mk, w_mv, w_o, post_norm_g):
    b, s, _ = x.shape
    cos, sin = rope_tables(positions)
    for l in range(DEPTH_2):
        h = rmsnorm_2(x, pre_norm_g[l])
        z = h @ w_in[l]
        q_lat, kv_lat, k_pe, gb, gc, xin, q_mem, gate = split_cols(z)

        q = (rmsnorm_2(q_lat, q_norm_g[l]) @ w_uq[l]).reshape(b, s, MLA_HEADS, QK_HEAD_DIM)
        q = jnp.concatenate([q[..., :QK_NOPE_DIM],
                             apply_rope(q[..., QK_NOPE_DIM:], cos[:, :, None, :], sin[:, :, None, :])], axis=-1)
        kv = (rmsnorm_2(kv_lat, kv_norm_g[l]) @ w_ukv[l]).reshape(b, s, MLA_HEADS, QK_NOPE_DIM + V_HEAD_DIM)
        k_nope, v = kv[..., :QK_NOPE_DIM], kv[..., QK_NOPE_DIM:]
        k_pe = apply_rope(k_pe, cos, sin)
        k = jnp.concatenate([k_nope, jnp.broadcast_to(k_pe[:, :, None, :], (b, s, MLA_HEADS, QK_ROPE_DIM))], axis=-1)
        a_out = mla_attention(q, k, v)

        c_out = short_gated_conv(gb, gc, xin, conv_w[l])

        mem_n = rmsnorm_2(mem, mem_norm_g[l])
        m_out = memory_attention(q_mem.reshape(b, s, MEM_HEADS, MEM_HEAD_DIM), mem_n, w_mk[l], w_mv[l])

        y = jnp.concatenate([a_out, c_out, m_out], axis=-1) * jax.nn.silu(gate)
        o = y @ w_o[l]
        x = x + rmsnorm_2(o, post_norm_g[l])
    return x


def setup_inputs(seed=0):
    out = dict(first_inputs(seed))
    for name, value in second_inputs(seed + 1).items():
        if name != "x":
            out[name + "_2"] = value
    return out


def reference(
    x, g_pre, g_post, w_in_a, w_out_a, sinks_a, w_in_b, w_out_b, w_in_c, b_f_c, w_out_c, mem_2,
    positions_2, pre_norm_g_2, w_in_2, q_norm_g_2, w_uq_2, kv_norm_g_2, w_ukv_2, conv_w_2,
    mem_norm_g_2, w_mk_2, w_mv_2, w_o_2, post_norm_g_2,
):
    x = first_block(
        x, g_pre, g_post, w_in_a, w_out_a, sinks_a, w_in_b, w_out_b, w_in_c, b_f_c, w_out_c,
    )
    return second_block(
        x, mem_2, positions_2, pre_norm_g_2, w_in_2, q_norm_g_2, w_uq_2, kv_norm_g_2, w_ukv_2,
        conv_w_2, mem_norm_g_2, w_mk_2, w_mv_2, w_o_2, post_norm_g_2,
    )


_drawn_inputs = setup_inputs


def setup_inputs(seed=0):
    import zlib

    import numpy as np

    out = dict(_drawn_inputs(seed))
    spreads = {}
    factors = {'q_norm_g_2': 8.0, 'kv_norm_g_2': 8.0, 'mem_norm_g_2': 8.0, 'post_norm_g_2': 3.068}
    for name, (base, spread) in spreads.items():
        noise = np.random.default_rng([zlib.crc32(name.encode()), seed]).standard_normal(out[name].shape)
        drawn = base * np.exp(spread * noise) if base else spread * noise
        out[name] = __import__('jax').numpy.asarray(drawn.astype(out[name].dtype))
    for name, factor in factors.items():
        out[name] = (out[name] * factor).astype(out[name].dtype)
    return out
```

```python
def build(nc, xT, memT, mem, pos, gains, sinks, consts, window, w1, w2, out):
    from contextlib import ExitStack

    import numpy as np
    import concourse.bass as bass
    from concourse import mybir

    F32, F32R, I32 = mybir.dt.float32, mybir.dt.float32r, mybir.dt.int32
    ACT = mybir.ActivationFunctionType
    ALU = mybir.AluOpType
    AX = mybir.AxisListType

    P = 128
    D, S, MEM = 2048, 512, 256
    KT, TB, MB = D // P, S // P, MEM // P
    EPS = 1e-6
    CW = KT * P

    HD, PAIRS, KVH = 64, 16, 4
    PAIR1 = 4
    WO1 = PAIR1 + 2 * PAIRS
    N1 = WO1 + KT

    LAYERS, MLA, MH, CT = 2, 8, 4, 4
    MK, MV, QL, KVL, KPE, CONV, QM, HEAD = 0, 4, 8, 12, 14, 15, 27, 31
    WO2 = HEAD + 3 * MLA
    N2 = WO2 + KT
    QRT, KVRT = 4, 2
    UK = QRT * 256
    UV = UK + KVRT * P
    HW = (UV + KVRT * 2 * P, UV)
    MLA_SCALE, MEM_SCALE = (128 + 64) ** -0.5, P ** -0.5
    STEPS = ((0, 1, 2, 3), (4, 5), (6, 7, 8, 9), (10, 11), (12, 13, 14, 15))
    H_SPLITS = (5, 10)
    LAST = MLA - 1

    PRE1, POST, MEMG, GL, GN = 0, 16, 64, 112, 34
    PRE, QG, KVG, TAP = 0, 16, 20, 22
    IDENT, ONES, SLOPE, FREQ, PHASE, SIGN, C_COLS = 0, 128, 256, 288, 289, 290, 291
    TWO_PI, PI = float(2 * np.pi), float(np.float32(np.pi))
    TURN_A = 6.28125
    TURN_B = float(np.round((TWO_PI - TURN_A) * 2 ** 20) / 2 ** 20)
    TURN_C = TWO_PI - TURN_A - TURN_B

    class Chunk:

        def __init__(self, n, slot, uses, back):
            self.n, self.slot, self.uses, self.back = n, slot, uses, back

    def chunk1(p, i=0):
        new = isinstance(i, int) and i == 0 and p < 2
        return Chunk(i * 2 + p, p % 2, i + p // 2, None if new else 2)

    def chunk2(l, p, i=0, stride=0):
        slot = p % 2
        n = l * N2 + (N1 + p)
        uses = l * ((N2 + 1 - slot) // 2) + (N1 // 2 + p // 2)
        if stride:
            n, uses = n + i * stride, uses + i * (stride // 2)
        return Chunk(n, slot, uses, 1 if p == 0 and stride == 0 else 2)

    POSTN, PREN, QN, KVN = 2, 3, 4, 5

    def norm_no(l, which):
        return l * 4 + which

    SQ_LAYER = KT + KT + QRT + KVRT
    ODD = KT // 2

    def sq_no(l, which):
        return l * SQ_LAYER + (0, KT, 2 * KT, 2 * KT + QRT, SQ_LAYER)[which - 2]

    residual = nc.dram_tensor("residual", (LAYERS + 1, P, KT * S), F32, kind="Internal").ap()\
        .rearrange("l p c -> p l c")
    ctx = ExitStack()
    with ctx:
        free = [(nc.sbuf_base + 63) // 64 * 64]

        def sb(name, cols, dt=F32, at=None):
            if at is None:
                at = free[0]
                free[0] += (cols * 4 + 63) // 64 * 64
            return nc.alloc_sbuf_tensor_at(name, [P, cols], dt, offset=at)

        raw = [sb(f"raw{s}", CW) for s in range(2)]
        hi = [sb(f"hi{s}", CW, F32R) for s in range(2)]
        lo = [sb(f"lo{s}", CW, F32R) for s in range(2)]
        h_hi, h_lo = sb("h_hi", KT * S, F32R), sb("h_lo", KT * S, F32R)
        g = sb("g", KT * S)
        m0 = free[0]
        m_hi, m_lo = sb("m_hi", KT * MEM, F32R), sb("m_lo", KT * MEM, F32R)
        m1 = m0 + 4 * KT * MEM
        a0 = free[0]
        area = sb("area", 4096)
        cst = sb("cst", C_COLS)
        gn = sb("gn", GL + LAYERS * GN)
        snk = sb("snk", 2 * PAIRS)
        cs = sb("cs", S)
        kr = sb("kr", S)
        r_mem = sb("r_mem", MEM)
        sqacc, sq, dg = sb("sqacc", S), sb("sq", 2 * S), sb("dg", S)
        qr = sqacc
        st = sb("st", 64)
        prob1, pt1 = sb("prob1", 2048, at=m0), sb("pt1", 2048, at=m0 + 8192)
        kdup, vall, win = sb("kdup", KVH * S, at=m1), sb("vall", TB * 256, at=m1 + 8192), sb("win", TB * 256, at=m1 + 12288)
        angle, posi = sb("angle", 3 * S, at=m0), sb("posi", S, I32, at=m0 + 12288)
        turns, memrow1 = sb("turns", S, I32, at=m1), sb("memrow1", D, at=m1 + 2048)
        memrow0 = sb("memrow0", D, at=a0 + 4096)
        prob_a, prob_b = sb("prob_a", 1024, at=m0 + 12288), sb("prob_b", 1024, at=m1 + 12288)
        kcur, vcur, q1 = sb("kcur", 640, at=a0), sb("vcur", 512, at=a0 + 2560), sb("q1", S, at=a0 + 4608)
        htmp, xr = sb("htmp", 2 * S, at=a0), sb("xr", 4 * S, at=a0)
        u = sb("u", S + 2, at=a0 + 4096)
        qm, ptm = sb("qm", 2 * S, at=a0), sb("ptm", MB * S, at=a0 + 4096)
        mk, mv = sb("mk", MH * MEM, at=a0 + 8192), sb("mv", MB * 512, at=a0 + 12288)
        qn, kn, v = sb("qn", S, at=a0), sb("kn", S, at=a0 + 2048), sb("v", TB * 256, at=a0 + 4096)
        pt = sb("pt", TB * S, at=a0 + 8192)
        tz, sg = sq[:, 0:S], sq[:, S:2 * S]
        cv, cg = sq[:, 0:S], sq[:, S:2 * S]

        ident, ones = cst[:, IDENT:IDENT + P], cst[:, ONES:ONES + P]
        ms, r, nt, half = st[:, 0:4], st[:, 4:8], st[:, 8:12], st[:, 12:16]
        mx, nm, ls, es, rl = (st[:, 16 + 8 * i:24 + 8 * i] for i in range(5))
        ss = st[:, 56:58]

        acc = [ctx.enter_context(nc.psum_tensor(f"acc{s}", [P, 512], F32)) for s in range(2)]
        ov = [ctx.enter_context(nc.psum_tensor(f"ov{s}", [P, 512], F32)) for s in range(2)]
        sc = ctx.enter_context(nc.psum_tensor("sc", [P, 2048], F32))

        def bank(b, n=512, off=0):
            return sc[:, 512 * b + off:512 * b + off + n]

        def tile(t, n=S):
            return slice(t * n, (t + 1) * n) if isinstance(t, int) else bass.ds(t * n, n)

        def col(c):
            return slice(c, c + 1) if isinstance(c, int) else bass.ds(c, 1)

        def sem(name):
            return ctx.enter_context(nc.semaphore(name))

        loaded = [sem("loaded0"), sem("loaded1")]
        consts_in, pos_in, gains_in, window_in = (sem(f"{n}_in") for n in ("consts", "pos", "gains", "window"))
        x_in = [sem(f"x_in{c}") for c in range(4)]
        memrows_in, memory_in, residual_in = sem("memrows_in"), sem("memory_in"), [sem("residual_in0"), sem("residual_in1")]
        stored, out_stored = sem("residual_stored"), sem("out_stored")
        waited = sem("waited")
        hi_done, lo_done, chunk_done = sem("hi_done"), sem("lo_done"), sem("chunk_done")
        evacuated = [sem("evacuated0"), sem("evacuated1")]
        squared, added, sums_done, ms_done, rs_done = (
            sem(n) for n in ("squared", "added", "sums_done", "ms_done", "rs_done"))
        x_squared, x_added = sem("x_squared"), sem("x_added")
        diag_done, r_done, norm_link, half_set = (sem(n) for n in ("diag_done", "r_done", "norm_link", "half_set"))
        normed_done, h_hi_done, h_even, h_odd = (sem(n) for n in ("normed", "h_hi_done", "h_even", "h_odd"))
        y_hi_done, y_done = sem("y_hi_done"), sem("y_done")
        mem_ss, r_mem_done = sem("mem_ss"), sem("r_mem_done")
        mt_done, mhi_done, m_done = (sem(n) for n in ("mem_normed", "mem_hi_done", "m_done"))
        scaled, x_even, x_odd = sem("scaled"), sem("x_even"), sem("x_odd")
        rope_link, angle_done, sin_done = sem("rope_link"), sem("angle_done"), sem("sin_done")
        kcur_pad, kcur_done, vcur_done, v_in = sem("kcur_pad"), sem("kcur_done"), sem("vcur_done"), sem("v_in")
        scores1, soft1_link, shift1, exp1, probs1 = (
            sem(n) for n in ("scores1", "soft1_link", "shift1", "exp1", "probs1"))
        turned1, pt1_act, pt1_dve, values1, tanh1, y1 = (
            sem(n) for n in ("turned1", "pt1_act", "pt1_dve", "values1", "tanh1", "y1"))
        lat_normed, lat_hi_done, lat_done = sem("lat_normed"), sem("lat_hi_done"), sem("lat_done")
        kr_link, conv_link, u_pad = sem("kr_link"), sem("conv_link"), sem("u_pad")
        scores_m, soft_m_link, shift_m, exp_m, probs_m, turned_m, ptm_done, values_m, om_done = (
            sem(n) for n in ("scores_m", "soft_m_link", "shift_m", "exp_m", "probs_m", "turned_m", "ptm_done", "values_m", "om_done"))
        qkv_done, qr_done, scores2, soft2_link, shift2, exp2, probs2 = (
            sem(n) for n in ("qkv_done", "qr_done", "scores2", "soft2_link", "shift2", "exp2", "probs2"))
        turned2, pt2_act, pt2_dve, values2, tanh2, gate_b, y_a, y_b = (
            sem(n) for n in ("turned2", "pt2_act", "pt2_dve", "values2", "tanh2", "gate_b", "y_a", "y_b"))
        pe_from_one, dve_from_one = (scores1, values1, values2), (y1, om_done, y_a)
        block = ctx.enter_context(nc.Block())

        @block.sync
        def _(sp):
            sp.dma_start(cst[:, :], consts).then_inc(consts_in, 16)
            sp.dma_start(posi[:, :], pos.partition_broadcast(P)).then_inc(pos_in, 16)
            for c in range(4):
                part = slice(4 * c * S, 4 * (c + 1) * S)
                sp.dma_start(g[:, part], xT[:, part]).then_inc(x_in[c], 16)
            sp.dma_start(gn[:, :], gains).then_inc(gains_in, 16)
            sp.dma_start(snk[:, :], sinks.partition_broadcast(P)).then_inc(gains_in, 16)
            sp.dma_start(win[:, :], window).then_inc(window_in, 16)

            def load(c, src, width=CW):
                if c.back is not None:
                    sp.wait_ge(lo_done, c.n + (1 - c.back))
                sp.dma_start(raw[c.slot][:, 0:width], src).then_inc(loaded[c.slot], 16)

            load(chunk1(0), w1[:, 0, :])
            load(chunk1(1), w1[:, 1, :])
            sp.dma_start(memrow0[:, :], mem[:, 0, :]).then_inc(memrows_in, 16)
            sp.dma_start(memrow1[:, :], mem[:, 1, :]).then_inc(memrows_in, 16)
            with sp.Fori(1, N1 // 2) as i:
                for j in range(2):
                    load(chunk1(j, i), w1[:, bass.ds(i * 2 + j, 1), :])
            with sp.Fori(0, LAYERS) as l:
                def load2(p, i=0, stride=0, width=CW):
                    c = chunk2(l, p, i, stride)
                    load(c, w2[:, bass.ds(c.n - N1, 1), 0:width], width)

                load2(0)
                load2(1)
                with sp.Fori(0, (HEAD - 3) // 2) as i:
                    load2(2, i, 2)
                    load2(3, i, 2)
                load2(HEAD - 1)
                with sp.Fori(0, MLA // 2) as i:
                    for j in range(6):
                        load2(HEAD + j, i, 6, HW[j // 3] if j % 3 == 0 else CW)
                with sp.Fori(0, KT // 2) as i:
                    load2(WO2, i, 2)
                    load2(WO2 + 1, i, 2)

        @block.gpsimd
        def _(pool):
            def settle():
                pool.sem_inc(waited, 1)

            def add_square(no, slot, first=False):
                src = sq[:, tile(slot)]
                pool.wait_ge(squared, no + 1)
                if first:
                    settle()
                    ins = pool.tensor_copy(sqacc[:, :], src)
                else:
                    pool.wait_ge(added, no + 2)
                    ins = pool.tensor_tensor(sqacc[:, :], sqacc[:, :], src, ALU.add)
                ins.then_inc(added, 1)

            def add_squares(no, tiles):
                add_square(no, 0, True)
                add_square(no + 1, 1)
                with pool.Fori(1, tiles // 2) as i:
                    add_square(i * 2 + no, 0)
                    add_square(i * 2 + no + 1, 1)

            def root(no, n=TB):
                pool.wait_ge(ms_done, no + 1)
                pool.tensor_tensor(r[:, 0:n], ms[:, 0:n], half[:, 0:n], ALU.pow).then_inc(rs_done, 1)

            pool.sem_inc(added, 2)
            pool.memset(half, -0.5).then_inc(half_set, 1)
            pool.wait_ge(half_set, 1)
            for c in range(4):
                pool.wait_ge(x_in[c], 16)
            pool.dma_start(residual[:, 0, :], g[:, :]).then_inc(stored, 16)

            def h_lo_odd(t, count):
                pool.wait_ge(h_hi_done, count)
                pool.tensor_tensor(h_lo[:, tile(t)], htmp[:, S:2 * S], h_hi[:, tile(t)].bitcast(F32),
                                   ALU.subtract).then_inc(h_odd, 1)

            root(0)
            for t in range(1, KT, 2):
                h_lo_odd(t, t + 1)
            root(1, MB)

            pool.wait_ge(v_in, 1)
            pool.memset(kcur[:, 0:P], 0.0).then_inc(kcur_pad, 1)
            pool.wait_ge(kcur_pad, 1)
            with pool.Fori(0, KVH) as n:
                with pool.Fori(0, PAIRS // KVH) as m:
                    i = n * (PAIRS // KVH) + m
                    pool.wait_ge(scores1, i + 1)
                    settle()
                    pool.tensor_copy(kcur[:, P:P + S], kdup[:, tile(n)]).then_inc(kcur_done, 1)
                    pool.wait_ge(values1, i + 1)
                    settle()
                    for dup in range(2):
                        pool.tensor_copy(vcur[:, :].rearrange("p (b d) -> p b d", b=TB)[:, :, dup * HD:(dup + 1) * HD],
                                         vall[:, :].rearrange("p (b d) -> p b d", b=TB)[:, :, tile(n, HD)])\
                            .then_inc(vcur_done, 1)

            def reload_residual(l, u_, slot):
                settle()
                pool.dma_start(xr[:, slot * 2 * S:(slot + 1) * 2 * S],
                               residual[:, col(l), tile(u_, 2 * S)]).then_inc(residual_in[slot], 16)

            def load_memory():
                settle()
                pool.dma_start(area[:, :], memT).then_inc(memory_in, 16)

            pool.wait_ge(values1, PAIRS + 1)
            load_memory()
            add_squares(sq_no(0, POSTN), KT)
            root(POSTN)

            def add_residual(l, w, to):
                slot, t = w % 2, 2 * w + 1
                pool.wait_ge(scaled, l * KT + (t + 1))
                pool.wait_ge(residual_in[slot], l * (4 * KT) + 16 * (w // 2 + 1))
                pool.tensor_tensor(g[:, tile(t)], g[:, tile(t)], xr[:, tile(2 * slot + 1)], ALU.add).then_inc(x_odd, 1)
                pool.wait_ge(x_odd, l * ODD + (w + 1))
                pool.wait_ge(x_even, l * ODD + (w + 1))
                if w + 2 < ODD:
                    reload_residual(l, w + 2, slot)
                else:
                    settle()
                done = out_stored if l is LAYERS else stored
                pool.dma_start(to, g[:, tile(w, 2 * S)]).then_inc(done, 16)

            with pool.Fori(0, LAYERS) as l:
                pool.wait_ge(m_done, l * KT + KT)
                reload_residual(l, 0, 0)
                reload_residual(l, 1, 1)
                for w in range(ODD + 1):
                    if w < ODD:
                        add_residual(l, w, residual[:, col(l + 1), tile(w, 2 * S)])
                    if w > 0:
                        add_square(sq_no(l, PREN) + (2 * w - 2), 0, w == 1)
                        add_square(sq_no(l, PREN) + (2 * w - 1), 1)
                root(norm_no(l, PREN))
                for t in range(1, KT, 2):
                    h_lo_odd(t, l * KT + (KT + t + 1))
                add_squares(sq_no(l, QN), QRT)
                root(norm_no(l, QN))
                add_square(sq_no(l, KVN), 0, True)
                add_square(sq_no(l, KVN) + 1, 1)
                root(norm_no(l, KVN))
                pool.wait_ge(values2, l * MLA + (MLA + 1))
                load_memory()
                add_squares(sq_no(l, KVN) + KVRT, KT)
                root(norm_no(l + 1, POSTN))

            pool.wait_ge(m_done, LAYERS * KT + KT)
            reload_residual(LAYERS, 0, 0)
            reload_residual(LAYERS, 1, 1)
            for w in range(ODD):
                add_residual(LAYERS, w, out[:, tile(w, 2 * S)])
            pool.wait_ge(out_stored, 16 * (KT // 2))
            pool.wait_ge(stored, 16 * (1 + LAYERS * KT // 2))

        @block.tensor
        def _(pe):
            def begin(c):
                pe.wait_ge(lo_done, c.n + 1)
                if c.back is not None:
                    pe.wait_ge(evacuated[c.slot], c.uses)

            def passes(to, w_hi, w_lo, x_hi, x_lo, first, last, w_moves=False):
                for n, (a, b) in enumerate(((w_hi, x_hi), (w_hi, x_lo), (w_lo, x_hi))):
                    a, b = (b, a) if w_moves else (a, b)
                    ins = pe.matmul(to, a, b, start=first and n == 0, stop=last and n == 2)
                return ins

            def k_tile(c, k, x_hi, x_lo, n, first, last):
                w, x = tile(k, P), tile(k, n)
                return passes(acc[c.slot][:, 0:n], hi[c.slot][:, w], lo[c.slot][:, w], x_hi[:, x], x_lo[:, x], first, last)

            def features(c, x_hi, x_lo, n=S, order=range(KT), ready=None, pause=0, meanwhile=None):
                begin(c)
                for j, k in enumerate(order):
                    if meanwhile is not None and j == pause:
                        meanwhile()
                    if ready is not None:
                        ready(j)
                    ins = k_tile(c, k, x_hi, x_lo, n, j == 0, j == KT - 1)
                ins.then_inc(chunk_done, 1)

            def features_behind_h(c, d, before):
                lag = KT // 2
                begin(c)
                for k in range(KT + lag):
                    if k < KT:
                        pe.wait_ge((h_even, h_odd)[k % 2], before + (k // 2 + 1))
                        ins = k_tile(c, k, h_hi, h_lo, S, k == 0, k == KT - 1)
                        if k == KT - 1:
                            ins.then_inc(chunk_done, 1)
                    if k == lag:
                        begin(d)
                    if k >= lag:
                        ins = k_tile(d, k - lag, h_hi, h_lo, S, k == lag, k == KT + lag - 1)
                ins.then_inc(chunk_done, 1)

            def rows(c, at, tiles, to, x_hi, x_lo, n):
                pe.wait_ge(lo_done, c.n + 1)
                cols = CW // tiles
                for b in range(n // P):
                    for j in range(tiles):
                        w, x = tile(j, cols), slice((at + j) * n + b * P, (at + j) * n + (b + 1) * P)
                        ins = passes(to(b), hi[c.slot][:, w], lo[c.slot][:, w], x_hi[:, x], x_lo[:, x],
                                     at + j == 0, at + j == KT - 1, True)
                ins.then_inc(chunk_done, 1)

            def sums(count_on, squares):
                pe.wait_ge(count_on, squares)
                for b in range(TB):
                    ins = pe.matmul(ov[0][:, b:b + 1], sqacc[:, tile(b, P)], ones[:, 0:1], start=True, stop=True)
                ins.then_inc(sums_done, 1)

            def spread(no, to, n=S):
                pe.wait_ge(diag_done, no + 1)
                pe.matmul(to, ones, dg[:, 0:n], start=True, stop=True).then_inc(r_done, 1)

            for s in pe_from_one:
                pe.sem_inc(s, 1)
            pe.wait_ge(consts_in, 16)
            sums(x_added, KT)
            spread(0, bank(0))

            features_behind_h(chunk1(0), chunk1(1), 0)
            spread(1, ov[1][:, 0:MEM], MEM)
            for c in range(2):
                rows(chunk1(2 + c), c * KT // 2, KT // 2, lambda b: bank(b, 256), h_hi, h_lo, S)

            def scores_first(i):
                c = chunk1(PAIR1, i)
                pe.wait_ge(evacuated[c.slot], c.uses + 1)
                pe.wait_ge(kcur_done, i + 1)
                for b in range(TB):
                    for par in range(2):
                        rows_ = slice(HD * par, HD * par + HD)
                        ins = pe.matmul(bank(2 * par + b // 2, 256, b % 2 * 256), q1[rows_, tile(b, P)], kcur[rows_, b * P:b * P + 256],
                                        start=True, stop=True)
                ins.then_inc(scores1, 1)

            def turn_first(i):
                pe.wait_ge(probs1, i + 1)
                for kb in range(TB):
                    for par in range(2):
                        for nxt in range(2):
                            b = kb + nxt
                            if b < TB:
                                src = par * 1024 + b * 256 + (1 - nxt) * P
                                ins = pe.transpose(bank(kb, P, par * 256 + nxt * P), prob1[:, src:src + P], ident)
                ins.then_inc(turned1, 1)

            def values_first(i):
                pe.wait_ge(pt1_act, i * 2 + 2)
                pe.wait_ge(pt1_dve, i * 2 + 2)
                pe.wait_ge(vcur_done, i * 2 + 2)
                pe.wait_ge(y1, i + 1)
                for par in range(2):
                    for kb in range(TB):
                        n = 256 if kb < TB - 1 else P
                        src = kb * 512 + par * 256
                        ins = pe.matmul(ov[par][:, kb * P:kb * P + n], vcur[:, tile(kb, P)], pt1[:, src:src + n],
                                        start=kb == 0, stop=kb == TB - 1, skip_group_check=True)
                ins.then_inc(values1, 1)

            def pair(i, first):
                features(chunk1(PAIR1, i), h_hi, h_lo, pause=6, meanwhile=None if first else lambda: turn_first(i - 1))
                if not first:
                    values_first(i - 1)
                scores_first(i)
                features(chunk1(PAIR1 + 1, i), h_hi, h_lo)

            pair(0, True)
            with pe.Fori(1, PAIRS) as i:
                pair(i, False)
            turn_first(PAIRS - 1)
            values_first(PAIRS - 1)
            features(chunk1(WO1), h_hi, h_lo, ready=lambda j: pe.wait_ge(y_done, j + 1))
            features(chunk1(WO1 + 1), h_hi, h_lo)
            with pe.Fori(1, KT // 2) as i:
                features(chunk1(WO1, i), h_hi, h_lo)
                features(chunk1(WO1 + 1, i), h_hi, h_lo)

            with pe.Fori(0, LAYERS) as l:
                pe.wait_ge(m_done, l * KT + KT)
                features(chunk2(l, MK), m_hi, m_lo, MEM, pause=KT // 2, meanwhile=lambda: sums(added, sq_no(l, PREN) + 2))
                spread(norm_no(l, POSTN), bank(0))
                for c in range(1, MH):
                    features(chunk2(l, MK + c), m_hi, m_lo, MEM)
                for c in range(MH):
                    rows(chunk2(l, MV + c), c * KT // MH, KT // MH, lambda b: bank(2 + b), m_hi, m_lo, MEM)
                    if c == 1:
                        sums(added, sq_no(l, QN) + 2)
                    if c == 2:
                        spread(norm_no(l, PREN), bank(1))
                features_behind_h(chunk2(l, QL), chunk2(l, QL + 1), l * ODD + ODD)
                for j in range(2, QRT):
                    features(chunk2(l, QL + j), h_hi, h_lo)
                features(chunk2(l, KVL), h_hi, h_lo)
                sums(added, sq_no(l, KVN) + 2)
                features(chunk2(l, KVL + 1), h_hi, h_lo)
                spread(norm_no(l, QN), bank(0))
                features(chunk2(l, KPE), h_hi, h_lo)
                sums(added, sq_no(l, KVN) + (KVRT + 2))
                with pe.Fori(0, CT // 2) as i:
                    for j in range(6):
                        features(chunk2(l, CONV + j, i, 6), h_hi, h_lo)
                spread(norm_no(l, KVN), bank(1))

                def scores_mem(c):
                    ch = chunk2(l, QM + c)
                    pe.wait_ge(evacuated[ch.slot], ch.uses + 1)
                    for b in range(TB):
                        ins = pe.matmul(bank(b, MEM), qm[:, (c % 2) * S + b * P:(c % 2) * S + (b + 1) * P], mk[:, tile(c, MEM)],
                                        start=True, stop=True)
                    ins.then_inc(scores_m, 1)

                def values_mem(c):
                    no = l * MH + (c + 1)
                    pe.wait_ge(probs_m, no)
                    for b in range(TB):
                        for k in range(MB):
                            ins = pe.transpose(bank(b, P, k * P), prob_a[:, b * MEM + k * P:b * MEM + (k + 1) * P], ident)
                    ins.then_inc(turned_m, 1)
                    pe.wait_ge(ptm_done, no)
                    pe.wait_ge(om_done, l * MH + (c + 1))
                    for k in range(MB):
                        ins = pe.matmul(ov[1][:, :], mv[:, k * 512 + c * P:k * 512 + (c + 1) * P], ptm[:, tile(k)],
                                        start=k == 0, stop=k == MB - 1)
                    ins.then_inc(values_m, 1)

                for c in range(MH):
                    features(chunk2(l, QM + c), h_hi, h_lo)
                    if c == 0:
                        pe.wait_ge(lat_done, l * 6 + 6)
                    else:
                        values_mem(c - 1)
                    scores_mem(c)
                values_mem(MH - 1)
                pe.wait_ge(om_done, l * MH + (MH + 1))

                def project(c, j, wait_banks):
                    begin(c)
                    w_hi, w_lo = hi[c.slot], lo[c.slot]

                    def product(to, at, x, first, last, w_moves=False):
                        w = slice(at, at + (2 * P if w_moves else P))
                        return passes(to, w_hi[:, w], w_lo[:, w], m_hi[:, x], m_lo[:, x], first, last, w_moves)

                    for k in range(QRT):
                        product(acc[c.slot][:, :], k * 256, tile(KVRT + k), k == 0, k == QRT - 1)
                    for k in range(KVRT):
                        product(ov[1][:, :], UK + k * P, tile(k), k == 0, k == KVRT - 1)
                    wait_banks()
                    for k in range(QRT):
                        ins = product(bank(0), k * 256 + P, tile(KVRT + k), k == 0, k == QRT - 1)
                    for b in range(TB if j == 0 else 0):
                        for k in range(KVRT):
                            ins = product(bank(1 + b // 2, 2 * P, b % 2 * 2 * P), UV + k * 2 * P,
                                          slice(k * S + b * P, k * S + (b + 1) * P), k == 0, k == KVRT - 1, True)
                    ins.then_inc(chunk_done, 1)

                def scores_head(no):
                    pe.wait_ge(qkv_done, no * 2)
                    pe.wait_ge(qr_done, no * 3)
                    for b in range(TB):
                        pe.matmul(bank(b), qn[:, tile(b, P)], kn[:, :], start=True, stop=False)
                        ins = pe.matmul(bank(b), qr[0:64, tile(b, P)], kr[0:64, :], start=False, stop=True)
                    ins.then_inc(scores2, 1)

                def turn_head(no):
                    pe.wait_ge(probs2, no)
                    for b in range(TB):
                        for k in range(TB):
                            src = (b % 2) * S + k * P
                            ins = pe.transpose(bank(b, P, k * P), (prob_a, prob_b)[b // 2][:, src:src + P], ident)
                    ins.then_inc(turned2, 1)

                def turned_read(no):
                    pe.wait_ge(pt2_act, no * 2)
                    pe.wait_ge(pt2_dve, no * 2)

                def values_head(no, j):
                    turned_read(no)
                    pe.wait_ge(y_a, no)
                    for k in range(TB):
                        ins = pe.matmul(ov[0][:, :], v[:, (2 * k + j) * P:(2 * k + j + 1) * P], pt[:, tile(k)], start=k == 0, stop=k == TB - 1)
                    ins.then_inc(values2, 1)

                def head(i, j, first):
                    no = l * MLA + (i * 2 + (j + 1))
                    project(chunk2(l, HEAD + 3 * j, i, 6), j, (lambda: None) if first else (lambda: turned_read(no - 1)))
                    if not first:
                        values_head(no - 1, 1 - j)
                    features(chunk2(l, HEAD + 3 * j + 1, i, 6), h_hi, h_lo)
                    scores_head(no)
                    features(chunk2(l, HEAD + 3 * j + 2, i, 6), h_hi, h_lo)
                    turn_head(no)

                head(0, 0, True)
                head(0, 1, False)
                with pe.Fori(1, MLA // 2) as i:
                    head(i, 0, False)
                    head(i, 1, False)
                values_head(l * MLA + MLA, 1)
                features(chunk2(l, WO2), h_hi, h_lo, order=[t for t in range(KT) if t != LAST] + [LAST],
                         ready=lambda j: pe.wait_ge(y_done, l * KT + (KT + j + 1)))
                features(chunk2(l, WO2 + 1), h_hi, h_lo)
                with pe.Fori(1, KT // 2) as i:
                    features(chunk2(l, WO2, i, 2), h_hi, h_lo)
                    features(chunk2(l, WO2 + 1, i, 2), h_hi, h_lo)
            sums(added, sq_no(LAYERS, PREN) + 2)
            spread(norm_no(LAYERS, POSTN), bank(0))

        @block.scalar
        def _(act):
            def split(c):
                act.wait_ge(loaded[c.slot], (c.uses + 1) * 16)
                if c.back is not None:
                    act.wait_ge(chunk_done, c.n + (1 - c.back))
                act.activation(hi[c.slot][:, :], raw[c.slot][:, :], ACT.Copy).then_inc(hi_done, 1)

            def multiplied(c):
                act.wait_ge(chunk_done, c.n + 1)

            def square(src, no, slot):
                act.wait_ge(added, no + 1)
                act.activation(sq[:, tile(slot)], src, ACT.Square).then_inc(squared, 1)

            def h_hi_tile(t, slot, count):
                act.wait_ge(normed_done, count)
                act.activation(h_hi[:, tile(t)], htmp[:, tile(slot)], ACT.Copy).then_inc(h_hi_done, 1)

            def y_hi_tile(t):
                act.activation(h_hi[:, tile(t)], g[:, tile(t)], ACT.Copy).then_inc(y_hi_done, 1)

            for t in range(KT):
                if t % 4 == 0:
                    act.wait_ge(x_in[t // 4], 16)
                if t >= 2:
                    act.wait_ge(x_added, t - 1)
                act.activation(sq[:, tile(t % 2)], g[:, tile(t)], ACT.Square).then_inc(x_squared, 1)
            split(chunk1(0))
            split(chunk1(1))
            act.wait_ge(angle_done, 1)
            act.activation(angle[:, 0:S], angle[:, 0:S], ACT.Sin).then_inc(sin_done, 1)
            for t in range(KT):
                h_hi_tile(t, t % 2, t + 1)
            act.wait_ge(memrows_in, 32)
            for b, rows_ in enumerate((memrow0, memrow1)):
                ins = act.activation(rows_[:, :], rows_[:, :], ACT.Square, accum_out=ss[:, b:b + 1])
            ins.then_inc(mem_ss, 1)

            for c in range(2):
                ch = chunk1(c)
                split(chunk1(2 + c))
                if c == 0:
                    act.wait_ge(mem_ss, 1)
                multiplied(ch)
                for j in range(2):
                    for half_ in range(2):
                        ins = act.activation(kdup[HD * half_:HD * (half_ + 1), tile(2 * c + j)],
                                             acc[ch.slot][HD * j:HD * (j + 1), :], ACT.Copy)
                ins.then_inc(evacuated[ch.slot], 2)
            act.wait_ge(r_done, 2)
            act.activation(r_mem[:, :], ov[1][:, 0:MEM], ACT.Copy).then_inc(r_mem_done, 1)
            split(chunk1(PAIR1))
            multiplied(chunk1(3))
            act.activation(vall[:, :].rearrange("p (b n) -> p b n", b=TB),
                           sc[:, :].rearrange("p (b n) -> p b n", b=TB)[:, :, 0:256], ACT.Copy).then_inc(v_in, 1)

            def turned_first(i, values_count):
                act.wait_ge(turned1, i + 1)
                act.wait_ge(values1, values_count)
                for b in range(2):
                    act.activation(pt1[:, tile(b)], bank(b), ACT.Copy).then_inc(pt1_act, 1)

            def pair(i, first):
                qc, zc = chunk1(PAIR1, i), chunk1(PAIR1 + 1, i)
                split(zc)
                if not first:
                    turned_first(i - 1, i)
                multiplied(qc)
                act.wait_ge(scores1, i + 1)
                act.activation(q1[:, :], acc[qc.slot][:, :], ACT.Copy, scale=HD ** -0.5).then_inc(evacuated[qc.slot], 1)
                split(chunk1(PAIR1 + 2, i))
                act.wait_ge(shift1, i + 1)
                for n in range(2 * TB):
                    act.activation(prob1[:, tile(n, 256)], prob1[:, tile(n, 256)], ACT.Exp,
                                   bias=nm[:, n:n + 1], accum_out=ls[:, n:n + 1])
                act.activation(es, es, ACT.Exp).then_inc(exp1, 1)
                multiplied(zc)
                act.wait_ge(evacuated[zc.slot], zc.uses)
                act.activation(tz, acc[zc.slot][:, :], ACT.Tanh, scale=0.5).then_inc(tanh1, 1)

            pair(0, True)
            with act.Fori(1, PAIRS) as i:
                pair(i, False)
            turned_first(PAIRS - 1, PAIRS)

            act.wait_ge(y1, PAIRS)
            act.wait_ge(chunk_done, WO1)
            with act.Fori(0, KT - 1) as t:
                y_hi_tile(t)
            act.wait_ge(y1, PAIRS + 1)
            y_hi_tile(KT - 1)

            def output_tile(t, slot, c, nxt, sq_at, m_at):
                if nxt is not None:
                    split(nxt)
                act.wait_ge(mt_done, m_at + 1)
                act.activation(m_hi[:, tile(t, MEM)], dg[:, tile(slot, MEM)], ACT.Copy).then_inc(mhi_done, 1)
                multiplied(c)
                square(acc[c.slot][:, :], sq_at, slot)
                act.activation(g[:, tile(t)], acc[c.slot][:, :], ACT.Copy).then_inc(evacuated[c.slot], 1)

            def output(chunk, sq_at, m_at):
                with act.Fori(0, KT // 2 - 1) as i:
                    for j in range(2):
                        output_tile(i * 2 + j, j, chunk(j, i), chunk(j + 1, i), i * 2 + (sq_at + j), i * 2 + (m_at + j))
                for j in range(2):
                    t = KT - 2 + j
                    output_tile(t, j, chunk(j, KT // 2 - 1), chunk(1, KT // 2 - 1) if j == 0 else None, sq_at + t, m_at + t)

            output(lambda p, i: chunk1(WO1 + p, i), sq_no(0, POSTN), 0)

            with act.Fori(0, LAYERS) as l:
                split(chunk2(l, MK))
                for c in range(MH + 1):
                    split(chunk2(l, MK + c + 1))
                    for t in STEPS[c]:
                        act.wait_ge((x_even, x_odd)[t % 2], l * ODD + (t // 2 + 1))
                        square(g[:, tile(t)], sq_no(l, PREN) + t, t % 2)
                    if c < MH:
                        ch = chunk2(l, MK + c)
                        multiplied(ch)
                        act.activation(mk[:, tile(c, MEM)], acc[ch.slot][:, 0:MEM], ACT.Copy)\
                            .then_inc(evacuated[ch.slot], 2)
                split(chunk2(l, MV + 2))
                split(chunk2(l, MV + 3))
                for t in range(KT):
                    if t in H_SPLITS:
                        split(chunk2(l, QL + H_SPLITS.index(t)))
                    h_hi_tile(t, t % 2, l * KT + (KT + t + 1))
                multiplied(chunk2(l, MV + MH - 1))
                act.activation(mv[:, :], sc[:, 1024:2048], ACT.Copy)

                def latent(p, t, sq_at):
                    c = chunk2(l, p)
                    if p > QL:
                        split(chunk2(l, p + 1))
                    multiplied(c)
                    square(acc[c.slot][:, :], sq_at, t % 2)
                    act.activation(g[:, tile(t)], acc[c.slot][:, :], ACT.Copy).then_inc(evacuated[c.slot], 1)

                def latent_hi(t, slot, count):
                    act.wait_ge(lat_normed, count)
                    act.activation(m_hi[:, tile(t)], htmp[:, tile(slot)], ACT.Copy).then_inc(lat_hi_done, 1)

                act.wait_ge(stored, l * (8 * KT) + (8 * KT + 16))
                for j in range(QRT):
                    latent(QL + j, KVRT + j, sq_no(l, QN) + j)
                for j in range(KVRT):
                    latent(KVL + j, j, sq_no(l, KVN) + j)
                split(chunk2(l, CONV))
                for j in range(QRT):
                    latent_hi(KVRT + j, j % 2, l * 6 + (j + 1))

                act.wait_ge(added, sq_no(l, KVN) + (KVRT + 2))
                with act.Fori(0, CT // 2) as i:
                    for j in range(2):
                        c = chunk2(l, CONV + 3 * j, i, 6)
                        split(chunk2(l, CONV + 3 * j + 1, i, 6))
                        multiplied(c)
                        before = chunk2(l, CONV + 3 * j - 2, i, 6)
                        act.wait_ge(evacuated[before.slot], before.uses + 1)
                        act.activation(cg, acc[c.slot][:, :], ACT.Copy).then_inc(evacuated[c.slot], 1)
                        split(chunk2(l, CONV + 3 * j + 2, i, 6))
                        split(chunk2(l, CONV + 3 * j + 3, i, 6))
                for j in range(KVRT):
                    latent_hi(j, j, l * 6 + (QRT + j + 1))

                act.wait_ge(lat_done, l * 6 + 6)
                for c in range(MH):
                    ch = chunk2(l, QM + c)
                    no = l * MH + (c + 1)
                    split(chunk2(l, QM + c + 1))
                    multiplied(ch)
                    act.activation(qm[:, tile(c % 2)], acc[ch.slot][:, :], ACT.Copy).then_inc(evacuated[ch.slot], 1)

                    def turned_mem(no):
                        act.wait_ge(turned_m, no)
                        for b in range(TB):
                            ins = act.activation(ptm[:, :].rearrange("p (k q) -> p k q", k=MB)[:, :, tile(b, P)],
                                                 bank(b, MEM).rearrange("p (k q) -> p k q", k=MB), ACT.Copy)
                        ins.then_inc(ptm_done, 1)

                    if c > 0:
                        turned_mem(no - 1)
                    act.wait_ge(shift_m, no)
                    for b in range(TB):
                        ins = act.activation(prob_a[:, tile(b, MEM)], bank(b, MEM), ACT.Exp, scale=MEM_SCALE,
                                             bias=nm[:, b:b + 1], accum_out=ls[:, b:b + 1])
                    ins.then_inc(exp_m, 1)
                turned_mem(l * MH + MH)

                with act.Fori(0, MLA // 2) as i:
                    for j in range(2):
                        no = l * MLA + (i * 2 + (j + 1))
                        hc, ga, gb = (chunk2(l, HEAD + 3 * j + n, i, 6) for n in range(3))
                        split(ga)
                        multiplied(hc)
                        act.activation(qn[:, :], acc[hc.slot][:, :], ACT.Copy).then_inc(evacuated[hc.slot], 1)
                        act.activation(kn[:, :], ov[1][:, :], ACT.Copy).then_inc(qkv_done, 1 if j == 0 else 2)
                        if j == 0:
                            act.wait_ge(values2, no)
                            act.activation(v[:, :], sc[:, 512:512 + TB * 256], ACT.Copy).then_inc(qkv_done, 1)
                        split(gb)
                        multiplied(ga)
                        before = chunk2(l, HEAD + 3 * j - 1, i, 6)
                        act.wait_ge(evacuated[before.slot], before.uses + 1)
                        act.activation(tz, acc[ga.slot][:, :], ACT.Tanh, scale=0.5).then_inc(tanh2, 1)
                        split(chunk2(l, HEAD + 3 * j + 3, i, 6))
                        act.wait_ge(shift2, no)
                        for b in range(TB):
                            ins = act.activation((prob_a, prob_b)[b // 2][:, tile(b % 2)], bank(b), ACT.Exp, scale=MLA_SCALE,
                                                 bias=nm[:, b:b + 1], accum_out=ls[:, b:b + 1])
                        ins.then_inc(exp2, 1)
                        multiplied(gb)
                        act.wait_ge(evacuated[ga.slot], ga.uses + 1)
                        act.activation(tz, acc[gb.slot][:, :], ACT.Tanh, scale=0.5).then_inc(tanh2, 1)
                        act.wait_ge(turned2, no)
                        act.wait_ge(values2, no)
                        for b in range(2):
                            act.activation(pt[:, :].rearrange("p (k q) -> p k q", k=TB)[:, :, tile(b, P)],
                                           bank(b).rearrange("p (k q) -> p k q", k=TB), ACT.Copy).then_inc(pt2_act, 1)

                act.wait_ge(chunk_done, l * N2 + (N1 + WO2))
                act.wait_ge(y_b, l * MLA + MLA)
                act.wait_ge(y_a, l * MLA + (LAST + 1))
                with act.Fori(0, LAST) as t:
                    y_hi_tile(t)
                with act.Fori(LAST + 1, KT) as t:
                    y_hi_tile(t)
                act.wait_ge(y_a, l * MLA + (MLA + 1))
                y_hi_tile(LAST)
                output(lambda p, i: chunk2(l, WO2 + p, i, 2), sq_no(l + 1, POSTN), l * KT + KT)

        @block.vector
        def _(dve):
            def split(c):
                dve.wait_ge(hi_done, c.n + 1)
                dve.tensor_tensor(lo[c.slot][:, :], raw[c.slot][:, :], hi[c.slot][:, :].bitcast(F32),
                                  ALU.subtract).then_inc(lo_done, 1)

            class Links:

                def __init__(self, sem_, start):
                    self.sem, self.start, self.n = sem_, start, 0

                def then(self, ins):
                    self.n += 1
                    ins.then_inc(self.sem, 1)
                    dve.wait_ge(self.sem, self.start + self.n)

            def norm(no, features_, sums_, n=TB):
                link = Links(norm_link, no * 4)
                dve.tensor_scalar(ms[:, 0:n], sums_, 1.0 / features_, EPS, ALU.mult, ALU.add).then_inc(ms_done, 1)
                dve.wait_ge(rs_done, no + 1)
                link.then(dve.tensor_tensor(nt[:, 0:n], r[:, 0:n], r[:, 0:n], ALU.mult))
                link.then(dve.tensor_tensor(nt[:, 0:n], nt[:, 0:n], ms[:, 0:n], ALU.mult))
                link.then(dve.tensor_scalar(nt[:, 0:n], nt[:, 0:n], -0.5, 1.5, ALU.mult, ALU.add))
                link.then(dve.tensor_tensor(r[:, 0:n], r[:, 0:n], nt[:, 0:n], ALU.mult))
                for b in range(n):
                    ins = dve.tensor_scalar(dg[:, tile(b, P)], ident, r[:, b:b + 1], None, ALU.mult)
                ins.then_inc(diag_done, 1)

            def token_norm(no, count, features_):
                dve.wait_ge(sums_done, count)
                norm(no, features_, ov[0][:, 0:TB])

            def normed(to, src, gain, r_b):
                return dve.scalar_tensor_tensor(to, src, gain, r_b, ALU.mult, ALU.mult)

            ang, kf, tmp = (angle[:, tile(n)] for n in range(3))
            rope = Links(rope_link, 0)
            for s in dve_from_one:
                dve.sem_inc(s, 1)
            dve.wait_ge(consts_in, 16)
            dve.wait_ge(pos_in, 16)
            rope.then(dve.tensor_copy(ang, posi[:, :]))
            rope.then(dve.tensor_scalar(ang, ang, cst[:, FREQ:FREQ + 1], None, ALU.mult))
            rope.then(dve.tensor_scalar(turns[:, :], ang, 1 / TWO_PI, None, ALU.mult))
            rope.then(dve.tensor_copy(kf, turns[:, :]))
            for part in (TURN_A, TURN_B, TURN_C):
                rope.then(dve.scalar_tensor_tensor(ang, kf, -part, ang, ALU.mult, ALU.add))
            rope.then(dve.tensor_scalar(ang, ang, cst[:, PHASE:PHASE + 1], None, ALU.add))
            for op, past, turn in ((ALU.is_gt, PI, -TWO_PI), (ALU.is_lt, -PI, TWO_PI)):
                rope.then(dve.tensor_scalar(tmp, ang, past, turn, op, ALU.mult))
                rope.then(dve.tensor_tensor(ang, ang, tmp, ALU.add))
            below_pi = float(np.nextafter(np.float32(np.pi), np.float32(0)))
            dve.tensor_scalar(ang, ang, below_pi, -below_pi, ALU.min, ALU.max).then_inc(angle_done, 1)

            dve.wait_ge(gains_in, 32)
            for t in range(1, KT):
                dve.wait_ge(x_squared, t + 1)
                if t > 1:
                    dve.wait_ge(x_added, t)
                a = sq[:, 0:S] if t == 1 else sqacc[:, :]
                dve.tensor_tensor(sqacc[:, :], a, sq[:, tile(t % 2)], ALU.add).then_inc(x_added, 2 if t == 1 else 1)
            token_norm(0, 1, D)
            split(chunk1(0))

            def h_tiles(gain, r_b, before, half_before, splits):
                for t in range(KT + 1):
                    if t in splits:
                        split(splits[t])
                    if t < KT:
                        if t >= 2 or not isinstance(before, int):
                            dve.wait_ge((h_even, h_odd)[t % 2], half_before + t // 2)
                        normed(htmp[:, tile(t % 2)], g[:, tile(t)], gn[:, col(gain + t)], r_b).then_inc(normed_done, 1)
                    if t % 2 == 1:
                        dve.wait_ge(h_hi_done, before + t)
                        x = tile(t - 1)
                        dve.tensor_tensor(h_lo[:, x], htmp[:, 0:S], h_hi[:, x].bitcast(F32), ALU.subtract).then_inc(h_even, 1)

            dve.wait_ge(r_done, 1)
            h_tiles(PRE1, bank(0), 0, 0, {4: chunk1(1)})
            dve.wait_ge(mem_ss, 1)
            norm(1, D, ss, MB)
            dve.wait_ge(sin_done, 1)
            rope.then(dve.tensor_scalar(cs[:, :], ang, cst[:, SIGN:SIGN + 1], None, ALU.mult))
            for n in range(2, PAIR1 + 1):
                split(chunk1(n))

            def softmax_first(i):
                link = Links(soft1_link, i * 5)
                dve.wait_ge(scores1, i + 2)
                for par in range(2):
                    half_ = tile(par, 1024)
                    ins = dve.scalar_tensor_tensor(prob1[:, half_], win[:, :], cst[:, col(i * 2 + (SLOPE + par))], sc[:, half_],
                                                   ALU.mult, ALU.add)
                link.then(ins)
                link.then(dve.tensor_reduce(mx, prob1[:, :].rearrange("p (n k) -> p n k", n=2 * TB), AX.X, ALU.max))
                sinks_ = [snk[:, col(i * 2 + par)] for par in range(2)]
                for par in range(2):
                    ins = dve.tensor_scalar(mx[:, tile(par, TB)], mx[:, tile(par, TB)], sinks_[par], None, ALU.max)
                link.then(ins)
                for par in range(2):
                    dve.tensor_scalar(es[:, tile(par, TB)], mx[:, tile(par, TB)], -1.0, sinks_[par], ALU.mult, ALU.add)
                dve.tensor_scalar(nm, mx, -1.0, None, ALU.mult).then_inc(shift1, 1)
                dve.wait_ge(exp1, i + 1)
                link.then(dve.tensor_tensor(ls, ls, es, ALU.add))
                link.then(dve.reciprocal(rl, ls))
                for n in range(2 * TB):
                    ins = dve.tensor_scalar(prob1[:, tile(n, 256)], prob1[:, tile(n, 256)], rl[:, n:n + 1], None, ALU.mult)
                ins.then_inc(probs1, 1)
                assert link.n == 5

            def y_first(i):
                zc = chunk1(PAIR1 + 1, i)
                dve.wait_ge(values1, i + 2)
                dve.wait_ge(evacuated[zc.slot], zc.uses + 1)
                for par in range(2):
                    rows_ = slice(HD * par, HD * par + HD)
                    ins = dve.scalar_tensor_tensor(g[rows_, tile(i)], ov[par][rows_, :], 0.5, sg[rows_, :], ALU.mult, ALU.mult)
                ins.then_inc(y1, 1)

            def turned_first(i):
                dve.wait_ge(turned1, i + 1)
                for b in range(2, TB):
                    dve.tensor_copy(pt1[:, tile(b)], bank(b)).then_inc(pt1_dve, 1)

            def pair(i, first):
                zc = chunk1(PAIR1 + 1, i)
                split(zc)
                if not first:
                    turned_first(i - 1)
                    y_first(i - 1)
                split(chunk1(PAIR1 + 2, i))
                softmax_first(i)
                dve.wait_ge(tanh1, i + 1)
                dve.scalar_tensor_tensor(sg, tz, 1.0, acc[zc.slot][:, :], ALU.add, ALU.mult).then_inc(evacuated[zc.slot], 1)

            def y_lo_tile(t, count):
                dve.wait_ge(y_hi_done, count)
                dve.tensor_tensor(h_lo[:, tile(t)], g[:, tile(t)], h_hi[:, tile(t)].bitcast(F32),
                                  ALU.subtract).then_inc(y_done, 1)

            dve.wait_ge(window_in, 16)
            dve.wait_ge(stored, 16)
            pair(0, True)
            with dve.Fori(1, PAIRS) as i:
                pair(i, False)
            turned_first(PAIRS - 1)
            with dve.Fori(0, KT - 1) as t:
                y_lo_tile(t, t + 1)
            y_first(PAIRS - 1)
            y_lo_tile(KT - 1, KT)

            def output_tile(t, slot, nxt, gain, m_at):
                if nxt is not None:
                    split(nxt)
                normed(dg[:, tile(slot, MEM)], area[:, tile(t, MEM)], gn[:, col(gain + t)], r_mem[:, :]).then_inc(mt_done, 1)
                dve.wait_ge(mhi_done, m_at + 1)
                dve.tensor_tensor(m_lo[:, tile(t, MEM)], dg[:, tile(slot, MEM)], m_hi[:, tile(t, MEM)].bitcast(F32),
                                  ALU.subtract).then_inc(m_done, 1)

            def output(chunk, gain, m_at):
                with dve.Fori(0, KT // 2 - 1) as i:
                    for j in range(2):
                        output_tile(i * 2 + j, j, chunk(j + 1, i), gain, i * 2 + (m_at + j))
                for j in range(2):
                    t = KT - 2 + j
                    output_tile(t, j, chunk(1, KT // 2 - 1) if j == 0 else None, gain, m_at + t)

            dve.wait_ge(r_mem_done, 1)
            dve.wait_ge(memory_in, 16)
            output(lambda p, i: chunk1(WO1 + p, i), MEMG, 0)

            def new_x(t, l):
                normed(g[:, tile(t)], g[:, tile(t)], gn[:, col(l * KT + (t + POST))], bank(0)).then_inc(scaled, 1)
                if t % 2 == 0:
                    w = t // 2
                    dve.wait_ge(scaled, l * KT + (t + 1))
                    dve.wait_ge(residual_in[w % 2], l * (4 * KT) + 16 * (w // 2 + 1))
                    dve.tensor_tensor(g[:, tile(t)], g[:, tile(t)], xr[:, tile(w % 2 * 2)], ALU.add).then_inc(x_even, 1)

            with dve.Fori(0, LAYERS) as l:
                split(chunk2(l, 0))
                for c in (chunk2(l, 0), chunk2(l, 1)):
                    dve.wait_ge(evacuated[c.slot], c.uses)
                token_norm(norm_no(l, POSTN), l * 4 + 2, D)
                split(chunk2(l, MK + 1))
                dve.wait_ge(r_done, norm_no(l, POSTN) + 1)
                for c in range(MH + 1):
                    if c > 0:
                        split(chunk2(l, MK + c + 1))
                    for t in STEPS[c]:
                        new_x(t, l)
                split(chunk2(l, MV + 2))
                token_norm(norm_no(l, PREN), l * 4 + 3, D)
                split(chunk2(l, MV + 3))
                dve.wait_ge(r_done, norm_no(l, PREN) + 1)
                h_tiles(l * GN + (GL + PRE), bank(1), l * KT + KT, l * ODD + ODD,
                        {t: chunk2(l, QL + n) for n, t in enumerate(H_SPLITS)})
                for j in range(1, QRT + 1):
                    split(chunk2(l, QL + j + 1))

                def latents(first, tiles, gain, r_b, before):
                    for n in range(tiles):
                        if before + n < 2:
                            dve.wait_ge((h_even, h_odd)[n], l * ODD + 2 * ODD)
                        else:
                            dve.wait_ge(lat_done, l * 6 + (before + n - 1))
                        normed(htmp[:, tile(n % 2)], g[:, tile(first + n)], gn[:, col(l * GN + (GL + gain + n))], r_b)\
                            .then_inc(lat_normed, 1)
                        dve.wait_ge(lat_hi_done, l * 6 + (before + n + 1))
                        x = tile(first + n)
                        dve.tensor_tensor(m_lo[:, x], htmp[:, tile(n % 2)], m_hi[:, x].bitcast(F32),
                                          ALU.subtract).then_inc(lat_done, 1)

                token_norm(norm_no(l, QN), l * 4 + 4, QRT * P)
                split(chunk2(l, KPE))
                split(chunk2(l, CONV))
                dve.wait_ge(r_done, norm_no(l, QN) + 1)
                for j in range(QRT):
                    c = chunk2(l, QL + j)
                    dve.wait_ge(evacuated[c.slot], c.uses + 1)
                latents(KVRT, QRT, QG, bank(0), 0)

                def rotate(to, src, sem_, start):
                    link = Links(sem_, start)
                    dve.tensor_tensor(to[0:64, :], src[0:64, :], cs[0:64, :], ALU.mult).then_inc(sem_, 1)
                    link.n = 1
                    link.then(dve.tensor_tensor(dg[0:64, :], src[64:128, :], cs[64:128, :], ALU.mult))
                    return link

                kc = chunk2(l, KPE)
                dve.wait_ge(chunk_done, kc.n + 1)
                rotate(kr, acc[kc.slot], kr_link, l * 2)
                dve.tensor_tensor(kr[0:64, :], kr[0:64, :], dg[0:64, :], ALU.add).then_inc(evacuated[kc.slot], 1)
                token_norm(norm_no(l, KVN), l * 4 + 5, KVRT * P)
                dve.memset(u[:, 0:1], 0.0)
                dve.memset(u[:, S + 1:S + 2], 0.0).then_inc(u_pad, 1)
                dve.wait_ge(u_pad, l + 1)
                dve.sem_inc(waited, 1)

                with dve.Fori(0, CT // 2) as i:
                    for j in range(2):
                        gc, xi, gb = (chunk2(l, CONV + 3 * j + n, i, 6) for n in range(3))
                        link = Links(conv_link, l * (3 * CT) + (i * 6 + 3 * j))
                        taps = [gn[:, col(l * GN + (i * 6 + (GL + TAP + 3 * j + n)))] for n in range(3)]
                        split(xi)
                        split(gb)
                        dve.wait_ge(chunk_done, xi.n + 1)
                        dve.wait_ge(evacuated[gc.slot], gc.uses + 1)
                        dve.tensor_tensor(u[:, 1:S + 1], acc[xi.slot][:, :], cg, ALU.mult).then_inc(evacuated[xi.slot], 1)
                        dve.wait_ge(evacuated[xi.slot], xi.uses + 1)
                        link.then(dve.tensor_scalar(cv, u[:, 0:S], taps[0], None, ALU.mult))
                        for n in (1, 2):
                            link.then(dve.scalar_tensor_tensor(cv, u[:, n:n + S], taps[n], cv, ALU.mult, ALU.add))
                        split(chunk2(l, CONV + 3 * j + 3, i, 6))
                        dve.wait_ge(chunk_done, gb.n + 1)
                        dve.tensor_tensor(g[:, tile(i * 2 + (MLA + j))], acc[gb.slot][:, :], cv, ALU.mult)\
                            .then_inc(evacuated[gb.slot], 1)
                dve.wait_ge(r_done, norm_no(l, KVN) + 1)
                for j in range(KVRT):
                    c = chunk2(l, KVL + j)
                    dve.wait_ge(evacuated[c.slot], c.uses + 1)
                latents(0, KVRT, KVG, bank(1), QRT)

                banks = sc[:, :].rearrange("p (b n) -> p b n", b=TB)
                for c in range(MH):
                    no = l * MH + (c + 1)
                    link = Links(soft_m_link, l * (2 * MH) + 2 * c)

                    def mem_out(c):
                        dve.wait_ge(values_m, l * MH + (c + 1))
                        dve.tensor_copy(g[:, tile(MLA + CT + c)], ov[1][:, :]).then_inc(om_done, 1)

                    split(chunk2(l, QM + c + 1))
                    if c > 0:
                        mem_out(c - 1)
                    dve.wait_ge(scores_m, no)
                    link.then(dve.tensor_reduce(mx[:, 0:TB], banks[:, :, 0:MEM], AX.X, ALU.max))
                    dve.tensor_scalar(nm[:, 0:TB], mx[:, 0:TB], -MEM_SCALE, None, ALU.mult).then_inc(shift_m, 1)
                    dve.wait_ge(exp_m, no)
                    link.then(dve.reciprocal(rl[:, 0:TB], ls[:, 0:TB]))
                    for b in range(TB):
                        ins = dve.tensor_scalar(prob_a[:, tile(b, MEM)], prob_a[:, tile(b, MEM)], rl[:, b:b + 1], None, ALU.mult)
                    ins.then_inc(probs_m, 1)
                mem_out(MH - 1)

                def y_head(no, t):
                    dve.wait_ge(values2, no + 1)
                    dve.scalar_tensor_tensor(g[:, tile(t)], ov[0][:, :], 0.5, sg, ALU.mult, ALU.mult).then_inc(y_a, 1)

                def head(i, j, first):
                    h = i * 2 + j
                    no = l * MLA + (i * 2 + (j + 1))
                    hc, ga, gb = (chunk2(l, HEAD + 3 * j + n, i, 6) for n in range(3))
                    link = Links(soft2_link, (no - 1) * 2)
                    split(ga)
                    dve.wait_ge(chunk_done, hc.n + 1)
                    rotate(qr, bank(0), qr_done, (no - 1) * 3)
                    dve.tensor_tensor(qr[0:64, :], qr[0:64, :], dg[0:64, :], ALU.add).then_inc(qr_done, 1)
                    split(gb)
                    if not first:
                        y_head(no - 1, h - 1)
                    dve.wait_ge(y_a, no)
                    dve.wait_ge(tanh2, no * 2 - 1)
                    dve.scalar_tensor_tensor(sg, tz, 1.0, acc[ga.slot][:, :], ALU.add, ALU.mult).then_inc(evacuated[ga.slot], 1)
                    split(chunk2(l, HEAD + 3 * j + 3, i, 6))
                    dve.wait_ge(scores2, no)
                    link.then(dve.tensor_reduce(mx[:, 0:TB], banks, AX.X, ALU.max))
                    dve.tensor_scalar(nm[:, 0:TB], mx[:, 0:TB], -MLA_SCALE, None, ALU.mult).then_inc(shift2, 1)
                    dve.wait_ge(exp2, no)
                    link.then(dve.reciprocal(rl[:, 0:TB], ls[:, 0:TB]))
                    for b in range(TB):
                        pr = (prob_a, prob_b)[b // 2][:, tile(b % 2)]
                        ins = dve.tensor_scalar(pr, pr, rl[:, b:b + 1], None, ALU.mult)
                    ins.then_inc(probs2, 1)
                    dve.wait_ge(tanh2, no * 2)
                    dve.scalar_tensor_tensor(dg[:, :], tz, 1.0, acc[gb.slot][:, :], ALU.add, ALU.mult).then_inc(evacuated[gb.slot], 1)
                    dve.wait_ge(evacuated[gb.slot], gb.uses + 1)
                    x = tile(h + MLA)
                    dve.scalar_tensor_tensor(g[:, x], g[:, x], 0.5, dg[:, :], ALU.mult, ALU.mult).then_inc(y_b, 1)
                    dve.wait_ge(turned2, no)
                    for b in range(2, TB):
                        dve.tensor_copy(pt[:, :].rearrange("p (k q) -> p k q", k=TB)[:, :, tile(b, P)],
                                        bank(b).rearrange("p (k q) -> p k q", k=TB)).then_inc(pt2_dve, 1)

                head(0, 0, True)
                head(0, 1, False)
                with dve.Fori(1, MLA // 2) as i:
                    head(i, 0, False)
                    head(i, 1, False)
                y_count = l * KT + KT
                with dve.Fori(0, LAST) as t:
                    y_lo_tile(t, y_count + t + 1)
                with dve.Fori(LAST + 1, KT) as t:
                    y_lo_tile(t, y_count + t)
                y_head(l * MLA + MLA, LAST)
                y_lo_tile(LAST, y_count + KT)
                dve.wait_ge(memory_in, l * 16 + 32)
                dve.sem_inc(waited, 1)
                output(lambda p, i: chunk2(l, WO2 + p, i, 2), l * KT + (MEMG + KT), l * KT + KT)

            for c in (chunk2(LAYERS, 0), chunk2(LAYERS, 1)):
                dve.wait_ge(evacuated[c.slot], c.uses)
            token_norm(norm_no(LAYERS, POSTN), LAYERS * 4 + 2, D)
            dve.wait_ge(r_done, norm_no(LAYERS, POSTN) + 1)
            for t in range(KT):
                new_x(t, LAYERS)


def kernel(**inputs):
    import numpy as np
    import concourse.bacc as bacc
    from concourse import mybir
    from concourse.bass_utils import run_bass_kernel_spmd

    P, D, S, MEM, KT = 128, 2048, 512, 256, 16
    a = {k: np.asarray(x) for k, x in inputs.items()}

    def turned(x):
        t, f = x.shape
        return np.ascontiguousarray(x.T.reshape(f // P, P, t).transpose(1, 0, 2).reshape(P, -1))

    def chunk(w):
        k, c = w.shape
        return w.reshape(k // P, P, c).transpose(1, 0, 2).reshape(P, -1)

    def wide(w, tiles):
        k, c = w.shape
        return list(w.reshape(-1, tiles, P, c).transpose(0, 2, 1, 3).reshape(-1, P, tiles * c))

    def per_partition(x):
        return x.reshape(-1, P).T

    def swapped(w):
        return np.concatenate([w, w[:, 32:], w[:, :32]], axis=1)

    wi = a["w_in_a"][0]
    tiles = []
    for i in range(16):
        tiles += [wi[:, P * i:P * (i + 1)], wi[:, 2560 + P * i:2560 + P * (i + 1)]]
    tiles += [a["w_out_a"][0][:, P * i:P * (i + 1)] for i in range(16)]
    keys = [chunk(wi[:, 2048 + P * c:2048 + P * (c + 1)]) for c in range(2)]
    w1 = np.stack(keys + wide(wi[:, 2304:2560], 8) + [chunk(t) for t in tiles], axis=1)

    w2 = []
    for l in range(2):
        wi, uq, ukv = a["w_in_2"][l], a["w_uq_2"][l], a["w_ukv_2"][l]
        col = lambda w, at: w[:, at:at + P]
        out = [chunk(col(a["w_mk_2"][l], P * c)) for c in range(4)] + wide(a["w_mv_2"][l], 4)
        tiles = [col(wi, P * c) for c in range(6)] + [swapped(wi[:, 768:832])]
        for c in range(4):
            tiles += [col(wi, 1344 + P * c), col(wi, 1856 + P * c), col(wi, 832 + P * c)]
        tiles += [col(wi, 2368 + P * c) for c in range(4)]
        out += [chunk(t) for t in tiles]
        for h in range(8):
            q = uq[:, 192 * h:192 * (h + 1)]
            q = chunk(np.concatenate([q[:, :128], swapped(q[:, 128:])], axis=1))
            parts = [q, chunk(ukv[:, 256 * h:256 * h + P])]
            if h % 2 == 0:
                parts.append(chunk(np.concatenate([ukv[:, 256 * n + P:256 * (n + 1)] for n in (h, h + 1)], axis=1)))
            parts.append(np.zeros((P, KT * P - sum(x.shape[1] for x in parts)), q.dtype))
            out.append(np.concatenate(parts, axis=1))
            out += [chunk(col(wi, 2880 + P * h)), chunk(col(wi, 2880 + P * (8 + h)))]
        w2 += out + [chunk(col(a["w_o_2"][l], P * c)) for c in range(16)]
    w2 = np.stack(w2, axis=1)

    gains = [per_partition(a["g_pre"][0]), per_partition(a["g_post"][0])]
    gains += [per_partition(a["post_norm_g_2"][l]) for l in range(2)]
    gains += [per_partition(a["mem_norm_g_2"][l]) for l in (0, 1, 1)]
    for l in range(2):
        gains += [per_partition(a[n][l]) for n in ("pre_norm_g_2", "q_norm_g_2", "kv_norm_g_2")]
        gains.append(a["conv_w_2"][l].reshape(3, 4, P).transpose(2, 1, 0).reshape(P, 12))

    row = np.arange(P)
    freq = (1.0 / (np.float32(10000.0) ** (np.arange(0, 64, 2, dtype=np.float32) / np.float32(64)))).astype(np.float32)
    slopes = (2.0 ** (-8.0 * np.arange(1, 33, dtype=np.float32) / 32)).astype(np.float32)
    consts = np.concatenate([
        np.eye(P, dtype=np.float32), np.ones((P, P), np.float32), np.broadcast_to(slopes, (P, 32)),
        freq[row % 32][:, None], np.where(row < 64, np.float32(np.pi / 2), np.float32(0))[:, None].astype(np.float32),
        np.where((row >= 64) & (row < 96), -1.0, 1.0)[:, None].astype(np.float32)], axis=1)
    dist = (row[:, None] + P - np.arange(2 * P)[None, :]).astype(np.float32)
    seen = (dist >= 0) & (dist < P)
    window = np.concatenate([np.where(seen & (np.arange(2 * P) >= P)[None, :], -dist, np.float32(-1e30))]
                            + [np.where(seen, -dist, np.float32(-1e30))] * 3, axis=1).astype(np.float32)

    arrays = {
        "xT": turned(a["x"][0]), "memT": turned(a["mem_2"][0]),
        "mem": np.ascontiguousarray(a["mem_2"][0].reshape(2, P, D).transpose(1, 0, 2)),
        "pos": a["positions_2"][0], "gains": np.concatenate(gains, axis=1), "sinks": a["sinks_a"][0],
        "consts": consts, "window": window, "w1": w1, "w2": w2,
    }
    nc = bacc.Bacc("TRN2", target_bir_lowering=False, num_devices=1)
    send, aps = {}, []
    for name, x in arrays.items():
        send[name + "_dram"] = np.ascontiguousarray(x)
        aps.append(nc.dram_tensor(name + "_dram", x.shape, mybir.dt.from_np(x.dtype), kind="ExternalInput").ap())
    out = nc.dram_tensor("out_dram", (P, KT * S), mybir.dt.float32, kind="ExternalOutput").ap()
    build(nc, *aps, out)
    r = run_bass_kernel_spmd(nc, [send], core_ids=[0])
    y = np.asarray(r.results[0]["out_dram"]).reshape(P, KT, S)
    return np.ascontiguousarray(y.transpose(2, 1, 0).reshape(1, S, D))
```

```python
def build(nc, xT, memT, mem, pos, gains, sinks, consts, window, w1, w2, out):
    from contextlib import ExitStack

    import numpy as np
    import concourse.bass as bass
    from concourse import mybir

    F32, F32R, I32 = mybir.dt.float32, mybir.dt.float32r, mybir.dt.int32
    ACT = mybir.ActivationFunctionType
    ALU = mybir.AluOpType
    AX = mybir.AxisListType

    P = 128
    D, S, MEM = 2048, 512, 256
    KT, TB, MB = D // P, S // P, MEM // P
    EPS = 1e-6
    CW = KT * P

    HD, PAIRS, KVH = 64, 16, 4
    PAIR1 = 4
    N1 = PAIR1 + 2 * PAIRS

    LAYERS, MLA, MH, CT = 2, 8, 4, 4
    WO, MK, MV, QL, KVL, KPE, CONV, QM, HEAD = 0, 16, 20, 24, 28, 30, 31, 43, 47
    N2 = HEAD + 3 * MLA
    QRT, KVRT = 4, 2
    UK = QRT * 256
    UV = UK + KVRT * P
    HW = (UV + KVRT * 2 * P, UV)
    MLA_SCALE, MEM_SCALE = (128 + 64) ** -0.5, P ** -0.5
    STEPS = ((0, 1, 2, 3), (4, 5), (6, 7, 8, 9), (10, 11), (12, 13, 14, 15))
    H_SPLITS = (2, 7)

    PRE1, POST, MEMG, GL, GN = 0, 16, 64, 96, 34
    PRE, QG, KVG, TAP = 0, 16, 20, 22
    IDENT, ONES, SLOPE, FREQ, PHASE, SIGN, C_COLS = 0, 128, 256, 288, 289, 290, 291
    TWO_PI, PI = float(2 * np.pi), float(np.float32(np.pi))
    TURN_A = 6.28125
    TURN_B = float(np.round((TWO_PI - TURN_A) * 2 ** 20) / 2 ** 20)
    TURN_C = TWO_PI - TURN_A - TURN_B

    class Chunk:

        def __init__(self, n, slot, uses, back):
            self.n, self.slot, self.uses, self.back = n, slot, uses, back

    def chunk1(p, i=0):
        new = isinstance(i, int) and i == 0 and p < 2
        return Chunk(i * 2 + p, p % 2, i + p // 2, None if new else 2)

    def chunk2(l, p, i=0, stride=0):
        turns = p // N2
        p = p % N2
        slot = p % 2
        per_turn = (N2 + 1 - slot) // 2
        n = l * N2 + (N1 + turns * N2 + p)
        uses = l * per_turn + (N1 // 2 + turns * per_turn + p // 2)
        if stride:
            n, uses = n + i * stride, uses + i * (stride // 2)
        return Chunk(n, slot, uses, 1 if p == 0 and stride == 0 else 2)

    POSTN, PREN, QN, KVN = 2, 3, 4, 5

    def norm_no(l, which):
        return l * 4 + which

    SQ_LAYER = KT + KT + QRT + KVRT
    ODD = KT // 2
    XR = 3

    def sq_no(l, which):
        return l * SQ_LAYER + (0, KT, 2 * KT, 2 * KT + QRT, SQ_LAYER)[which - 2]

    def loads_of(l, w):
        slot = w % XR
        return slot, l * len(range(slot, ODD, XR)) + (w // XR + 1)

    residual = nc.dram_tensor("residual", (LAYERS + 1, P, KT * S), F32, kind="Internal").ap()\
        .rearrange("l p c -> p l c")
    ctx = ExitStack()
    with ctx:
        free = [(nc.sbuf_base + 63) // 64 * 64]

        def sb(name, cols, dt=F32, at=None):
            if at is None:
                at = free[0]
                free[0] += (cols * 4 + 63) // 64 * 64
            return nc.alloc_sbuf_tensor_at(name, [P, cols], dt, offset=at)

        raw = [sb(f"raw{s}", CW) for s in range(2)]
        hi = [sb(f"hi{s}", CW, F32R) for s in range(2)]
        lo = [sb(f"lo{s}", CW, F32R) for s in range(2)]
        h_hi, h_lo = sb("h_hi", KT * S, F32R), sb("h_lo", KT * S, F32R)
        g = sb("g", KT * S)
        m0 = free[0]
        m_hi, m_lo = sb("m_hi", KT * MEM, F32R), sb("m_lo", KT * MEM, F32R)
        m1 = m0 + 4 * KT * MEM
        a0 = free[0]
        area = sb("area", 4096)
        cst = sb("cst", C_COLS)
        gn = sb("gn", GL + LAYERS * GN)
        snk = sb("snk", 2 * PAIRS)
        cs = sb("cs", S)
        kr = sb("kr", S)
        r_mem = sb("r_mem", MEM)
        sqacc, sq, dg = sb("sqacc", S), sb("sq", 2 * S), sb("dg", S)
        qr = sqacc
        st = sb("st", 64)
        prob1, pt1 = sb("prob1", 2048, at=m0), sb("pt1", 2048, at=m0 + 8192)
        kdup, vall, win = sb("kdup", KVH * S, at=m1), sb("vall", TB * 256, at=m1 + 8192), sb("win", TB * 256, at=m1 + 12288)
        angle, posi = sb("angle", 3 * S, at=m0), sb("posi", S, I32, at=m0 + 12288)
        turns, memrow1 = sb("turns", S, I32, at=m0 + 14336), sb("memrow1", D, at=m1 + 2048)
        memrow0, sqx = sb("memrow0", D, at=a0 + 8192), sb("sqx", 4 * S, at=a0)
        x_last = sb("x_last", KT * S, at=m0)
        prob_a, prob_b = sb("prob_a", 1024, at=m0 + 12288), sb("prob_b", 1024, at=m1 + 12288)
        kcur, vcur, q1 = sb("kcur", 640, at=a0), sb("vcur", 512, at=a0 + 2560), sb("q1", S, at=a0 + 4608)
        htmp, xr = sb("htmp", 2 * S, at=a0), sb("xr", 2 * XR * S, at=a0)
        u = sb("u", S + 2, at=a0 + 4096)
        qm, ptm = sb("qm", 2 * S, at=a0), sb("ptm", MB * S, at=a0 + 4096)
        mv, mk = sb("mv", MB * 512, at=a0 + 8192), sb("mk", MH * MEM, at=a0 + 12288)
        qn, kn, v = sb("qn", S, at=a0), sb("kn", S, at=a0 + 2048), sb("v", TB * 256, at=a0 + 4096)
        pt = sb("pt", TB * S, at=a0 + 8192)
        tz, sg = sq[:, 0:S], sq[:, S:2 * S]
        cv, cg = sq[:, 0:S], sq[:, S:2 * S]

        ident, ones = cst[:, IDENT:IDENT + P], cst[:, ONES:ONES + P]
        ms, r, nt, half = st[:, 0:4], st[:, 4:8], st[:, 8:12], st[:, 12:16]
        mx, nm, ls, es, rl = (st[:, 16 + 8 * i:24 + 8 * i] for i in range(5))
        ss = st[:, 56:58]

        acc = [ctx.enter_context(nc.psum_tensor(f"acc{s}", [P, 512], F32)) for s in range(2)]
        ov = [ctx.enter_context(nc.psum_tensor(f"ov{s}", [P, 512], F32)) for s in range(2)]
        sc = ctx.enter_context(nc.psum_tensor("sc", [P, 2048], F32))

        def bank(b, n=512, off=0):
            return sc[:, 512 * b + off:512 * b + off + n]

        def tile(t, n=S):
            return slice(t * n, (t + 1) * n) if isinstance(t, int) else bass.ds(t * n, n)

        def col(c):
            return slice(c, c + 1) if isinstance(c, int) else bass.ds(c, 1)

        def sem(name):
            return ctx.enter_context(nc.semaphore(name))

        loaded = [sem("loaded0"), sem("loaded1")]
        consts_in, pos_in, gains_in, window_in = (sem(f"{n}_in") for n in ("consts", "pos", "gains", "window"))
        x_in = [sem(f"x_in{c}") for c in range(4)]
        memrows_in, memory_in, residual_in = sem("memrows_in"), sem("memory_in"), [sem(f"residual_in{n}") for n in range(XR)]
        x_last_in = [sem(f"x_last_in{c}") for c in range(4)]
        x_stored, stored, out_stored = sem("x_stored"), sem("residual_stored"), sem("out_stored")
        waited = sem("waited")
        hi_done, lo_done, chunk_done = sem("hi_done"), sem("lo_done"), sem("chunk_done")
        evacuated = [sem("evacuated0"), sem("evacuated1")]
        squared, added, sums_done, ms_done, rs_done = (
            sem(n) for n in ("squared", "added", "sums_done", "ms_done", "rs_done"))
        x_squared, x_added = sem("x_squared"), sem("x_added")
        diag_done, r_done, norm_link, half_set = (sem(n) for n in ("diag_done", "r_done", "norm_link", "half_set"))
        normed_done, h_hi_done, h_even, h_odd = (sem(n) for n in ("normed", "h_hi_done", "h_even", "h_odd"))
        y_hi_done, y_done = sem("y_hi_done"), sem("y_done")
        mem_ss, r_mem_done = sem("mem_ss"), sem("r_mem_done")
        mt_done, mhi_done, m_done = (sem(n) for n in ("mem_normed", "mem_hi_done", "m_done"))
        scaled, x_even, x_odd = sem("scaled"), sem("x_even"), sem("x_odd")
        rope_link, angle_done, sin_done = sem("rope_link"), sem("angle_done"), sem("sin_done")
        kcur_pad, kcur_done, vcur_done, v_in = sem("kcur_pad"), sem("kcur_done"), sem("vcur_done"), sem("v_in")
        scores1, soft1_link, shift1, exp1, probs1 = (
            sem(n) for n in ("scores1", "soft1_link", "shift1", "exp1", "probs1"))
        turned1, pt1_act, pt1_dve, values1, tanh1, y1 = (
            sem(n) for n in ("turned1", "pt1_act", "pt1_dve", "values1", "tanh1", "y1"))
        lat_normed, lat_hi_done, lat_done = sem("lat_normed"), sem("lat_hi_done"), sem("lat_done")
        kr_link, conv_link, u_pad = sem("kr_link"), sem("conv_link"), sem("u_pad")
        scores_m, soft_m_link, shift_m, exp_m, probs_m, turned_m, ptm_done, values_m, om_done = (
            sem(n) for n in ("scores_m", "soft_m_link", "shift_m", "exp_m", "probs_m", "turned_m", "ptm_done", "values_m", "om_done"))
        qkv_done, qr_done, scores2, soft2_link, shift2, exp2, probs2 = (
            sem(n) for n in ("qkv_done", "qr_done", "scores2", "soft2_link", "shift2", "exp2", "probs2"))
        turned2, pt2_act, pt2_dve, values2, tanh2, gate_b, y_a, y_b = (
            sem(n) for n in ("turned2", "pt2_act", "pt2_dve", "values2", "tanh2", "gate_b", "y_a", "y_b"))
        pe_from_one, dve_from_one = (scores1, values1, values2), (y1, om_done, y_a)
        block = ctx.enter_context(nc.Block())

        @block.sync
        def _(sp):
            sp.dma_start(cst[:, :], consts).then_inc(consts_in, 16)
            for c in range(4):
                part = tile(c, 4 * S)
                sp.dma_start(g[:, part], xT[:, part]).then_inc(x_in[c], 16)
            sp.dma_start(gn[:, :], gains).then_inc(gains_in, 16)

            def load(c, src, width=CW):
                if c.back is not None:
                    sp.wait_ge(lo_done, c.n + (1 - c.back))
                sp.dma_start(raw[c.slot][:, 0:width], src).then_inc(loaded[c.slot], 16)

            load(chunk1(0), w1[:, 0, :])
            load(chunk1(1), w1[:, 1, :])
            sp.dma_start(posi[:, :], pos.partition_broadcast(P)).then_inc(pos_in, 16)
            sp.dma_start(snk[:, :], sinks.partition_broadcast(P)).then_inc(window_in, 16)
            sp.dma_start(win[:, :], window).then_inc(window_in, 16)
            sp.dma_start(memrow0[:, :], mem[:, 0, :]).then_inc(memrows_in, 16)
            sp.dma_start(memrow1[:, :], mem[:, 1, :]).then_inc(memrows_in, 16)
            with sp.Fori(1, N1 // 2) as i:
                for j in range(2):
                    load(chunk1(j, i), w1[:, bass.ds(i * 2 + j, 1), :])
            with sp.Fori(0, LAYERS) as l:
                def load2(p, i=0, stride=0, width=CW):
                    c = chunk2(l, p, i, stride)
                    load(c, w2[:, bass.ds(c.n - N1, 1), 0:width], width)

                load2(0)
                load2(1)
                with sp.Fori(0, (HEAD - 3) // 2) as i:
                    load2(2, i, 2)
                    load2(3, i, 2)
                load2(HEAD - 1)
                with sp.Fori(0, MLA // 2) as i:
                    for j in range(6):
                        load2(HEAD + j, i, 6, HW[j // 3] if j % 3 == 0 else CW)
            for p in range(2):
                load(chunk2(LAYERS, p), w2[:, LAYERS * N2 + p, :])
            with sp.Fori(1, KT // 2) as i:
                for p in range(2):
                    load(chunk2(LAYERS, p, i, 2), w2[:, bass.ds(i * 2 + (LAYERS * N2 + p), 1), :])

        @block.gpsimd
        def _(pool):
            def settle():
                pool.sem_inc(waited, 1)

            def add_square(no, slot):
                pool.wait_ge(squared, no + 1)
                pool.wait_ge(added, no + 2)
                pool.tensor_tensor(sqacc[:, :], sqacc[:, :], sq[:, tile(slot)], ALU.add).then_inc(added, 1)

            def add_first_squares(no):
                pool.wait_ge(squared, no + 2)
                pool.tensor_tensor(sqacc[:, :], sq[:, 0:S], sq[:, S:2 * S], ALU.add).then_inc(added, 2)

            def add_squares(no, tiles):
                add_first_squares(no)
                with pool.Fori(1, tiles // 2) as i:
                    add_square(i * 2 + no, 0)
                    add_square(i * 2 + no + 1, 1)

            def root(no, n=TB):
                pool.wait_ge(ms_done, no + 1)
                pool.tensor_tensor(r[:, 0:n], ms[:, 0:n], half[:, 0:n], ALU.pow).then_inc(rs_done, 1)

            pool.sem_inc(added, 2)
            pool.memset(half, -0.5).then_inc(half_set, 1)
            pool.wait_ge(half_set, 1)
            for c in range(4):
                pool.wait_ge(x_in[c], 16)
            pool.dma_start(residual[:, 0, :], g[:, :]).then_inc(x_stored, 16)

            def h_lo_odd(t, count):
                pool.wait_ge(h_hi_done, count)
                pool.tensor_tensor(h_lo[:, tile(t)], htmp[:, S:2 * S], h_hi[:, tile(t)].bitcast(F32),
                                   ALU.subtract).then_inc(h_odd, 1)

            root(0)
            for t in range(1, KT, 2):
                h_lo_odd(t, t + 1)
            root(1, MB)

            pool.wait_ge(v_in, 1)
            pool.memset(kcur[:, 0:P], 0.0).then_inc(kcur_pad, 1)
            pool.wait_ge(kcur_pad, 1)
            with pool.Fori(0, KVH) as n:
                with pool.Fori(0, PAIRS // KVH) as m:
                    i = n * (PAIRS // KVH) + m
                    pool.wait_ge(scores1, i + 1)
                    settle()
                    pool.tensor_copy(kcur[:, P:P + S], kdup[:, tile(n)]).then_inc(kcur_done, 1)
                    pool.wait_ge(values1, i + 1)
                    settle()
                    for dup in range(2):
                        pool.tensor_copy(vcur[:, :].rearrange("p (b d) -> p b d", b=TB)[:, :, dup * HD:(dup + 1) * HD],
                                         vall[:, :].rearrange("p (b d) -> p b d", b=TB)[:, :, tile(n, HD)])\
                            .then_inc(vcur_done, 1)

            def add_residual(l, w):
                t = 2 * w + 1
                pool.wait_ge(scaled, l * KT + (t + 1))
                if l is LAYERS:
                    pool.wait_ge(x_last_in[w // 2], 16)
                    x = x_last[:, tile(t)]
                else:
                    slot, loads = loads_of(l, w)
                    pool.wait_ge(residual_in[slot], loads * 16)
                    x = xr[:, tile(2 * slot + 1)]
                pool.tensor_tensor(g[:, tile(t)], g[:, tile(t)], x, ALU.add).then_inc(x_odd, 1)

            with pool.Fori(0, LAYERS) as l:
                pool.wait_ge(y_hi_done, l * KT + KT)
                settle()
                pool.dma_start(area[:, :], memT).then_inc(memory_in, 16)
                add_squares(sq_no(l, POSTN), KT)
                root(norm_no(l, POSTN))
                for w in range(ODD + 1):
                    if w < ODD:
                        add_residual(l, w)
                    if w == 1:
                        add_first_squares(sq_no(l, PREN))
                    elif w > 1:
                        add_square(sq_no(l, PREN) + (2 * w - 2), 0)
                        add_square(sq_no(l, PREN) + (2 * w - 1), 1)
                root(norm_no(l, PREN))
                for t in range(1, KT, 2):
                    h_lo_odd(t, l * KT + (KT + t + 1))
                add_squares(sq_no(l, QN), QRT)
                root(norm_no(l, QN))
                add_first_squares(sq_no(l, KVN))
                root(norm_no(l, KVN))
            add_squares(sq_no(LAYERS, POSTN), KT)
            root(norm_no(LAYERS, POSTN))
            for w in range(ODD):
                add_residual(LAYERS, w)

        @block.tensor
        def _(pe):
            def begin(c):
                pe.wait_ge(lo_done, c.n + 1)
                if c.back is not None:
                    pe.wait_ge(evacuated[c.slot], c.uses)

            def passes(to, w_hi, w_lo, x_hi, x_lo, first, last, w_moves=False):
                for n, (a, b) in enumerate(((w_hi, x_hi), (w_hi, x_lo), (w_lo, x_hi))):
                    a, b = (b, a) if w_moves else (a, b)
                    ins = pe.matmul(to, a, b, start=first and n == 0, stop=last and n == 2)
                return ins

            def k_tile(c, k, x_hi, x_lo, n, first, last):
                w, x = tile(k, P), tile(k, n)
                return passes(acc[c.slot][:, 0:n], hi[c.slot][:, w], lo[c.slot][:, w], x_hi[:, x], x_lo[:, x], first, last)

            def features(c, x_hi, x_lo, n=S, order=range(KT), ready=None, pause=0, meanwhile=None):
                begin(c)
                for j, k in enumerate(order):
                    if meanwhile is not None and j == pause:
                        meanwhile()
                    if ready is not None:
                        ready(j)
                    ins = k_tile(c, k, x_hi, x_lo, n, j == 0, j == KT - 1)
                ins.then_inc(chunk_done, 1)

            def features_behind_h(c, d, before):
                lag = KT // 2
                begin(c)
                for k in range(KT + lag):
                    if k < KT:
                        pe.wait_ge((h_even, h_odd)[k % 2], before + (k // 2 + 1))
                        ins = k_tile(c, k, h_hi, h_lo, S, k == 0, k == KT - 1)
                        if k == KT - 1:
                            ins.then_inc(chunk_done, 1)
                    if k == lag:
                        begin(d)
                    if k >= lag:
                        ins = k_tile(d, k - lag, h_hi, h_lo, S, k == lag, k == KT + lag - 1)
                ins.then_inc(chunk_done, 1)

            def rows(c, at, tiles, to, x_hi, x_lo, n):
                pe.wait_ge(lo_done, c.n + 1)
                cols = CW // tiles
                for b in range(n // P):
                    for j in range(tiles):
                        w, x = tile(j, cols), slice((at + j) * n + b * P, (at + j) * n + (b + 1) * P)
                        ins = passes(to(b), hi[c.slot][:, w], lo[c.slot][:, w], x_hi[:, x], x_lo[:, x],
                                     at + j == 0, at + j == KT - 1, True)
                ins.then_inc(chunk_done, 1)

            def sums(count_on, squares):
                pe.wait_ge(count_on, squares)
                for b in range(TB):
                    ins = pe.matmul(ov[0][:, b:b + 1], sqacc[:, tile(b, P)], ones[:, 0:1], start=True, stop=True)
                ins.then_inc(sums_done, 1)

            def spread(no, to, n=S):
                pe.wait_ge(diag_done, no + 1)
                pe.matmul(to, ones, dg[:, 0:n], start=True, stop=True).then_inc(r_done, 1)

            for s in pe_from_one:
                pe.sem_inc(s, 1)
            pe.wait_ge(consts_in, 16)
            sums(x_added, ODD + 1)
            spread(0, bank(0))

            features_behind_h(chunk1(0), chunk1(1), 0)
            spread(1, ov[1][:, 0:MEM], MEM)
            for c in range(2):
                rows(chunk1(2 + c), c * KT // 2, KT // 2, lambda b: bank(b, 256), h_hi, h_lo, S)

            def scores_first(i):
                c = chunk1(PAIR1, i)
                pe.wait_ge(evacuated[c.slot], c.uses + 1)
                pe.wait_ge(kcur_done, i + 1)
                for b in range(TB):
                    for par in range(2):
                        rows_ = slice(HD * par, HD * par + HD)
                        ins = pe.matmul(bank(2 * par + b // 2, 256, b % 2 * 256), q1[rows_, tile(b, P)], kcur[rows_, b * P:b * P + 256],
                                        start=True, stop=True)
                ins.then_inc(scores1, 1)

            def turn_first(i):
                pe.wait_ge(probs1, i + 1)
                for kb in range(TB):
                    for par in range(2):
                        for nxt in range(2):
                            b = kb + nxt
                            if b < TB:
                                src = par * 1024 + b * 256 + (1 - nxt) * P
                                ins = pe.transpose(bank(kb, P, par * 256 + nxt * P), prob1[:, src:src + P], ident)
                ins.then_inc(turned1, 1)

            def values_first(i):
                pe.wait_ge(pt1_act, i * 2 + 2)
                pe.wait_ge(pt1_dve, i * 2 + 2)
                pe.wait_ge(vcur_done, i * 2 + 2)
                pe.wait_ge(y1, i + 1)
                for par in range(2):
                    for kb in range(TB):
                        n = 256 if kb < TB - 1 else P
                        src = kb * 512 + par * 256
                        ins = pe.matmul(ov[par][:, kb * P:kb * P + n], vcur[:, tile(kb, P)], pt1[:, src:src + n],
                                        start=kb == 0, stop=kb == TB - 1, skip_group_check=True)
                ins.then_inc(values1, 1)

            def pair(i, first):
                features(chunk1(PAIR1, i), h_hi, h_lo, pause=6, meanwhile=None if first else lambda: turn_first(i - 1))
                if not first:
                    values_first(i - 1)
                scores_first(i)
                features(chunk1(PAIR1 + 1, i), h_hi, h_lo)

            pair(0, True)
            with pe.Fori(1, PAIRS) as i:
                pair(i, False)
            turn_first(PAIRS - 1)
            values_first(PAIRS - 1)

            def out_product(l):
                features(chunk2(l, WO), h_hi, h_lo, ready=lambda j: pe.wait_ge(y_done, l * KT + (j + 1)))
                features(chunk2(l, WO + 1), h_hi, h_lo)
                with pe.Fori(1, KT // 2) as i:
                    for p in range(2):
                        features(chunk2(l, WO + p, i, 2), h_hi, h_lo)

            with pe.Fori(0, LAYERS) as l:
                out_product(l)
                pe.wait_ge(m_done, l * KT + KT)
                features(chunk2(l, MK), m_hi, m_lo, MEM, pause=KT // 2, meanwhile=lambda: sums(added, sq_no(l, PREN) + 2))
                spread(norm_no(l, POSTN), bank(0))
                for c in range(1, MH):
                    features(chunk2(l, MK + c), m_hi, m_lo, MEM)
                for c in range(MH):
                    rows(chunk2(l, MV + c), c * KT // MH, KT // MH, lambda b: bank(2 + b), m_hi, m_lo, MEM)
                    if c == 1:
                        sums(added, sq_no(l, QN) + 2)
                    if c == 2:
                        spread(norm_no(l, PREN), bank(1))
                features_behind_h(chunk2(l, QL), chunk2(l, QL + 1), l * ODD + ODD)
                for j in range(2, QRT):
                    features(chunk2(l, QL + j), h_hi, h_lo)
                features(chunk2(l, KVL), h_hi, h_lo)
                sums(added, sq_no(l, KVN) + 2)
                features(chunk2(l, KVL + 1), h_hi, h_lo)
                spread(norm_no(l, QN), bank(0))
                features(chunk2(l, KPE), h_hi, h_lo)
                sums(added, sq_no(l, KVN) + (KVRT + 2))
                with pe.Fori(0, CT // 2) as i:
                    for j in range(6):
                        features(chunk2(l, CONV + j, i, 6), h_hi, h_lo)
                spread(norm_no(l, KVN), bank(1))

                def scores_mem(c):
                    ch = chunk2(l, QM + c)
                    pe.wait_ge(evacuated[ch.slot], ch.uses + 1)
                    for b in range(TB):
                        ins = pe.matmul(bank(b, MEM), qm[:, (c % 2) * S + b * P:(c % 2) * S + (b + 1) * P], mk[:, tile(c, MEM)],
                                        start=True, stop=True)
                    ins.then_inc(scores_m, 1)

                def turn_mem(c):
                    pe.wait_ge(probs_m, l * MH + (c + 1))
                    for b in range(TB):
                        for k in range(MB):
                            ins = pe.transpose(bank(b, P, k * P), prob_a[:, b * MEM + k * P:b * MEM + (k + 1) * P], ident)
                    ins.then_inc(turned_m, 1)

                def values_mem(c):
                    pe.wait_ge(ptm_done, l * MH + (c + 1))
                    pe.wait_ge(om_done, l * MH + (c + 1))
                    for k in range(MB):
                        ins = pe.matmul(ov[0][:, :], mv[:, k * 512 + c * P:k * 512 + (c + 1) * P], ptm[:, tile(k)],
                                        start=k == 0, stop=k == MB - 1)
                    ins.then_inc(values_m, 1)

                for c in range(MH):
                    if c == 0:
                        features(chunk2(l, QM), h_hi, h_lo)
                        pe.wait_ge(lat_done, l * 6 + 6)
                    else:
                        features(chunk2(l, QM + c), h_hi, h_lo, pause=6, meanwhile=lambda: turn_mem(c - 1))
                        values_mem(c - 1)
                    scores_mem(c)

                def project(c, j, free_banks):
                    begin(c)
                    w_hi, w_lo = hi[c.slot], lo[c.slot]

                    def product(to, at, x, first, last, w_moves=False):
                        w = slice(at, at + (2 * P if w_moves else P))
                        return passes(to, w_hi[:, w], w_lo[:, w], m_hi[:, x], m_lo[:, x], first, last, w_moves)

                    for k in range(QRT):
                        product(acc[c.slot][:, :], k * 256, tile(KVRT + k), k == 0, k == QRT - 1)
                    for k in range(KVRT):
                        product(ov[1][:, :], UK + k * P, tile(k), k == 0, k == KVRT - 1)
                    free_banks()
                    for k in range(QRT):
                        ins = product(bank(0), k * 256 + P, tile(KVRT + k), k == 0, k == QRT - 1)
                    for b in range(TB if j == 0 else 0):
                        for k in range(KVRT):
                            ins = product(bank(1 + b // 2, 2 * P, b % 2 * 2 * P), UV + k * 2 * P,
                                          slice(k * S + b * P, k * S + (b + 1) * P), k == 0, k == KVRT - 1, True)
                    ins.then_inc(chunk_done, 1)

                def scores_head(no):
                    pe.wait_ge(qkv_done, no * 2)
                    pe.wait_ge(qr_done, no * 3)
                    for b in range(TB):
                        pe.matmul(bank(b), qn[:, tile(b, P)], kn[:, :], start=True, stop=False)
                        ins = pe.matmul(bank(b), qr[0:64, tile(b, P)], kr[0:64, :], start=False, stop=True)
                    ins.then_inc(scores2, 1)

                def turn_head(no):
                    pe.wait_ge(probs2, no)
                    for b in range(TB):
                        for k in range(TB):
                            src = (b % 2) * S + k * P
                            ins = pe.transpose(bank(b, P, k * P), (prob_a, prob_b)[b // 2][:, src:src + P], ident)
                    ins.then_inc(turned2, 1)

                def turned_read(no):
                    pe.wait_ge(pt2_act, no * 2)
                    pe.wait_ge(pt2_dve, no * 2)

                def values_head(no, j):
                    turned_read(no)
                    pe.wait_ge(y_a, no)
                    for k in range(TB):
                        ins = pe.matmul(ov[0][:, :], v[:, (2 * k + j) * P:(2 * k + j + 1) * P], pt[:, tile(k)], start=k == 0, stop=k == TB - 1)
                    ins.then_inc(values2, 1)

                def end_of_memory():
                    turn_mem(MH - 1)
                    pe.wait_ge(ptm_done, l * MH + MH)

                def head(i, j, first=False):
                    no = l * MLA + (i * 2 + (j + 1))
                    project(chunk2(l, HEAD + 3 * j, i, 6), j, end_of_memory if first else lambda: turned_read(no - 1))
                    if first:
                        values_mem(MH - 1)
                    else:
                        values_head(no - 1, 1 - j)
                    features(chunk2(l, HEAD + 3 * j + 1, i, 6), h_hi, h_lo)
                    scores_head(no)
                    features(chunk2(l, HEAD + 3 * j + 2, i, 6), h_hi, h_lo)
                    turn_head(no)

                head(0, 0, True)
                pe.wait_ge(om_done, l * MH + (MH + 1))
                head(0, 1)
                with pe.Fori(1, MLA // 2) as i:
                    head(i, 0)
                    head(i, 1)
                values_head(l * MLA + MLA, 1)
            out_product(LAYERS)
            sums(added, sq_no(LAYERS, PREN) + 2)
            spread(norm_no(LAYERS, POSTN), bank(0))

        @block.scalar
        def _(act):
            def split(c):
                act.wait_ge(loaded[c.slot], (c.uses + 1) * 16)
                if c.back is not None:
                    act.wait_ge(chunk_done, c.n + (1 - c.back))
                act.activation(hi[c.slot][:, :], raw[c.slot][:, :], ACT.Copy).then_inc(hi_done, 1)

            def multiplied(c):
                act.wait_ge(chunk_done, c.n + 1)

            def square(src, no, slot):
                act.wait_ge(added, no + 1)
                act.activation(sq[:, tile(slot)], src, ACT.Square).then_inc(squared, 1)

            def h_hi_tile(t, slot, count):
                act.wait_ge(normed_done, count)
                act.activation(h_hi[:, tile(t)], htmp[:, tile(slot)], ACT.Copy).then_inc(h_hi_done, 1)

            def y_hi_tile(t):
                act.activation(h_hi[:, tile(t)], g[:, tile(t)], ACT.Copy).then_inc(y_hi_done, 1)

            for w in range(ODD):
                if w % 2 == 0:
                    act.wait_ge(x_in[w // 2], 16)
                if w >= 2:
                    act.wait_ge(x_added, w - 1)
                act.activation(sqx[:, tile(w % 2, 2 * S)], g[:, tile(w, 2 * S)], ACT.Square).then_inc(x_squared, 1)
            split(chunk1(0))
            split(chunk1(1))
            for t in range(KT):
                h_hi_tile(t, t % 2, t + 1)
            act.wait_ge(memrows_in, 32)
            for b, rows_ in enumerate((memrow0, memrow1)):
                ins = act.activation(rows_[:, :], rows_[:, :], ACT.Square, accum_out=ss[:, b:b + 1])
            ins.then_inc(mem_ss, 1)

            for c in range(2):
                ch = chunk1(c)
                split(chunk1(2 + c))
                if c == 0:
                    act.wait_ge(mem_ss, 1)
                multiplied(ch)
                for j in range(2):
                    for half_ in range(2):
                        ins = act.activation(kdup[HD * half_:HD * (half_ + 1), tile(2 * c + j)],
                                             acc[ch.slot][HD * j:HD * (j + 1), :], ACT.Copy)
                ins.then_inc(evacuated[ch.slot], 2)
            act.wait_ge(r_done, 2)
            act.activation(r_mem[:, :], ov[1][:, 0:MEM], ACT.Copy).then_inc(r_mem_done, 1)
            act.wait_ge(angle_done, 1)
            act.activation(angle[:, 0:S], angle[:, 0:S], ACT.Sin).then_inc(sin_done, 1)
            split(chunk1(PAIR1))
            multiplied(chunk1(3))
            act.activation(vall[:, :].rearrange("p (b n) -> p b n", b=TB),
                           sc[:, :].rearrange("p (b n) -> p b n", b=TB)[:, :, 0:256], ACT.Copy).then_inc(v_in, 1)

            def turned_first(i, values_count):
                act.wait_ge(turned1, i + 1)
                act.wait_ge(values1, values_count)
                for b in range(2):
                    act.activation(pt1[:, tile(b)], bank(b), ACT.Copy).then_inc(pt1_act, 1)

            def pair(i, first):
                qc, zc = chunk1(PAIR1, i), chunk1(PAIR1 + 1, i)
                split(zc)
                if not first:
                    turned_first(i - 1, i)
                multiplied(qc)
                act.wait_ge(scores1, i + 1)
                act.activation(q1[:, :], acc[qc.slot][:, :], ACT.Copy, scale=HD ** -0.5).then_inc(evacuated[qc.slot], 1)
                split(chunk1(PAIR1 + 2, i))
                act.wait_ge(shift1, i + 1)
                for n in range(2 * TB):
                    act.activation(prob1[:, tile(n, 256)], prob1[:, tile(n, 256)], ACT.Exp,
                                   bias=nm[:, n:n + 1], accum_out=ls[:, n:n + 1])
                act.activation(es, es, ACT.Exp).then_inc(exp1, 1)
                multiplied(zc)
                act.wait_ge(evacuated[zc.slot], zc.uses)
                act.activation(tz, acc[zc.slot][:, :], ACT.Tanh, scale=0.5).then_inc(tanh1, 1)

            pair(0, True)
            with act.Fori(1, PAIRS) as i:
                pair(i, False)
            turned_first(PAIRS - 1, PAIRS)

            def y_hi_tiles(nxt, last_ready):
                with act.Fori(0, KT // 2) as t:
                    y_hi_tile(t)
                split(nxt)
                with act.Fori(KT // 2, KT - 1) as t:
                    y_hi_tile(t)
                last_ready()
                y_hi_tile(KT - 1)

            act.wait_ge(y1, PAIRS)
            act.wait_ge(chunk_done, N1)
            act.wait_ge(x_stored, 16)
            y_hi_tiles(chunk2(0, WO + 1), lambda: act.wait_ge(y1, PAIRS + 1))

            def reload_residual(l, w):
                slot = w % XR
                act.dma_start(xr[:, tile(slot, 2 * S)], residual[:, col(l), tile(w, 2 * S)]).then_inc(residual_in[slot], 16)

            def output_tile(l, t, slot, c, nxt, memory):
                if nxt is not None:
                    split(nxt)
                if memory:
                    act.wait_ge(mt_done, l * KT + t + 1)
                    act.activation(m_hi[:, tile(t, MEM)], dg[:, tile(slot, MEM)], ACT.Copy).then_inc(mhi_done, 1)
                multiplied(c)
                square(acc[c.slot][:, :], t + sq_no(l, POSTN), slot)
                act.activation(g[:, tile(t)], acc[c.slot][:, :], ACT.Copy).then_inc(evacuated[c.slot], 1)

            def output(l, memory):
                output_tile(l, 0, 0, chunk2(l, WO), None, memory)
                output_tile(l, 1, 1, chunk2(l, WO + 1), chunk2(l, WO + 2), memory)
                with act.Fori(1, KT // 2 - (not memory)) as i:
                    for j in range(2):
                        output_tile(l, i * 2 + j, j, chunk2(l, WO + j, i, 2), chunk2(l, WO + j + 1, i, 2), memory)
                if not memory:
                    output_tile(l, KT - 2, 0, chunk2(l, WO + KT - 2), chunk2(l, WO + KT - 1), False)
                    output_tile(l, KT - 1, 1, chunk2(l, WO + KT - 1), None, False)

            with act.Fori(0, LAYERS) as l:
                output(l, True)
                act.wait_ge(m_done, l * KT + KT)
                for w in range(XR):
                    reload_residual(l, w)
                split(chunk2(l, MK + 1))
                for c in range(MH + 1):
                    split(chunk2(l, MK + c + 2))
                    for t in STEPS[c]:
                        act.wait_ge((x_even, x_odd)[t % 2], l * ODD + (t // 2 + 1))
                        square(g[:, tile(t)], sq_no(l, PREN) + t, t % 2)
                        if t % 2 == 1:
                            w = t // 2
                            act.dma_start(residual[:, col(l + 1), tile(w, 2 * S)], g[:, tile(w, 2 * S)]).then_inc(stored, 16)
                            if w + XR < ODD:
                                reload_residual(l, w + XR)
                    if c < MH:
                        ch = chunk2(l, MK + c)
                        multiplied(ch)
                        act.activation(mk[:, tile(c, MEM)], acc[ch.slot][:, 0:MEM], ACT.Copy)\
                            .then_inc(evacuated[ch.slot], 2)
                split(chunk2(l, MV + 3))
                for t in range(KT):
                    if t in H_SPLITS:
                        split(chunk2(l, QL + H_SPLITS.index(t)))
                    h_hi_tile(t, t % 2, l * KT + (KT + t + 1))
                multiplied(chunk2(l, MV + MH - 1))
                act.activation(mv[:, :], sc[:, 1024:2048], ACT.Copy)

                def latent(p, t, sq_at):
                    c = chunk2(l, p)
                    if p > QL:
                        split(chunk2(l, p + 1))
                    multiplied(c)
                    square(acc[c.slot][:, :], sq_at, t % 2)
                    act.activation(g[:, tile(t)], acc[c.slot][:, :], ACT.Copy).then_inc(evacuated[c.slot], 1)

                def latent_hi(t, slot, count):
                    act.wait_ge(lat_normed, count)
                    act.activation(m_hi[:, tile(t)], htmp[:, tile(slot)], ACT.Copy).then_inc(lat_hi_done, 1)

                act.wait_ge(stored, l * (8 * KT) + 8 * KT)
                for j in range(QRT):
                    latent(QL + j, MLA + KVRT + j, sq_no(l, QN) + j)
                for j in range(KVRT):
                    latent(KVL + j, MLA + j, sq_no(l, KVN) + j)
                split(chunk2(l, CONV))
                for j in range(QRT):
                    latent_hi(KVRT + j, j % 2, l * 6 + (j + 1))

                act.wait_ge(added, sq_no(l, KVN) + (KVRT + 2))
                with act.Fori(0, CT // 2) as i:
                    for j in range(2):
                        c = chunk2(l, CONV + 3 * j, i, 6)
                        split(chunk2(l, CONV + 3 * j + 1, i, 6))
                        multiplied(c)
                        before = chunk2(l, CONV + 3 * j - 2, i, 6)
                        act.wait_ge(evacuated[before.slot], before.uses + 1)
                        act.activation(cg, acc[c.slot][:, :], ACT.Copy).then_inc(evacuated[c.slot], 1)
                        split(chunk2(l, CONV + 3 * j + 2, i, 6))
                        split(chunk2(l, CONV + 3 * j + 3, i, 6))
                for j in range(KVRT):
                    latent_hi(j, j, l * 6 + (QRT + j + 1))

                act.wait_ge(lat_done, l * 6 + 6)
                def turned_mem(c):
                    act.wait_ge(turned_m, l * MH + (c + 1))
                    for b in range(TB):
                        ins = act.activation(ptm[:, :].rearrange("p (k q) -> p k q", k=MB)[:, :, tile(b, P)],
                                             bank(b, MEM).rearrange("p (k q) -> p k q", k=MB), ACT.Copy)
                    ins.then_inc(ptm_done, 1)

                for c in range(MH):
                    ch = chunk2(l, QM + c)
                    split(chunk2(l, QM + c + 1))
                    if c > 0:
                        turned_mem(c - 1)
                    multiplied(ch)
                    act.activation(qm[:, tile(c % 2)], acc[ch.slot][:, :], ACT.Copy).then_inc(evacuated[ch.slot], 1)
                    act.wait_ge(shift_m, l * MH + (c + 1))
                    for b in range(TB):
                        ins = act.activation(prob_a[:, tile(b, MEM)], bank(b, MEM), ACT.Exp, scale=MEM_SCALE,
                                             bias=nm[:, b:b + 1], accum_out=ls[:, b:b + 1])
                    ins.then_inc(exp_m, 1)

                def head(i, j, first=False, last=False):
                    no = l * MLA + (i * 2 + (j + 1))
                    hc, ga, gb = (chunk2(l, HEAD + 3 * j + n, i, 6) for n in range(3))
                    split(ga)
                    if first:
                        turned_mem(MH - 1)
                    multiplied(hc)
                    act.activation(qn[:, :], acc[hc.slot][:, :], ACT.Copy).then_inc(evacuated[hc.slot], 1)
                    act.activation(kn[:, :], ov[1][:, :], ACT.Copy).then_inc(qkv_done, 1 if j == 0 else 2)
                    if j == 0:
                        if first:
                            act.wait_ge(values_m, l * MH + MH)
                        act.wait_ge(values2, no)
                        act.activation(v[:, :], sc[:, 512:512 + TB * 256], ACT.Copy).then_inc(qkv_done, 1)
                    split(gb)
                    multiplied(ga)
                    before = chunk2(l, HEAD + 3 * j - 1, i, 6)
                    act.wait_ge(evacuated[before.slot], before.uses + 1)
                    act.activation(tz, acc[ga.slot][:, :], ACT.Tanh, scale=0.5).then_inc(tanh2, 1)
                    if not last:
                        split(chunk2(l, HEAD + 3 * j + 3, i, 6))
                    act.wait_ge(shift2, no)
                    for b in range(TB):
                        ins = act.activation((prob_a, prob_b)[b // 2][:, tile(b % 2)], bank(b), ACT.Exp, scale=MLA_SCALE,
                                             bias=nm[:, b:b + 1], accum_out=ls[:, b:b + 1])
                    ins.then_inc(exp2, 1)
                    multiplied(gb)
                    act.wait_ge(evacuated[ga.slot], ga.uses + 1)
                    act.activation(tz, acc[gb.slot][:, :], ACT.Tanh, scale=0.5).then_inc(tanh2, 1)
                    act.wait_ge(turned2, no)
                    act.wait_ge(values2, no)
                    for b in range(2):
                        act.activation(pt[:, :].rearrange("p (k q) -> p k q", k=TB)[:, :, tile(b, P)],
                                       bank(b).rearrange("p (k q) -> p k q", k=TB), ACT.Copy).then_inc(pt2_act, 1)

                head(0, 0, first=True)
                head(0, 1)
                with act.Fori(1, MLA // 2 - 1) as i:
                    head(i, 0)
                    head(i, 1)
                head(MLA // 2 - 1, 0)
                head(MLA // 2 - 1, 1, last=True)

                split(chunk2(l, N2 + WO))
                act.wait_ge(y_b, l * MLA + MLA)
                act.wait_ge(y_a, l * MLA + MLA)
                act.sem_inc(waited, 1)
                y_hi_tiles(chunk2(l, N2 + WO + 1), lambda: act.wait_ge(y_a, l * MLA + (MLA + 1)))

            for c in range(4):
                act.dma_start(x_last[:, tile(c, 4 * S)], residual[:, LAYERS, tile(c, 4 * S)]).then_inc(x_last_in[c], 16)
            output(LAYERS, False)
            for w in range(ODD):
                act.wait_ge(x_even, LAYERS * ODD + w + 1)
                act.wait_ge(x_odd, LAYERS * ODD + w + 1)
                act.dma_start(out[:, tile(w, 2 * S)], g[:, tile(w, 2 * S)]).then_inc(out_stored, 16)
            act.wait_ge(out_stored, 16 * ODD)
            act.wait_ge(stored, LAYERS * 16 * ODD)

        @block.vector
        def _(dve):
            def split(c):
                dve.wait_ge(hi_done, c.n + 1)
                dve.tensor_tensor(lo[c.slot][:, :], raw[c.slot][:, :], hi[c.slot][:, :].bitcast(F32),
                                  ALU.subtract).then_inc(lo_done, 1)

            class Links:

                def __init__(self, sem_, start):
                    self.sem, self.start, self.n = sem_, start, 0

                def then(self, ins):
                    self.n += 1
                    ins.then_inc(self.sem, 1)
                    dve.wait_ge(self.sem, self.start + self.n)

            def norm(no, features_, sums_, n=TB):
                link = Links(norm_link, no * 4)
                dve.tensor_scalar(ms[:, 0:n], sums_, 1.0 / features_, EPS, ALU.mult, ALU.add).then_inc(ms_done, 1)
                dve.wait_ge(rs_done, no + 1)
                link.then(dve.tensor_tensor(nt[:, 0:n], r[:, 0:n], r[:, 0:n], ALU.mult))
                link.then(dve.tensor_tensor(nt[:, 0:n], nt[:, 0:n], ms[:, 0:n], ALU.mult))
                link.then(dve.tensor_scalar(nt[:, 0:n], nt[:, 0:n], -0.5, 1.5, ALU.mult, ALU.add))
                link.then(dve.tensor_tensor(r[:, 0:n], r[:, 0:n], nt[:, 0:n], ALU.mult))
                for b in range(n):
                    ins = dve.tensor_scalar(dg[:, tile(b, P)], ident, r[:, b:b + 1], None, ALU.mult)
                ins.then_inc(diag_done, 1)

            def token_norm(no, count, features_):
                dve.wait_ge(sums_done, count)
                norm(no, features_, ov[0][:, 0:TB])

            def normed(to, src, gain, r_b):
                return dve.scalar_tensor_tensor(to, src, gain, r_b, ALU.mult, ALU.mult)

            for m in dve_from_one:
                dve.sem_inc(m, 1)
            dve.wait_ge(consts_in, 16)
            for w in range(1, ODD):
                dve.wait_ge(x_squared, w + 1)
                if w > 1:
                    dve.wait_ge(x_added, w)
                a = sqx[:, 0:2 * S] if w == 1 else sq[:, :]
                dve.tensor_tensor(sq[:, :], a, sqx[:, tile(w % 2, 2 * S)], ALU.add).then_inc(x_added, 2 if w == 1 else 1)
            dve.wait_ge(x_added, ODD)
            dve.tensor_tensor(sqacc[:, :], sq[:, 0:S], sq[:, S:2 * S], ALU.add).then_inc(x_added, 1)
            token_norm(0, 1, D)
            split(chunk1(0))

            def h_tiles(gain, r_b, before, half_before, splits):
                for t in range(KT + 1):
                    if t in splits:
                        split(splits[t])
                    if t < KT:
                        if t >= 2 or not isinstance(before, int):
                            dve.wait_ge((h_even, h_odd)[t % 2], half_before + t // 2)
                        normed(htmp[:, tile(t % 2)], g[:, tile(t)], gn[:, col(gain + t)], r_b).then_inc(normed_done, 1)
                    if t % 2 == 1:
                        dve.wait_ge(h_hi_done, before + t)
                        x = tile(t - 1)
                        dve.tensor_tensor(h_lo[:, x], htmp[:, 0:S], h_hi[:, x].bitcast(F32), ALU.subtract).then_inc(h_even, 1)

            dve.wait_ge(gains_in, 16)
            dve.wait_ge(r_done, 1)
            h_tiles(PRE1, bank(0), 0, 0, {4: chunk1(1)})
            dve.wait_ge(mem_ss, 1)
            norm(1, D, ss, MB)
            split(chunk1(2))

            ang, kf, tmp = (angle[:, tile(n)] for n in range(3))
            rope = Links(rope_link, 0)
            dve.wait_ge(pos_in, 16)
            rope.then(dve.tensor_copy(ang, posi[:, :]))
            rope.then(dve.tensor_scalar(ang, ang, cst[:, FREQ:FREQ + 1], None, ALU.mult))
            rope.then(dve.tensor_scalar(turns[:, :], ang, 1 / TWO_PI, None, ALU.mult))
            rope.then(dve.tensor_copy(kf, turns[:, :]))
            for part in (TURN_A, TURN_B, TURN_C):
                rope.then(dve.scalar_tensor_tensor(ang, kf, -part, ang, ALU.mult, ALU.add))
            rope.then(dve.tensor_scalar(ang, ang, cst[:, PHASE:PHASE + 1], None, ALU.add))
            for op, past, turn in ((ALU.is_gt, PI, -TWO_PI), (ALU.is_lt, -PI, TWO_PI)):
                rope.then(dve.tensor_scalar(tmp, ang, past, turn, op, ALU.mult))
                rope.then(dve.tensor_tensor(ang, ang, tmp, ALU.add))
            below_pi = float(np.nextafter(np.float32(np.pi), np.float32(0)))
            dve.tensor_scalar(ang, ang, below_pi, -below_pi, ALU.min, ALU.max).then_inc(angle_done, 1)
            split(chunk1(3))
            dve.wait_ge(sin_done, 1)
            rope.then(dve.tensor_scalar(cs[:, :], ang, cst[:, SIGN:SIGN + 1], None, ALU.mult))
            split(chunk1(PAIR1))

            def softmax_first(i):
                link = Links(soft1_link, i * 5)
                dve.wait_ge(scores1, i + 2)
                for par in range(2):
                    half_ = tile(par, 1024)
                    ins = dve.scalar_tensor_tensor(prob1[:, half_], win[:, :], cst[:, col(i * 2 + (SLOPE + par))], sc[:, half_],
                                                   ALU.mult, ALU.add)
                link.then(ins)
                link.then(dve.tensor_reduce(mx, prob1[:, :].rearrange("p (n k) -> p n k", n=2 * TB), AX.X, ALU.max))
                sinks_ = [snk[:, col(i * 2 + par)] for par in range(2)]
                for par in range(2):
                    ins = dve.tensor_scalar(mx[:, tile(par, TB)], mx[:, tile(par, TB)], sinks_[par], None, ALU.max)
                link.then(ins)
                for par in range(2):
                    dve.tensor_scalar(es[:, tile(par, TB)], mx[:, tile(par, TB)], -1.0, sinks_[par], ALU.mult, ALU.add)
                dve.tensor_scalar(nm, mx, -1.0, None, ALU.mult).then_inc(shift1, 1)
                dve.wait_ge(exp1, i + 1)
                link.then(dve.tensor_tensor(ls, ls, es, ALU.add))
                link.then(dve.reciprocal(rl, ls))
                for n in range(2 * TB):
                    ins = dve.tensor_scalar(prob1[:, tile(n, 256)], prob1[:, tile(n, 256)], rl[:, n:n + 1], None, ALU.mult)
                ins.then_inc(probs1, 1)
                assert link.n == 5

            def y_first(i):
                zc = chunk1(PAIR1 + 1, i)
                dve.wait_ge(values1, i + 2)
                dve.wait_ge(evacuated[zc.slot], zc.uses + 1)
                for par in range(2):
                    rows_ = slice(HD * par, HD * par + HD)
                    ins = dve.scalar_tensor_tensor(g[rows_, tile(i)], ov[par][rows_, :], 0.5, sg[rows_, :], ALU.mult, ALU.mult)
                ins.then_inc(y1, 1)

            def turned_first(i):
                dve.wait_ge(turned1, i + 1)
                for b in range(2, TB):
                    dve.tensor_copy(pt1[:, tile(b)], bank(b)).then_inc(pt1_dve, 1)

            def pair(i, first):
                zc = chunk1(PAIR1 + 1, i)
                split(zc)
                if not first:
                    turned_first(i - 1)
                    y_first(i - 1)
                split(chunk1(PAIR1 + 2, i))
                softmax_first(i)
                dve.wait_ge(tanh1, i + 1)
                dve.scalar_tensor_tensor(sg, tz, 1.0, acc[zc.slot][:, :], ALU.add, ALU.mult).then_inc(evacuated[zc.slot], 1)

            def y_lo_tile(t, count):
                dve.wait_ge(y_hi_done, count)
                dve.tensor_tensor(h_lo[:, tile(t)], g[:, tile(t)], h_hi[:, tile(t)].bitcast(F32),
                                  ALU.subtract).then_inc(y_done, 1)

            dve.wait_ge(window_in, 32)
            dve.wait_ge(x_stored, 16)
            pair(0, True)
            with dve.Fori(1, PAIRS) as i:
                pair(i, False)
            turned_first(PAIRS - 1)

            def y_lo_tiles(before, nxt, last):
                with dve.Fori(0, KT // 2) as t:
                    y_lo_tile(t, before + t + 1)
                split(nxt)
                with dve.Fori(KT // 2, KT - 1) as t:
                    y_lo_tile(t, before + t + 1)
                last()
                y_lo_tile(KT - 1, before + KT)

            y_lo_tiles(0, chunk2(0, WO + 1), lambda: y_first(PAIRS - 1))

            def output_tile(l, t, slot, nxt, memory):
                if nxt is not None:
                    split(nxt)
                if memory:
                    normed(dg[:, tile(slot, MEM)], area[:, tile(t, MEM)], gn[:, col(l * KT + t + MEMG)], r_mem[:, :])\
                        .then_inc(mt_done, 1)
                    dve.wait_ge(mhi_done, l * KT + t + 1)
                    dve.tensor_tensor(m_lo[:, tile(t, MEM)], dg[:, tile(slot, MEM)], m_hi[:, tile(t, MEM)].bitcast(F32),
                                      ALU.subtract).then_inc(m_done, 1)

            def output(l, memory):
                output_tile(l, 0, 0, None, memory)
                output_tile(l, 1, 1, chunk2(l, WO + 2), memory)
                with dve.Fori(1, KT // 2 - (not memory)) as i:
                    for j in range(2):
                        output_tile(l, i * 2 + j, j, chunk2(l, WO + j + 1, i, 2), memory)
                if not memory:
                    output_tile(l, KT - 2, 0, chunk2(l, WO + KT - 1), False)

            dve.wait_ge(r_mem_done, 1)

            def new_x(t, l):
                normed(g[:, tile(t)], g[:, tile(t)], gn[:, col(l * KT + (t + POST))], bank(0)).then_inc(scaled, 1)
                if t % 2 == 0:
                    dve.wait_ge(scaled, l * KT + (t + 1))
                    if l is LAYERS:
                        dve.wait_ge(x_last_in[t // 4], 16)
                        x = x_last[:, tile(t)]
                    else:
                        slot, loads = loads_of(l, t // 2)
                        dve.wait_ge(residual_in[slot], loads * 16)
                        x = xr[:, tile(2 * slot)]
                    dve.tensor_tensor(g[:, tile(t)], g[:, tile(t)], x, ALU.add).then_inc(x_even, 1)

            with dve.Fori(0, LAYERS) as l:
                dve.wait_ge(memory_in, l * 16 + 16)
                output(l, True)
                for c in (chunk2(l, MK), chunk2(l, MK + 1)):
                    dve.wait_ge(evacuated[c.slot], c.uses)
                token_norm(norm_no(l, POSTN), l * 4 + 2, D)
                split(chunk2(l, MK + 1))
                dve.wait_ge(r_done, norm_no(l, POSTN) + 1)
                for c in range(MH + 1):
                    if c > 0:
                        split(chunk2(l, MK + c + 1))
                    for t in STEPS[c]:
                        new_x(t, l)
                split(chunk2(l, MV + 2))
                token_norm(norm_no(l, PREN), l * 4 + 3, D)
                split(chunk2(l, MV + 3))
                dve.wait_ge(r_done, norm_no(l, PREN) + 1)
                h_tiles(l * GN + (GL + PRE), bank(1), l * KT + KT, l * ODD + ODD,
                        {t: chunk2(l, QL + n) for n, t in enumerate(H_SPLITS)})
                for j in range(1, QRT + 1):
                    split(chunk2(l, QL + j + 1))

                def latents(first, tiles, gain, r_b, before):
                    for n in range(tiles):
                        if before + n < 2:
                            dve.wait_ge((h_even, h_odd)[n], l * ODD + 2 * ODD)
                        else:
                            dve.wait_ge(lat_done, l * 6 + (before + n - 1))
                        normed(htmp[:, tile(n % 2)], g[:, tile(MLA + first + n)], gn[:, col(l * GN + (GL + gain + n))], r_b)\
                            .then_inc(lat_normed, 1)
                        dve.wait_ge(lat_hi_done, l * 6 + (before + n + 1))
                        x = tile(first + n)
                        dve.tensor_tensor(m_lo[:, x], htmp[:, tile(n % 2)], m_hi[:, x].bitcast(F32),
                                          ALU.subtract).then_inc(lat_done, 1)

                token_norm(norm_no(l, QN), l * 4 + 4, QRT * P)
                split(chunk2(l, KPE))
                split(chunk2(l, CONV))
                dve.wait_ge(r_done, norm_no(l, QN) + 1)
                for j in range(QRT):
                    c = chunk2(l, QL + j)
                    dve.wait_ge(evacuated[c.slot], c.uses + 1)
                latents(KVRT, QRT, QG, bank(0), 0)

                def rotate(to, src, sem_, start):
                    link = Links(sem_, start)
                    dve.tensor_tensor(to[0:64, :], src[0:64, :], cs[0:64, :], ALU.mult).then_inc(sem_, 1)
                    link.n = 1
                    link.then(dve.tensor_tensor(dg[0:64, :], src[64:128, :], cs[64:128, :], ALU.mult))
                    return link

                kc = chunk2(l, KPE)
                dve.wait_ge(chunk_done, kc.n + 1)
                rotate(kr, acc[kc.slot], kr_link, l * 2)
                dve.tensor_tensor(kr[0:64, :], kr[0:64, :], dg[0:64, :], ALU.add).then_inc(evacuated[kc.slot], 1)
                token_norm(norm_no(l, KVN), l * 4 + 5, KVRT * P)
                dve.memset(u[:, 0:1], 0.0)
                dve.memset(u[:, S + 1:S + 2], 0.0).then_inc(u_pad, 1)
                dve.wait_ge(u_pad, l + 1)
                dve.sem_inc(waited, 1)

                with dve.Fori(0, CT // 2) as i:
                    for j in range(2):
                        gc, xi, gb = (chunk2(l, CONV + 3 * j + n, i, 6) for n in range(3))
                        link = Links(conv_link, l * (3 * CT) + (i * 6 + 3 * j))
                        taps = [gn[:, col(l * GN + (i * 6 + (GL + TAP + 3 * j + n)))] for n in range(3)]
                        split(xi)
                        split(gb)
                        dve.wait_ge(chunk_done, xi.n + 1)
                        dve.wait_ge(evacuated[gc.slot], gc.uses + 1)
                        dve.tensor_tensor(u[:, 1:S + 1], acc[xi.slot][:, :], cg, ALU.mult).then_inc(evacuated[xi.slot], 1)
                        dve.wait_ge(evacuated[xi.slot], xi.uses + 1)
                        link.then(dve.tensor_scalar(cv, u[:, 0:S], taps[0], None, ALU.mult))
                        for n in (1, 2):
                            link.then(dve.scalar_tensor_tensor(cv, u[:, n:n + S], taps[n], cv, ALU.mult, ALU.add))
                        split(chunk2(l, CONV + 3 * j + 3, i, 6))
                        dve.wait_ge(chunk_done, gb.n + 1)
                        dve.tensor_tensor(g[:, tile(i * 2 + j)], acc[gb.slot][:, :], cv, ALU.mult)\
                            .then_inc(evacuated[gb.slot], 1)
                dve.wait_ge(r_done, norm_no(l, KVN) + 1)
                for j in range(KVRT):
                    c = chunk2(l, KVL + j)
                    dve.wait_ge(evacuated[c.slot], c.uses + 1)
                latents(0, KVRT, KVG, bank(1), QRT)

                banks = sc[:, :].rearrange("p (b n) -> p b n", b=TB)
                for c in range(MH):
                    no = l * MH + (c + 1)
                    link = Links(soft_m_link, l * (2 * MH) + 2 * c)

                    def mem_out(c):
                        dve.wait_ge(values_m, l * MH + (c + 1))
                        dve.tensor_copy(g[:, tile(CT + c)], ov[0][:, :]).then_inc(om_done, 1)

                    split(chunk2(l, QM + c + 1))
                    if c > 0:
                        mem_out(c - 1)
                    dve.wait_ge(scores_m, no)
                    link.then(dve.tensor_reduce(mx[:, 0:TB], banks[:, :, 0:MEM], AX.X, ALU.max))
                    dve.tensor_scalar(nm[:, 0:TB], mx[:, 0:TB], -MEM_SCALE, None, ALU.mult).then_inc(shift_m, 1)
                    dve.wait_ge(exp_m, no)
                    link.then(dve.reciprocal(rl[:, 0:TB], ls[:, 0:TB]))
                    for b in range(TB):
                        ins = dve.tensor_scalar(prob_a[:, tile(b, MEM)], prob_a[:, tile(b, MEM)], rl[:, b:b + 1], None, ALU.mult)
                    ins.then_inc(probs_m, 1)

                def y_head(no, t):
                    dve.wait_ge(values2, no + 1)
                    dve.scalar_tensor_tensor(g[:, tile(t)], ov[0][:, :], 0.5, sg, ALU.mult, ALU.mult).then_inc(y_a, 1)

                def head(i, j, first=False, last=False):
                    h = i * 2 + j
                    no = l * MLA + (i * 2 + (j + 1))
                    hc, ga, gb = (chunk2(l, HEAD + 3 * j + n, i, 6) for n in range(3))
                    link = Links(soft2_link, (no - 1) * 2)
                    split(ga)
                    dve.wait_ge(chunk_done, hc.n + 1)
                    rotate(qr, bank(0), qr_done, (no - 1) * 3)
                    dve.tensor_tensor(qr[0:64, :], qr[0:64, :], dg[0:64, :], ALU.add).then_inc(qr_done, 1)
                    split(gb)
                    if first:
                        mem_out(MH - 1)
                    else:
                        y_head(no - 1, h + (MLA - 1))
                    dve.wait_ge(y_a, no)
                    dve.wait_ge(tanh2, no * 2 - 1)
                    dve.scalar_tensor_tensor(sg, tz, 1.0, acc[ga.slot][:, :], ALU.add, ALU.mult).then_inc(evacuated[ga.slot], 1)
                    if not last:
                        split(chunk2(l, HEAD + 3 * j + 3, i, 6))
                    dve.wait_ge(scores2, no)
                    link.then(dve.tensor_reduce(mx[:, 0:TB], banks, AX.X, ALU.max))
                    dve.tensor_scalar(nm[:, 0:TB], mx[:, 0:TB], -MLA_SCALE, None, ALU.mult).then_inc(shift2, 1)
                    dve.wait_ge(exp2, no)
                    link.then(dve.reciprocal(rl[:, 0:TB], ls[:, 0:TB]))
                    for b in range(TB):
                        pr = (prob_a, prob_b)[b // 2][:, tile(b % 2)]
                        ins = dve.tensor_scalar(pr, pr, rl[:, b:b + 1], None, ALU.mult)
                    ins.then_inc(probs2, 1)
                    dve.wait_ge(tanh2, no * 2)
                    dve.scalar_tensor_tensor(dg[:, :], tz, 1.0, acc[gb.slot][:, :], ALU.add, ALU.mult).then_inc(evacuated[gb.slot], 1)
                    dve.wait_ge(evacuated[gb.slot], gb.uses + 1)
                    x = tile(h)
                    dve.scalar_tensor_tensor(g[:, x], g[:, x], 0.5, dg[:, :], ALU.mult, ALU.mult).then_inc(y_b, 1)
                    dve.wait_ge(turned2, no)
                    for b in range(2, TB):
                        dve.tensor_copy(pt[:, :].rearrange("p (k q) -> p k q", k=TB)[:, :, tile(b, P)],
                                        bank(b).rearrange("p (k q) -> p k q", k=TB)).then_inc(pt2_dve, 1)

                head(0, 0, first=True)
                head(0, 1)
                with dve.Fori(1, MLA // 2 - 1) as i:
                    head(i, 0)
                    head(i, 1)
                head(MLA // 2 - 1, 0)
                head(MLA // 2 - 1, 1, last=True)
                split(chunk2(l, N2 + WO))
                y_lo_tiles(l * KT + KT, chunk2(l, N2 + WO + 1), lambda: y_head(l * MLA + MLA, KT - 1))

            output(LAYERS, False)
            for c in (chunk2(LAYERS, KT), chunk2(LAYERS, KT + 1)):
                dve.wait_ge(evacuated[c.slot], c.uses)
            token_norm(norm_no(LAYERS, POSTN), LAYERS * 4 + 2, D)
            dve.wait_ge(r_done, norm_no(LAYERS, POSTN) + 1)
            for t in range(KT):
                new_x(t, LAYERS)


def kernel(**inputs):
    import numpy as np
    import concourse.bacc as bacc
    from concourse import mybir
    from concourse.bass_utils import run_bass_kernel_spmd

    P, D, S, MEM, KT = 128, 2048, 512, 256, 16
    a = {k: np.asarray(x) for k, x in inputs.items()}

    def turned(x):
        t, f = x.shape
        return np.ascontiguousarray(x.T.reshape(f // P, P, t).transpose(1, 0, 2).reshape(P, -1))

    def chunk(w):
        k, c = w.shape
        return w.reshape(k // P, P, c).transpose(1, 0, 2).reshape(P, -1)

    def wide(w, tiles):
        k, c = w.shape
        return list(w.reshape(-1, tiles, P, c).transpose(0, 2, 1, 3).reshape(-1, P, tiles * c))

    def per_partition(x):
        return x.reshape(-1, P).T

    def swapped(w):
        return np.concatenate([w, w[:, 32:], w[:, :32]], axis=1)

    wi = a["w_in_a"][0]
    tiles = []
    for i in range(16):
        tiles += [wi[:, P * i:P * (i + 1)], wi[:, 2560 + P * i:2560 + P * (i + 1)]]
    keys = [chunk(wi[:, 2048 + P * c:2048 + P * (c + 1)]) for c in range(2)]
    w1 = np.stack(keys + wide(wi[:, 2304:2560], 8) + [chunk(t) for t in tiles], axis=1)

    w2 = [chunk(a["w_out_a"][0][:, P * c:P * (c + 1)]) for c in range(16)]
    for l in range(2):
        wi, uq, ukv = a["w_in_2"][l], a["w_uq_2"][l], a["w_ukv_2"][l]
        col = lambda w, at: w[:, at:at + P]
        out = [chunk(col(a["w_mk_2"][l], P * c)) for c in range(4)] + wide(a["w_mv_2"][l], 4)
        tiles = [col(wi, P * c) for c in range(6)] + [swapped(wi[:, 768:832])]
        for c in range(4):
            tiles += [col(wi, 1344 + P * c), col(wi, 1856 + P * c), col(wi, 832 + P * c)]
        tiles += [col(wi, 2368 + P * c) for c in range(4)]
        out += [chunk(t) for t in tiles]
        for h in range(8):
            q = uq[:, 192 * h:192 * (h + 1)]
            q = chunk(np.concatenate([q[:, :128], swapped(q[:, 128:])], axis=1))
            parts = [q, chunk(ukv[:, 256 * h:256 * h + P])]
            if h % 2 == 0:
                parts.append(chunk(np.concatenate([ukv[:, 256 * n + P:256 * (n + 1)] for n in (h, h + 1)], axis=1)))
            parts.append(np.zeros((P, KT * P - sum(x.shape[1] for x in parts)), q.dtype))
            out.append(np.concatenate(parts, axis=1))
            out += [chunk(col(wi, 2880 + P * h)), chunk(col(wi, 2880 + P * (8 + h)))]
        wo = np.concatenate([a["w_o_2"][l][1024:], a["w_o_2"][l][:1024]])
        w2 += out + [chunk(col(wo, P * c)) for c in range(16)]
    w2 = np.stack(w2, axis=1)

    gains = [per_partition(a["g_pre"][0]), per_partition(a["g_post"][0])]
    gains += [per_partition(a["post_norm_g_2"][l]) for l in range(2)]
    gains += [per_partition(a["mem_norm_g_2"][l]) for l in range(2)]
    for l in range(2):
        gains += [per_partition(a[n][l]) for n in ("pre_norm_g_2", "q_norm_g_2", "kv_norm_g_2")]
        gains.append(a["conv_w_2"][l].reshape(3, 4, P).transpose(2, 1, 0).reshape(P, 12))

    row = np.arange(P)
    freq = (1.0 / (np.float32(10000.0) ** (np.arange(0, 64, 2, dtype=np.float32) / np.float32(64)))).astype(np.float32)
    slopes = (2.0 ** (-8.0 * np.arange(1, 33, dtype=np.float32) / 32)).astype(np.float32)
    consts = np.concatenate([
        np.eye(P, dtype=np.float32), np.ones((P, P), np.float32), np.broadcast_to(slopes, (P, 32)),
        freq[row % 32][:, None], np.where(row < 64, np.float32(np.pi / 2), np.float32(0))[:, None].astype(np.float32),
        np.where((row >= 64) & (row < 96), -1.0, 1.0)[:, None].astype(np.float32)], axis=1)
    dist = (row[:, None] + P - np.arange(2 * P)[None, :]).astype(np.float32)
    seen = (dist >= 0) & (dist < P)
    window = np.concatenate([np.where(seen & (np.arange(2 * P) >= P)[None, :], -dist, np.float32(-1e30))]
                            + [np.where(seen, -dist, np.float32(-1e30))] * 3, axis=1).astype(np.float32)

    arrays = {
        "xT": turned(a["x"][0]), "memT": turned(a["mem_2"][0]),
        "mem": np.ascontiguousarray(a["mem_2"][0].reshape(2, P, D).transpose(1, 0, 2)),
        "pos": a["positions_2"][0], "gains": np.concatenate(gains, axis=1), "sinks": a["sinks_a"][0],
        "consts": consts, "window": window, "w1": w1, "w2": w2,
    }
    nc = bacc.Bacc("TRN2", target_bir_lowering=False, num_devices=1)
    send, aps = {}, []
    for name, x in arrays.items():
        send[name + "_dram"] = np.ascontiguousarray(x)
        aps.append(nc.dram_tensor(name + "_dram", x.shape, mybir.dt.from_np(x.dtype), kind="ExternalInput").ap())
    out = nc.dram_tensor("out_dram", (P, KT * S), mybir.dt.float32, kind="ExternalOutput").ap()
    build(nc, *aps, out)
    r = run_bass_kernel_spmd(nc, [send], core_ids=[0])
    y = np.asarray(r.results[0]["out_dram"]).reshape(P, KT, S)
    return np.ascontiguousarray(y.transpose(2, 1, 0).reshape(1, S, D))
```

```python
def build(nc, xT, memT, mem, pos, gains, sinks, consts, window, w1, w2, wm, out):
    from contextlib import ExitStack

    import numpy as np
    import concourse.bass as bass
    from concourse import mybir

    F32, F32R, I32 = mybir.dt.float32, mybir.dt.float32r, mybir.dt.int32
    ACT = mybir.ActivationFunctionType
    ALU = mybir.AluOpType
    AX = mybir.AxisListType

    P = 128
    D, S, MEM = 2048, 512, 256
    KT, TB, MB = D // P, S // P, MEM // P
    EPS = 1e-6
    CW = KT * P

    HD, PAIRS, KVH = 64, 16, 4
    HALVES = (slice(0, HD), slice(HD, 2 * HD))
    PAIR1 = 4
    N1 = PAIR1 + 2 * PAIRS

    LAYERS, MLA, MH, CT = 2, 8, 4, 4
    WO, QL, KVL, KPE, CONV, QM, HEAD = 0, 16, 20, 22, 23, 35, 39
    N2 = HEAD + 3 * MLA
    QRT, KVRT = 4, 2
    QW = (2 * P, P)
    UK = [QRT * w for w in QW]
    UV = UK[0] + KVRT * P
    HW = (UV + KVRT * 2 * P, UK[1] + KVRT * P)
    MLA_SCALE, MEM_SCALE = (128 + 64) ** -0.5, P ** -0.5

    PRE1, POST, MEMG, GL, GN = 0, 16, 64, 96, 34
    PRE, QG, KVG, TAP = 0, 16, 20, 22
    IDENT, ONES, SLOPE, FREQ, PHASE, SIGN, C_COLS = 0, 128, 256, 288, 289, 290, 291
    TWO_PI, PI = float(2 * np.pi), float(np.float32(np.pi))
    TURN_A = 6.28125
    TURN_B = float(np.round((TWO_PI - TURN_A) * 2 ** 20) / 2 ** 20)
    TURN_C = TWO_PI - TURN_A - TURN_B

    class Chunk:

        def __init__(self, n, slot, uses, back):
            self.n, self.slot, self.uses, self.back = n, slot, uses, back

    def chunk1(p, i=0):
        new = isinstance(i, int) and i == 0 and p < 2
        return Chunk(i * 2 + p, p % 2, i + p // 2, None if new else 2)

    def chunk2(l, p, i=0, stride=0):
        turns = p // N2
        p = p % N2
        slot = p % 2
        per_turn = (N2 + 1 - slot) // 2
        n = l * N2 + (N1 + turns * N2 + p)
        uses = l * per_turn + (N1 // 2 + turns * per_turn + p // 2)
        if stride:
            n, uses = n + i * stride, uses + i * (stride // 2)
        return Chunk(n, slot, uses, 1 if p == 0 and stride == 0 else 2)

    POSTN, PREN, QN, KVN = 2, 3, 4, 5

    def norm_no(l, which):
        return l * 4 + which

    SQ_LAYER = KT + KT + QRT + KVRT
    ODD = KT // 2
    HT = 4
    XR = 3

    def sq_no(l, which):
        return l * SQ_LAYER + (0, KT, 2 * KT, 2 * KT + QRT, SQ_LAYER)[which - 2]

    def loads_of(l, w):
        slot = w % XR
        return slot, l * len(range(slot, ODD, XR)) + (w // XR + 1)

    residual = nc.dram_tensor("residual", (LAYERS + 1, P, KT * S), F32, kind="Internal").ap()\
        .rearrange("l p c -> p l c")
    ctx = ExitStack()
    with ctx:
        free = [(nc.sbuf_base + 63) // 64 * 64]

        def sb(name, cols, dt=F32, at=None):
            if at is None:
                at = free[0]
                free[0] += (cols * 4 + 63) // 64 * 64
            return nc.alloc_sbuf_tensor_at(name, [P, cols], dt, offset=at)

        raw = [sb(f"raw{s}", CW) for s in range(2)]
        hi = [sb(f"hi{s}", CW, F32R) for s in range(2)]
        lo = [sb(f"lo{s}", CW, F32R) for s in range(2)]
        h_hi, h_lo = sb("h_hi", KT * S, F32R), sb("h_lo", KT * S, F32R)
        g = sb("g", KT * S)
        m0 = free[0]
        m_hi, m_lo = sb("m_hi", KT * MEM, F32R), sb("m_lo", KT * MEM, F32R)
        m1 = m0 + 4 * KT * MEM
        m_n = sb("m_n", KT * MEM, at=m0)
        raw_m = [sb(f"raw_m{s}", CW, at=m1 + 4 * CW * s) for s in range(2)]
        a0 = free[0]
        area = sb("area", 4096)
        cst = sb("cst", C_COLS)
        gn = sb("gn", GL + LAYERS * GN)
        snk = sb("snk", 2 * PAIRS)
        cs = sb("cs", S)
        kr_hi = sb("kr_hi", S, F32R)
        r_mem = sb("r_mem", MEM)
        qr = sb("qr", S, F32R, at=free[0])
        sqacc, sq, dg = sb("sqacc", S), sb("sq", 2 * S), sb("dg", S)
        st = sb("st", 64)
        prob1, pt1 = sb("prob1", 2048, at=m0), sb("pt1", 2048, at=m0 + 8192)
        k_hi_all, vall = sb("k_hi_all", KVH * S, F32R, at=m1), sb("vall", TB * 256, at=m1 + 8192)
        win = sb("win", TB * 256, at=m1 + 12288)
        angle, posi = sb("angle", 3 * S, at=m0), sb("posi", S, I32, at=m0 + 12288)
        turns, memrow1 = sb("turns", S, I32, at=m0 + 14336), sb("memrow1", D, at=m1 + 2048)
        memrow0, sqx = sb("memrow0", D, at=a0 + 8192), sb("sqx", 4 * S, at=a0)
        x_last = sb("x_last", KT * S, at=m0)
        prob_m = sb("prob_m", TB * MEM, at=m0 + 12288)
        qn_lo, kn_lo = sb("qn_lo", S, F32R, at=m0 + 12288), sb("kn_lo", S, F32R, at=m0 + 14336)
        kr_lo, rot = sb("kr_lo", S, F32R, at=m1 + 12288), sb("rot", S, at=m1 + 14336)
        k_hi, k_lo = sb("k_hi", 640, F32R, at=a0), sb("k_lo", 640, F32R, at=a0 + 2560)
        vcur, q1 = sb("vcur", 512, at=a0 + 5120), sb("q1", 2 * S, F32R, at=a0 + 7168)
        k_lo_all = sb("k_lo_all", 2 * S, F32R, at=a0 + 11264)
        htmp, xr = sb("htmp", HT * S, at=a0), sb("xr", 2 * XR * S, at=a0)
        u = sb("u", S + 2, at=a0 + 4096)
        qm, ptm = sb("qm", 2 * S, at=a0), sb("ptm", MB * S, at=a0 + 4096)
        mv, mk = sb("mv", MB * 512, at=a0 + 8192), sb("mk", MH * MEM, at=a0 + 12288)
        qn_hi, kn_hi, v = sb("qn_hi", S, F32R, at=a0), sb("kn_hi", S, F32R, at=a0 + 2048), sb("v", TB * 256, at=a0 + 4096)
        prob2 = sb("prob2", TB * S, at=a0 + 8192)
        tz, sg = sq[:, 0:S], sq[:, S:2 * S]
        cv, cg = sq[:, 0:S], sq[:, S:2 * S]

        ident, ones = cst[:, IDENT:IDENT + P], cst[:, ONES:ONES + P]
        ms, r, nt, half = st[:, 0:4], st[:, 4:8], st[:, 8:12], st[:, 12:16]
        mx, nm, ls, es, rl = (st[:, 16 + 8 * i:24 + 8 * i] for i in range(5))
        ss = st[:, 56:58]

        acc = [ctx.enter_context(nc.psum_tensor(f"acc{s}", [P, 512], F32)) for s in range(2)]
        ov = [ctx.enter_context(nc.psum_tensor(f"ov{s}", [P, 512], F32)) for s in range(2)]
        sc = ctx.enter_context(nc.psum_tensor("sc", [P, 2048], F32))

        def bank(b, n=512, off=0):
            return sc[:, 512 * b + off:512 * b + off + n]

        def tile(t, n=S):
            return slice(t * n, (t + 1) * n) if isinstance(t, int) else bass.ds(t * n, n)

        def col(c):
            return slice(c, c + 1) if isinstance(c, int) else bass.ds(c, 1)

        def sem(name):
            return ctx.enter_context(nc.semaphore(name))

        loaded = [sem("loaded0"), sem("loaded1")]
        consts_in, pos_in, gains_in, window_in = (sem(f"{n}_in") for n in ("consts", "pos", "gains", "window"))
        x_in = [sem(f"x_in{c}") for c in range(4)]
        memrows_in, memory_in, residual_in = sem("memrows_in"), sem("memory_in"), [sem(f"residual_in{n}") for n in range(XR)]
        x_last_in = [sem(f"x_last_in{c}") for c in range(4)]
        x_stored, stored, out_stored = sem("x_stored"), sem("residual_stored"), sem("out_stored")
        waited = sem("waited")
        hi_done, lo_done, chunk_done = sem("hi_done"), sem("lo_done"), sem("chunk_done")
        evacuated = [sem("evacuated0"), sem("evacuated1")]
        squared, added, sums_done, ms_done, rs_done = (
            sem(n) for n in ("squared", "added", "sums_done", "ms_done", "rs_done"))
        x_squared, x_added = sem("x_squared"), sem("x_added")
        diag_done, r_done, norm_link, half_set = (sem(n) for n in ("diag_done", "r_done", "norm_link", "half_set"))
        normed_done, h_hi_done, h_even, h_odd = (sem(n) for n in ("normed", "h_hi_done", "h_even", "h_odd"))
        y_hi_done, y_done = sem("y_hi_done"), sem("y_done")
        mem_ss, r_mem_done = sem("mem_ss"), sem("r_mem_done")
        m_done, mem_chunk_done, mk_in = (sem(n) for n in ("m_done", "mem_chunk_done", "mk_in"))
        mem_loaded = [sem("mem_loaded0"), sem("mem_loaded1")]
        scaled, x_new, x_odd = sem("scaled"), sem("x_new"), sem("x_odd")
        rope_link, angle_done, sin_done = sem("rope_link"), sem("angle_done"), sem("sin_done")
        k_hi_in, q_hi_done = sem("k_hi_in"), sem("q_hi_done")
        kcur_pad, kcur_done, vcur_done, v_in = sem("kcur_pad"), sem("kcur_done"), sem("vcur_done"), sem("v_in")
        scores1, soft1_link, shift1, exp1, probs1 = (
            sem(n) for n in ("scores1", "soft1_link", "shift1", "exp1", "probs1"))
        turned1, pt1_act, pt1_dve, values1, tanh1, y1 = (
            sem(n) for n in ("turned1", "pt1_act", "pt1_dve", "values1", "tanh1", "y1"))
        lat_normed, lat_hi_done, lat_done = sem("lat_normed"), sem("lat_hi_done"), sem("lat_done")
        kr_link, kr_hi_done, conv_link, u_pad = (sem(n) for n in ("kr_link", "kr_hi_done", "conv_link", "u_pad"))
        scores_m, soft_m_link, shift_m, exp_m, probs_m, turned_m, ptm_done, values_m, om_done = (
            sem(n) for n in ("scores_m", "soft_m_link", "shift_m", "exp_m", "probs_m", "turned_m", "ptm_done", "values_m", "om_done"))
        qk_hi_done, rot_link, qr_hi_done, qk_done, v_done = (sem(n) for n in ("qk_hi_done", "rot_link", "qr_hi_done", "qk_done", "v_done"))
        scores2, soft2_link, shift2, exp2, probs2 = (sem(n) for n in ("scores2", "soft2_link", "shift2", "exp2", "probs2"))
        turned2, pt2_act, pt2_dve, values2, tanh2, y_a, y_b = (
            sem(n) for n in ("turned2", "pt2_act", "pt2_dve", "values2", "tanh2", "y_a", "y_b"))
        pe_from_one, dve_from_one = (scores1, values1, values2), (y1, om_done, y_a)
        block = ctx.enter_context(nc.Block())

        @block.sync
        def _(sp):
            sp.dma_start(cst[:, :], consts).then_inc(consts_in, 16)
            for c in range(4):
                part = tile(c, 4 * S)
                sp.dma_start(g[:, part], xT[:, part]).then_inc(x_in[c], 16)
            sp.dma_start(gn[:, :], gains).then_inc(gains_in, 16)

            def load(c, src, width=CW):
                if c.back is not None:
                    sp.wait_ge(lo_done, c.n + (1 - c.back))
                sp.dma_start(raw[c.slot][:, 0:width], src).then_inc(loaded[c.slot], 16)

            load(chunk1(0), w1[:, 0, :])
            load(chunk1(1), w1[:, 1, :])
            sp.dma_start(posi[:, :], pos.partition_broadcast(P)).then_inc(pos_in, 16)
            sp.dma_start(snk[:, :], sinks.partition_broadcast(P)).then_inc(window_in, 16)
            sp.dma_start(win[:, :], window).then_inc(window_in, 16)
            sp.dma_start(memrow0[:, :], mem[:, 0, :]).then_inc(memrows_in, 16)
            sp.dma_start(memrow1[:, :], mem[:, 1, :]).then_inc(memrows_in, 16)
            with sp.Fori(1, N1 // 2) as i:
                for j in range(2):
                    load(chunk1(j, i), w1[:, bass.ds(i * 2 + j, 1), :])
            with sp.Fori(0, LAYERS) as l:
                def load2(p, i=0, stride=0, width=CW):
                    c = chunk2(l, p, i, stride)
                    load(c, w2[:, bass.ds(c.n - N1, 1), 0:width], width)

                def load_memory_weights(c):
                    sp.dma_start(raw_m[c % 2][:, :], wm[:, bass.ds(l * (2 * MH) + c, 1), :]).then_inc(mem_loaded[c % 2], 16)

                load2(0)
                load2(1)
                load2(2)
                load2(3)
                sp.wait_ge(y_hi_done, l * KT + KT)
                load_memory_weights(0)
                load_memory_weights(1)
                with sp.Fori(0, (QL - 2) // 2) as i:
                    load2(4, i, 2)
                    load2(5, i, 2)
                for c in range(2, 2 * MH):
                    sp.wait_ge(mem_chunk_done, l * (2 * MH) + (c - 1))
                    load_memory_weights(c)
                with sp.Fori(0, (HEAD - QL - 3) // 2) as i:
                    load2(QL + 2, i, 2)
                    load2(QL + 3, i, 2)
                load2(HEAD - 1)
                with sp.Fori(0, MLA // 2) as i:
                    for j in range(6):
                        load2(HEAD + j, i, 6, HW[j // 3] if j % 3 == 0 else CW)
            for p in range(2):
                load(chunk2(LAYERS, p), w2[:, LAYERS * N2 + p, :])
            with sp.Fori(1, KT // 2) as i:
                for p in range(2):
                    load(chunk2(LAYERS, p, i, 2), w2[:, bass.ds(i * 2 + (LAYERS * N2 + p), 1), :])

        @block.gpsimd
        def _(pool):
            def settle():
                pool.sem_inc(waited, 1)

            def add_square(no, slot):
                pool.wait_ge(squared, no + 1)
                pool.wait_ge(added, no + 2)
                pool.tensor_tensor(sqacc[:, :], sqacc[:, :], sq[:, tile(slot)], ALU.add).then_inc(added, 1)

            def add_first_squares(no):
                pool.wait_ge(squared, no + 2)
                pool.tensor_tensor(sqacc[:, :], sq[:, 0:S], sq[:, S:2 * S], ALU.add).then_inc(added, 2)

            def add_squares(no, tiles):
                add_first_squares(no)
                with pool.Fori(1, tiles // 2) as i:
                    add_square(i * 2 + no, 0)
                    add_square(i * 2 + no + 1, 1)

            def root(no, n=TB):
                pool.wait_ge(ms_done, no + 1)
                pool.tensor_tensor(r[:, 0:n], ms[:, 0:n], half[:, 0:n], ALU.pow).then_inc(rs_done, 1)

            pool.sem_inc(added, 2)
            pool.memset(half, -0.5).then_inc(half_set, 1)
            pool.wait_ge(half_set, 1)
            for c in range(4):
                pool.wait_ge(x_in[c], 16)
            pool.dma_start(residual[:, 0, :], g[:, :]).then_inc(x_stored, 16)

            def h_lo_odd(t, count):
                pool.wait_ge(h_hi_done, count)
                pool.tensor_tensor(h_lo[:, tile(t)], htmp[:, tile(t % HT)], h_hi[:, tile(t)].bitcast(F32),
                                   ALU.subtract).then_inc(h_odd, 1)

            root(0)
            for t in range(1, KT, 2):
                h_lo_odd(t, t + 1)
            root(1, MB)

            pool.wait_ge(v_in, 1)
            pool.memset(k_hi[:, 0:P].bitcast(F32), 0.0).then_inc(kcur_pad, 1)
            pool.memset(k_lo[:, 0:P].bitcast(F32), 0.0).then_inc(kcur_pad, 1)
            pool.wait_ge(kcur_pad, 2)
            with pool.Fori(0, KVH // 2) as n:
                for j in range(2):
                    with pool.Fori(0, PAIRS // KVH) as m:
                        i = n * (2 * PAIRS // KVH) + m + j * (PAIRS // KVH)
                        pool.wait_ge(scores1, i + 1)
                        settle()
                        pool.tensor_copy(k_hi[:, P:P + S], k_hi_all[:, tile(n * 2 + j)]).then_inc(kcur_done, 1)
                        for done, half_ in enumerate(HALVES):
                            pool.wait_ge(kcur_done, i * 3 + done + 1)
                            settle()
                            pool.tensor_copy(k_lo[half_, P:P + S], k_lo_all[HALVES[j], tile(n)]).then_inc(kcur_done, 1)
                        pool.wait_ge(kcur_done, i * 3 + 3)
                        settle()
                        pool.wait_ge(values1, i + 1)
                        settle()
                        for half_ in HALVES:
                            pool.tensor_copy(vcur[:, :].rearrange("p (b d) -> p b d", b=TB)[:, :, half_],
                                             vall[:, :].rearrange("p (b d) -> p b d", b=TB)[:, :, tile(n * 2 + j, HD)])\
                                .then_inc(vcur_done, 1)

            def add_residual(w):
                t = 2 * w + 1
                pool.wait_ge(scaled, LAYERS * KT + (t + 1))
                pool.wait_ge(x_last_in[w // 2], 16)
                pool.tensor_tensor(g[:, tile(t)], g[:, tile(t)], x_last[:, tile(t)], ALU.add).then_inc(x_odd, 1)

            with pool.Fori(0, LAYERS) as l:
                pool.wait_ge(y_hi_done, l * KT + KT)
                settle()
                pool.dma_start(area[:, :], memT).then_inc(memory_in, 16)
                add_squares(sq_no(l, POSTN), KT)
                root(norm_no(l, POSTN))
                add_squares(sq_no(l, PREN), KT)
                root(norm_no(l, PREN))
                for t in range(1, KT, 2):
                    h_lo_odd(t, l * KT + (KT + t + 1))
                add_squares(sq_no(l, QN), QRT)
                root(norm_no(l, QN))
                add_first_squares(sq_no(l, KVN))
                root(norm_no(l, KVN))
            add_squares(sq_no(LAYERS, POSTN), KT)
            root(norm_no(LAYERS, POSTN))
            for w in range(ODD):
                add_residual(w)

        @block.tensor
        def _(pe):
            def begin(c):
                pe.wait_ge(lo_done, c.n + 1)
                if c.back is not None:
                    pe.wait_ge(evacuated[c.slot], c.uses)

            def passes(to, w_hi, w_lo, x_hi, x_lo, first, last, w_moves=False):
                for n, (a, b) in enumerate(((w_hi, x_hi), (w_hi, x_lo), (w_lo, x_hi))):
                    a, b = (b, a) if w_moves else (a, b)
                    ins = pe.matmul(to, a, b, start=first and n == 0, stop=last and n == 2)
                return ins

            def k_tile(c, k, x_hi, x_lo, first, last):
                w, x = tile(k, P), tile(k)
                return passes(acc[c.slot][:, :], hi[c.slot][:, w], lo[c.slot][:, w], x_hi[:, x], x_lo[:, x], first, last)

            def features(c, x_hi, x_lo, ready=None, pause=0, meanwhile=None):
                begin(c)
                for k in range(KT):
                    if meanwhile is not None and k == pause:
                        meanwhile()
                    if ready is not None:
                        ready(k)
                    ins = k_tile(c, k, x_hi, x_lo, k == 0, k == KT - 1)
                ins.then_inc(chunk_done, 1)

            def features_behind_h(c, d, before):
                lag = KT // 2
                begin(c)
                for k in range(KT + lag):
                    if k < KT:
                        pe.wait_ge((h_even, h_odd)[k % 2], before + (k // 2 + 1))
                        ins = k_tile(c, k, h_hi, h_lo, k == 0, k == KT - 1)
                        if k == KT - 1:
                            ins.then_inc(chunk_done, 1)
                    if k == lag:
                        begin(d)
                    if k >= lag:
                        ins = k_tile(d, k - lag, h_hi, h_lo, k == lag, k == KT + lag - 1)
                ins.then_inc(chunk_done, 1)

            def rows(c, at, tiles, to, x_hi, x_lo, n):
                pe.wait_ge(lo_done, c.n + 1)
                cols = CW // tiles
                for b in range(n // P):
                    for j in range(tiles):
                        w, x = tile(j, cols), slice((at + j) * n + b * P, (at + j) * n + (b + 1) * P)
                        ins = passes(to(b), hi[c.slot][:, w], lo[c.slot][:, w], x_hi[:, x], x_lo[:, x],
                                     at + j == 0, at + j == KT - 1, True)
                ins.then_inc(chunk_done, 1)

            def sums(count_on, squares):
                pe.wait_ge(count_on, squares)
                for b in range(TB):
                    ins = pe.matmul(ov[0][:, b:b + 1], sqacc[:, tile(b, P)], ones[:, 0:1], start=True, stop=True)
                ins.then_inc(sums_done, 1)

            def spread(no, to, n=S):
                pe.wait_ge(diag_done, no + 1)
                pe.matmul(to, ones, dg[:, 0:n], start=True, stop=True).then_inc(r_done, 1)

            for s in pe_from_one:
                pe.sem_inc(s, 1)
            pe.wait_ge(consts_in, 16)
            sums(x_added, ODD + 1)
            spread(0, bank(0))

            features_behind_h(chunk1(0), chunk1(1), 0)
            spread(1, ov[1][:, 0:MEM], MEM)
            for c in range(2):
                rows(chunk1(2 + c), c * KT // 2, KT // 2, lambda b: bank(b, 256), h_hi, h_lo, S)

            def scores_first(i):
                c = chunk1(PAIR1, i)
                pe.wait_ge(evacuated[c.slot], c.uses + 1)
                pe.wait_ge(kcur_done, i * 3 + 3)
                for b in range(TB):
                    for par in range(2):
                        to = bank(2 * par + b // 2, 256, b % 2 * 256)
                        q, k = tile(par * TB + b, P), slice(b * P, b * P + 256)
                        pe.matmul(to, q1[:, q], k_hi[:, k], start=True, stop=False)
                        ins = pe.matmul(to, q1[HALVES[par], q], k_lo[HALVES[par], k], start=False, stop=True)
                ins.then_inc(scores1, 1)

            def turn_first(i):
                pe.wait_ge(probs1, i + 1)
                for kb in range(TB):
                    for par in range(2):
                        for nxt in range(2):
                            b = kb + nxt
                            if b < TB:
                                src = par * 1024 + b * 256 + (1 - nxt) * P
                                ins = pe.transpose(bank(kb, P, par * 256 + nxt * P), prob1[:, src:src + P], ident)
                ins.then_inc(turned1, 1)

            def values_first(i):
                pe.wait_ge(pt1_act, i * 2 + 2)
                pe.wait_ge(pt1_dve, i * 2 + 2)
                pe.wait_ge(vcur_done, i * 2 + 2)
                pe.wait_ge(y1, i + 1)
                for par in range(2):
                    for kb in range(TB):
                        n = 256 if kb < TB - 1 else P
                        src = kb * 512 + par * 256
                        ins = pe.matmul(ov[par][:, kb * P:kb * P + n], vcur[:, tile(kb, P)], pt1[:, src:src + n],
                                        start=kb == 0, stop=kb == TB - 1, skip_group_check=True)
                ins.then_inc(values1, 1)

            def pair(i, first):
                features(chunk1(PAIR1, i), h_hi, h_lo, pause=8, meanwhile=None if first else lambda: turn_first(i - 1))
                if not first:
                    values_first(i - 1)
                scores_first(i)
                features(chunk1(PAIR1 + 1, i), h_hi, h_lo)

            pair(0, True)
            with pe.Fori(1, PAIRS) as i:
                pair(i, False)
            turn_first(PAIRS - 1)
            values_first(PAIRS - 1)

            def out_product(l):
                features(chunk2(l, WO), h_hi, h_lo, ready=lambda j: pe.wait_ge(y_done, l * KT + (j + 1)))
                features(chunk2(l, WO + 1), h_hi, h_lo)
                with pe.Fori(1, KT // 2) as i:
                    for p in range(2):
                        features(chunk2(l, WO + p, i, 2), h_hi, h_lo)

            with pe.Fori(0, LAYERS) as l:
                out_product(l)
                def memory_keys(c, to, meanwhile=None):
                    pe.wait_ge(mem_loaded[c % 2], l * (16 * MH) + 16 * (c // 2 + 1))
                    for k in range(KT):
                        if k == KT // 2 and meanwhile is not None:
                            meanwhile()
                        ins = pe.matmul(to, raw_m[c % 2][:, tile(k, P)], m_n[:, tile(k, MEM)], start=k == 0, stop=k == KT - 1)
                    ins.then_inc(mem_chunk_done, 1)

                def memory_values(c):
                    pe.wait_ge(mem_loaded[c % 2], l * (16 * MH) + 16 * ((MH + c) // 2 + 1))
                    for b in range(MB):
                        for j in range(KT // MH):
                            k = c * KT // MH + j
                            ins = pe.matmul(bank(2 + b), m_n[:, k * MEM + b * P:k * MEM + (b + 1) * P], raw_m[c % 2][:, tile(j)],
                                            start=k == 0, stop=k == KT - 1)
                    ins.then_inc(mem_chunk_done, 1)

                pe.wait_ge(m_done, l * KT + KT)
                memory_keys(0, ov[1][:, 0:MEM], lambda: sums(added, sq_no(l, PREN) + 2))
                spread(norm_no(l, POSTN), bank(0))
                memory_keys(1, ov[1][:, MEM:2 * MEM])
                memory_keys(2, bank(1, MEM))
                memory_keys(3, bank(1, MEM, MEM))
                memory_values(0)
                sums(added, sq_no(l, QN) + 2)
                memory_values(1)
                pe.wait_ge(mk_in, l * 2 + 2)
                spread(norm_no(l, PREN), bank(1))
                memory_values(2)
                memory_values(3)
                features_behind_h(chunk2(l, QL), chunk2(l, QL + 1), l * ODD + ODD)
                for j in range(2, QRT):
                    features(chunk2(l, QL + j), h_hi, h_lo)
                features(chunk2(l, KVL), h_hi, h_lo)
                sums(added, sq_no(l, KVN) + 2)
                features(chunk2(l, KVL + 1), h_hi, h_lo)
                spread(norm_no(l, QN), bank(0))
                features(chunk2(l, KPE), h_hi, h_lo)
                sums(added, sq_no(l, KVN) + (KVRT + 2))
                with pe.Fori(0, CT // 2) as i:
                    for j in range(6):
                        features(chunk2(l, CONV + j, i, 6), h_hi, h_lo)
                spread(norm_no(l, KVN), bank(1))

                def scores_mem(c):
                    ch = chunk2(l, QM + c)
                    pe.wait_ge(evacuated[ch.slot], ch.uses + 1)
                    for b in range(TB):
                        ins = pe.matmul(bank(b, MEM), qm[:, (c % 2) * S + b * P:(c % 2) * S + (b + 1) * P], mk[:, tile(c, MEM)],
                                        start=True, stop=True)
                    ins.then_inc(scores_m, 1)

                def turn_mem(c):
                    pe.wait_ge(probs_m, l * MH + (c + 1))
                    for b in range(TB):
                        for k in range(MB):
                            ins = pe.transpose(bank(b, P, k * P), prob_m[:, b * MEM + k * P:b * MEM + (k + 1) * P], ident)
                    ins.then_inc(turned_m, 1)

                def values_mem(c):
                    pe.wait_ge(ptm_done, l * MH + (c + 1))
                    pe.wait_ge(om_done, l * MH + (c + 1))
                    for k in range(MB):
                        ins = pe.matmul(ov[0][:, :], mv[:, k * 512 + c * P:k * 512 + (c + 1) * P], ptm[:, tile(k)],
                                        start=k == 0, stop=k == MB - 1)
                    ins.then_inc(values_m, 1)

                for c in range(MH):
                    if c == 0:
                        features(chunk2(l, QM), h_hi, h_lo)
                        pe.wait_ge(lat_done, l * 6 + 6)
                    else:
                        features(chunk2(l, QM + c), h_hi, h_lo, pause=8, meanwhile=lambda: turn_mem(c - 1))
                        values_mem(c - 1)
                    scores_mem(c)

                def project(c, j, free_banks):
                    begin(c)
                    w_hi, w_lo = hi[c.slot], lo[c.slot]

                    def product(to, at, x, first, last, w_moves=False):
                        w = slice(at, at + (2 * P if w_moves else P))
                        return passes(to, w_hi[:, w], w_lo[:, w], m_hi[:, x], m_lo[:, x], first, last, w_moves)

                    for k in range(QRT):
                        product(acc[c.slot][:, :], k * QW[j], tile(KVRT + k), k == 0, k == QRT - 1)
                    for k in range(KVRT):
                        ins = product(ov[1][:, :], UK[j] + k * P, tile(k), k == 0, k == KVRT - 1)
                    if j == 0:
                        free_banks()
                        for k in range(QRT):
                            product(bank(0), k * QW[j] + P, tile(KVRT + k), k == 0, k == QRT - 1)
                        for b in range(TB):
                            for k in range(KVRT):
                                ins = product(bank(1 + b // 2, 2 * P, b % 2 * 2 * P), UV + k * 2 * P,
                                              slice(k * S + b * P, k * S + (b + 1) * P), k == 0, k == KVRT - 1, True)
                    ins.then_inc(chunk_done, 1)

                def scores_head(no, i, j):
                    pe.wait_ge(v_done, l * (MLA // 2) + (i + 1))
                    pe.wait_ge(qk_done, no)
                    for b in range(TB):
                        q, r64 = tile(b, P), HALVES[j]
                        passes(bank(b), qn_hi[:, q], qn_lo[:, q], kn_hi[:, :], kn_lo[:, :], True, False)
                        pe.matmul(bank(b), qr[:, q], kr_hi[:, :], start=False, stop=False)
                        ins = pe.matmul(bank(b), qr[r64, q], kr_lo[r64, :], start=False, stop=True)
                    ins.then_inc(scores2, 1)

                def turn_head(no):
                    pe.wait_ge(probs2, no)
                    for b in range(TB):
                        for k in range(TB):
                            src = b * S + k * P
                            ins = pe.transpose(bank(b, P, k * P), prob2[:, src:src + P], ident)
                    ins.then_inc(turned2, 1)

                def turned_read(no):
                    pe.wait_ge(pt2_act, no * 2)
                    pe.wait_ge(pt2_dve, no * 2)

                def values_head(no, j):
                    turned_read(no)
                    pe.wait_ge(y_a, no)
                    for k in range(TB):
                        ins = pe.matmul(ov[0][:, :], v[:, (2 * k + j) * P:(2 * k + j + 1) * P], prob2[:, tile(k)], start=k == 0, stop=k == TB - 1)
                    ins.then_inc(values2, 1)

                def end_of_memory():
                    turn_mem(MH - 1)
                    pe.wait_ge(ptm_done, l * MH + MH)

                def head(i, j, first=False):
                    no = l * MLA + (i * 2 + (j + 1))
                    project(chunk2(l, HEAD + 3 * j, i, 6), j, end_of_memory if first else lambda: turned_read(no - 1))
                    if first:
                        values_mem(MH - 1)
                    else:
                        values_head(no - 1, 1 - j)
                    features(chunk2(l, HEAD + 3 * j + 1, i, 6), h_hi, h_lo)
                    scores_head(no, i, j)
                    features(chunk2(l, HEAD + 3 * j + 2, i, 6), h_hi, h_lo)
                    turn_head(no)

                head(0, 0, True)
                pe.wait_ge(om_done, l * MH + (MH + 1))
                head(0, 1)
                with pe.Fori(1, MLA // 2) as i:
                    head(i, 0)
                    head(i, 1)
                values_head(l * MLA + MLA, 1)
            out_product(LAYERS)
            sums(added, sq_no(LAYERS, PREN) + 2)
            spread(norm_no(LAYERS, POSTN), bank(0))

        @block.scalar
        def _(act):
            def split(c, width=CW):
                act.wait_ge(loaded[c.slot], (c.uses + 1) * 16)
                if c.back is not None:
                    act.wait_ge(chunk_done, c.n + (1 - c.back))
                act.activation(hi[c.slot][:, 0:width], raw[c.slot][:, 0:width], ACT.Copy).then_inc(hi_done, 1)

            def multiplied(c):
                act.wait_ge(chunk_done, c.n + 1)

            def square(src, no, slot):
                act.wait_ge(added, no + 1)
                act.activation(sq[:, tile(slot)], src, ACT.Square).then_inc(squared, 1)

            def h_hi_tile(t, count):
                act.wait_ge(normed_done, count)
                act.activation(h_hi[:, tile(t)], htmp[:, tile(t % HT)], ACT.Copy).then_inc(h_hi_done, 1)

            def y_hi_tile(t):
                act.activation(h_hi[:, tile(t)], g[:, tile(t)], ACT.Copy).then_inc(y_hi_done, 1)

            for w in range(ODD):
                if w % 2 == 0:
                    act.wait_ge(x_in[w // 2], 16)
                if w >= 2:
                    act.wait_ge(x_added, w - 1)
                act.activation(sqx[:, tile(w % 2, 2 * S)], g[:, tile(w, 2 * S)], ACT.Square).then_inc(x_squared, 1)
            split(chunk1(0))
            split(chunk1(1))
            for t in range(KT):
                h_hi_tile(t, t + 1)
            act.wait_ge(memrows_in, 32)
            for b, rows_ in enumerate((memrow0, memrow1)):
                ins = act.activation(rows_[:, :], rows_[:, :], ACT.Square, accum_out=ss[:, b:b + 1])
            ins.then_inc(mem_ss, 1)

            for c in range(2):
                ch = chunk1(c)
                split(chunk1(2 + c))
                if c == 0:
                    act.wait_ge(mem_ss, 1)
                multiplied(ch)
                for j in range(2):
                    for half_ in range(2):
                        ins = act.activation(k_hi_all[HALVES[half_], tile(2 * c + j)], acc[ch.slot][HALVES[j], :], ACT.Copy)
                ins.then_inc(k_hi_in, 1)
            act.wait_ge(r_done, 2)
            act.activation(r_mem[:, :], ov[1][:, 0:MEM], ACT.Copy).then_inc(r_mem_done, 1)
            act.wait_ge(angle_done, 1)
            act.activation(angle[:, 0:S], angle[:, 0:S], ACT.Sin).then_inc(sin_done, 1)
            split(chunk1(PAIR1))
            multiplied(chunk1(3))
            act.activation(vall[:, :].rearrange("p (b n) -> p b n", b=TB),
                           sc[:, :].rearrange("p (b n) -> p b n", b=TB)[:, :, 0:256], ACT.Copy).then_inc(v_in, 1)

            def turned_first(i, values_count):
                act.wait_ge(turned1, i + 1)
                act.wait_ge(values1, values_count)
                for b in range(2):
                    act.activation(pt1[:, tile(b)], bank(b), ACT.Copy).then_inc(pt1_act, 1)

            def pair(i, first):
                qc, zc = chunk1(PAIR1, i), chunk1(PAIR1 + 1, i)
                split(zc)
                if not first:
                    turned_first(i - 1, i)
                multiplied(qc)
                act.wait_ge(scores1, i + 1)
                for par, half_ in enumerate(HALVES):
                    ins = act.activation(q1[half_, tile(par)], acc[qc.slot][half_, :], ACT.Copy, scale=HD ** -0.5)
                ins.then_inc(q_hi_done, 1)
                split(chunk1(PAIR1 + 2, i))
                act.wait_ge(shift1, i + 1)
                for n in range(2 * TB):
                    act.activation(prob1[:, tile(n, 256)], prob1[:, tile(n, 256)], ACT.Exp,
                                   bias=nm[:, n:n + 1], accum_out=ls[:, n:n + 1])
                act.activation(es, es, ACT.Exp).then_inc(exp1, 1)
                multiplied(zc)
                act.wait_ge(evacuated[zc.slot], zc.uses)
                act.activation(tz, acc[zc.slot][:, :], ACT.Tanh, scale=0.5).then_inc(tanh1, 1)

            pair(0, True)
            with act.Fori(1, PAIRS) as i:
                pair(i, False)
            turned_first(PAIRS - 1, PAIRS)

            def y_hi_tiles(nxt, last_ready):
                with act.Fori(0, KT // 2) as t:
                    y_hi_tile(t)
                split(nxt)
                with act.Fori(KT // 2, KT - 1) as t:
                    y_hi_tile(t)
                last_ready()
                y_hi_tile(KT - 1)

            act.wait_ge(y1, PAIRS)
            act.wait_ge(chunk_done, N1)
            act.wait_ge(x_stored, 16)
            y_hi_tiles(chunk2(0, WO + 1), lambda: act.wait_ge(y1, PAIRS + 1))

            def reload_residual(l, w):
                slot = w % XR
                act.dma_start(xr[:, tile(slot, 2 * S)], residual[:, col(l), tile(w, 2 * S)]).then_inc(residual_in[slot], 16)

            def output_tile(l, t, slot, c, nxt):
                if nxt is not None:
                    split(nxt)
                multiplied(c)
                square(acc[c.slot][:, :], t + sq_no(l, POSTN), slot)
                act.activation(g[:, tile(t)], acc[c.slot][:, :], ACT.Copy).then_inc(evacuated[c.slot], 1)

            def output(l, more):
                output_tile(l, 0, 0, chunk2(l, WO), None)
                output_tile(l, 1, 1, chunk2(l, WO + 1), chunk2(l, WO + 2))
                with act.Fori(1, KT // 2 - (not more)) as i:
                    for j in range(2):
                        output_tile(l, i * 2 + j, j, chunk2(l, WO + j, i, 2), chunk2(l, WO + j + 1, i, 2))
                if not more:
                    output_tile(l, KT - 2, 0, chunk2(l, WO + KT - 2), chunk2(l, WO + KT - 1))
                    output_tile(l, KT - 1, 1, chunk2(l, WO + KT - 1), None)

            with act.Fori(0, LAYERS) as l:
                output(l, True)
                split(chunk2(l, QL + 1))
                act.wait_ge(m_done, l * KT + KT)
                for w in range(XR):
                    reload_residual(l, w)

                def memory_keys(half_, src):
                    act.wait_ge(mem_chunk_done, l * (2 * MH) + (2 * half_ + 2))
                    act.activation(mk[:, tile(half_)], src, ACT.Copy).then_inc(mk_in, 1)

                for t in range(KT):
                    if t == 6:
                        memory_keys(0, ov[1][:, :])
                    act.wait_ge(x_new, l * KT + (t + 1))
                    square(g[:, tile(t)], sq_no(l, PREN) + t, t % 2)
                    if t % 2 == 1:
                        w = t // 2
                        act.dma_start(residual[:, col(l + 1), tile(w, 2 * S)], g[:, tile(w, 2 * S)]).then_inc(stored, 16)
                        if w + XR < ODD:
                            reload_residual(l, w + XR)
                memory_keys(1, bank(1))
                for t in range(KT):
                    h_hi_tile(t, l * KT + (KT + t + 1))
                act.wait_ge(mem_chunk_done, l * (2 * MH) + 2 * MH)
                act.activation(mv[:, :], sc[:, 1024:2048], ACT.Copy)

                def latent(p, t, sq_at):
                    c = chunk2(l, p)
                    if p > QL:
                        split(chunk2(l, p + 1))
                    multiplied(c)
                    square(acc[c.slot][:, :], sq_at, t % 2)
                    act.activation(g[:, tile(t)], acc[c.slot][:, :], ACT.Copy).then_inc(evacuated[c.slot], 1)

                def latent_hi(t, slot, count):
                    act.wait_ge(lat_normed, count)
                    act.activation(m_hi[:, tile(t)], htmp[:, tile(slot)], ACT.Copy).then_inc(lat_hi_done, 1)

                act.wait_ge(stored, l * (8 * KT) + 8 * KT)
                for j in range(QRT):
                    latent(QL + j, MLA + KVRT + j, sq_no(l, QN) + j)
                for j in range(KVRT):
                    latent(KVL + j, MLA + j, sq_no(l, KVN) + j)
                split(chunk2(l, CONV))
                for j in range(QRT):
                    latent_hi(KVRT + j, j % 2, l * 6 + (j + 1))

                act.wait_ge(kr_link, l * 3 + 3)
                for n in range(2):
                    ins = act.activation(kr_hi[64 * n:64 * n + 64, :], rot[0:64, :], ACT.Copy)
                ins.then_inc(kr_hi_done, 1)

                act.wait_ge(added, sq_no(l, KVN) + (KVRT + 2))
                with act.Fori(0, CT // 2) as i:
                    for j in range(2):
                        c = chunk2(l, CONV + 3 * j, i, 6)
                        split(chunk2(l, CONV + 3 * j + 1, i, 6))
                        multiplied(c)
                        before = chunk2(l, CONV + 3 * j - 2, i, 6)
                        act.wait_ge(evacuated[before.slot], before.uses + 1)
                        act.activation(cg, acc[c.slot][:, :], ACT.Copy).then_inc(evacuated[c.slot], 1)
                        split(chunk2(l, CONV + 3 * j + 2, i, 6))
                        split(chunk2(l, CONV + 3 * j + 3, i, 6))
                for j in range(KVRT):
                    latent_hi(j, j, l * 6 + (QRT + j + 1))

                act.wait_ge(lat_done, l * 6 + 6)
                def turned_mem(c):
                    act.wait_ge(turned_m, l * MH + (c + 1))
                    for b in range(TB):
                        ins = act.activation(ptm[:, :].rearrange("p (k q) -> p k q", k=MB)[:, :, tile(b, P)],
                                             bank(b, MEM).rearrange("p (k q) -> p k q", k=MB), ACT.Copy)
                    ins.then_inc(ptm_done, 1)

                for c in range(MH):
                    ch = chunk2(l, QM + c)
                    split(chunk2(l, QM + c + 1))
                    if c > 0:
                        turned_mem(c - 1)
                    multiplied(ch)
                    act.activation(qm[:, tile(c % 2)], acc[ch.slot][:, :], ACT.Copy).then_inc(evacuated[ch.slot], 1)
                    act.wait_ge(shift_m, l * MH + (c + 1))
                    for b in range(TB):
                        ins = act.activation(prob_m[:, tile(b, MEM)], bank(b, MEM), ACT.Exp, scale=MEM_SCALE,
                                             bias=nm[:, b:b + 1], accum_out=ls[:, b:b + 1])
                    ins.then_inc(exp_m, 1)

                def head(i, j, first=False, last=False):
                    no = l * MLA + (i * 2 + (j + 1))
                    hc, ga, gb = (chunk2(l, HEAD + 3 * j + n, i, 6) for n in range(3))
                    split(ga)
                    if first:
                        turned_mem(MH - 1)
                    multiplied(hc)
                    act.activation(kn_hi[:, :], ov[1][:, :], ACT.Copy)
                    act.activation(qn_hi[:, :], acc[hc.slot][:, :], ACT.Copy).then_inc(qk_hi_done, 1)
                    if j == 0:
                        act.wait_ge(rot_link, l * MLA + (i * 2 + 2))
                    act.activation(qr[HALVES[j], :], rot[HALVES[j], :], ACT.Copy).then_inc(qr_hi_done, 1)
                    if j == 0:
                        if first:
                            act.wait_ge(values_m, l * MH + MH)
                        act.wait_ge(values2, no)
                        act.activation(v[:, :], sc[:, 512:512 + TB * 256], ACT.Copy).then_inc(v_done, 1)
                    split(gb)
                    multiplied(ga)
                    before = chunk2(l, HEAD + 3 * j - 1, i, 6)
                    act.wait_ge(evacuated[before.slot], before.uses + 1)
                    act.activation(tz, acc[ga.slot][:, :], ACT.Tanh, scale=0.5).then_inc(tanh2, 1)
                    if not last:
                        split(chunk2(l, HEAD + 3 * j + 3, i, 6), HW[1 - j])
                    act.wait_ge(shift2, no)
                    for b in range(TB):
                        ins = act.activation(prob2[:, tile(b)], bank(b), ACT.Exp, scale=MLA_SCALE,
                                             bias=nm[:, b:b + 1], accum_out=ls[:, b:b + 1])
                    ins.then_inc(exp2, 1)
                    multiplied(gb)
                    act.wait_ge(evacuated[ga.slot], ga.uses + 1)
                    act.activation(tz, acc[gb.slot][:, :], ACT.Tanh, scale=0.5).then_inc(tanh2, 1)
                    act.wait_ge(turned2, no)
                    for b in range(2):
                        act.activation(prob2[:, :].rearrange("p (k q) -> p k q", k=TB)[:, :, tile(b, P)],
                                       bank(b).rearrange("p (k q) -> p k q", k=TB), ACT.Copy).then_inc(pt2_act, 1)

                head(0, 0, first=True)
                head(0, 1)
                with act.Fori(1, MLA // 2 - 1) as i:
                    head(i, 0)
                    head(i, 1)
                head(MLA // 2 - 1, 0)
                head(MLA // 2 - 1, 1, last=True)

                split(chunk2(l, N2 + WO))
                act.wait_ge(y_b, l * MLA + MLA)
                act.wait_ge(y_a, l * MLA + MLA)
                act.sem_inc(waited, 1)
                y_hi_tiles(chunk2(l, N2 + WO + 1), lambda: act.wait_ge(y_a, l * MLA + (MLA + 1)))

            for c in range(4):
                act.dma_start(x_last[:, tile(c, 4 * S)], residual[:, LAYERS, tile(c, 4 * S)]).then_inc(x_last_in[c], 16)
            output(LAYERS, False)
            for w in range(ODD):
                act.wait_ge(x_new, LAYERS * KT + w + 1)
                act.wait_ge(x_odd, w + 1)
                act.dma_start(out[:, tile(w, 2 * S)], g[:, tile(w, 2 * S)]).then_inc(out_stored, 16)
            act.wait_ge(out_stored, 16 * ODD)
            act.wait_ge(stored, LAYERS * 16 * ODD)

        @block.vector
        def _(dve):
            def split(c, width=CW):
                dve.wait_ge(hi_done, c.n + 1)
                dve.tensor_tensor(lo[c.slot][:, 0:width], raw[c.slot][:, 0:width], hi[c.slot][:, 0:width].bitcast(F32),
                                  ALU.subtract).then_inc(lo_done, 1)

            class Links:

                def __init__(self, sem_, start):
                    self.sem, self.start, self.n = sem_, start, 0

                def then(self, ins):
                    self.n += 1
                    ins.then_inc(self.sem, 1)
                    dve.wait_ge(self.sem, self.start + self.n)

            def norm(no, features_, sums_, n=TB):
                link = Links(norm_link, no * 4)
                dve.tensor_scalar(ms[:, 0:n], sums_, 1.0 / features_, EPS, ALU.mult, ALU.add).then_inc(ms_done, 1)
                dve.wait_ge(rs_done, no + 1)
                link.then(dve.tensor_tensor(nt[:, 0:n], r[:, 0:n], r[:, 0:n], ALU.mult))
                link.then(dve.tensor_tensor(nt[:, 0:n], nt[:, 0:n], ms[:, 0:n], ALU.mult))
                link.then(dve.tensor_scalar(nt[:, 0:n], nt[:, 0:n], -0.5, 1.5, ALU.mult, ALU.add))
                link.then(dve.tensor_tensor(r[:, 0:n], r[:, 0:n], nt[:, 0:n], ALU.mult))
                for b in range(n):
                    ins = dve.tensor_scalar(dg[:, tile(b, P)], ident, r[:, b:b + 1], None, ALU.mult)
                ins.then_inc(diag_done, 1)

            def token_norm(no, count, features_):
                dve.wait_ge(sums_done, count)
                norm(no, features_, ov[0][:, 0:TB])

            def normed(to, src, gain, r_b):
                return dve.scalar_tensor_tensor(to, src, gain, r_b, ALU.mult, ALU.mult)

            for m in dve_from_one:
                dve.sem_inc(m, 1)
            dve.wait_ge(consts_in, 16)
            for w in range(1, ODD):
                dve.wait_ge(x_squared, w + 1)
                if w > 1:
                    dve.wait_ge(x_added, w)
                a = sqx[:, 0:2 * S] if w == 1 else sq[:, :]
                dve.tensor_tensor(sq[:, :], a, sqx[:, tile(w % 2, 2 * S)], ALU.add).then_inc(x_added, 2 if w == 1 else 1)
            dve.wait_ge(x_added, ODD)
            dve.tensor_tensor(sqacc[:, :], sq[:, 0:S], sq[:, S:2 * S], ALU.add).then_inc(x_added, 1)
            token_norm(0, 1, D)
            split(chunk1(0))

            def h_tiles(gain, r_b, before, half_before, splits=None):
                def lo_even(t):
                    dve.wait_ge(h_hi_done, before + (t + 1))
                    dve.tensor_tensor(h_lo[:, tile(t)], htmp[:, tile(t % HT)], h_hi[:, tile(t)].bitcast(F32), ALU.subtract)\
                        .then_inc(h_even, 1)

                for t in range(KT):
                    if splits is not None and t in splits:
                        split(splits[t])
                    if t >= HT or not isinstance(before, int):
                        dve.wait_ge((h_even, h_odd)[t % 2], half_before + (max(t - HT, -1) + 2) // 2)
                    normed(htmp[:, tile(t % HT)], g[:, tile(t)], gn[:, col(gain + t)], r_b).then_inc(normed_done, 1)
                    if t >= 2 and t % 2 == 0:
                        lo_even(t - 2)
                lo_even(KT - 2)

            dve.wait_ge(gains_in, 16)
            dve.wait_ge(r_done, 1)
            h_tiles(PRE1, bank(0), 0, 0, {4: chunk1(1)})
            dve.wait_ge(mem_ss, 1)
            norm(1, D, ss, MB)
            split(chunk1(2))
            for c in range(2):
                ch = chunk1(c)
                dve.wait_ge(k_hi_in, c + 1)
                for j, half_ in enumerate(HALVES):
                    ins = dve.tensor_tensor(k_lo_all[half_, tile(c)], acc[ch.slot][half_, :],
                                            k_hi_all[half_, tile(2 * c + j)].bitcast(F32), ALU.subtract)
                ins.then_inc(evacuated[ch.slot], 2)
            split(chunk1(3))

            ang, kf, tmp = (angle[:, tile(n)] for n in range(3))
            rope = Links(rope_link, 0)
            dve.wait_ge(pos_in, 16)
            rope.then(dve.tensor_copy(ang, posi[:, :]))
            rope.then(dve.tensor_scalar(ang, ang, cst[:, FREQ:FREQ + 1], None, ALU.mult))
            rope.then(dve.tensor_scalar(turns[:, :], ang, 1 / TWO_PI, None, ALU.mult))
            rope.then(dve.tensor_copy(kf, turns[:, :]))
            for part in (TURN_A, TURN_B, TURN_C):
                rope.then(dve.scalar_tensor_tensor(ang, kf, -part, ang, ALU.mult, ALU.add))
            rope.then(dve.tensor_scalar(ang, ang, cst[:, PHASE:PHASE + 1], None, ALU.add))
            for op, past, turn in ((ALU.is_gt, PI, -TWO_PI), (ALU.is_lt, -PI, TWO_PI)):
                rope.then(dve.tensor_scalar(tmp, ang, past, turn, op, ALU.mult))
                rope.then(dve.tensor_tensor(ang, ang, tmp, ALU.add))
            below_pi = float(np.nextafter(np.float32(np.pi), np.float32(0)))
            dve.tensor_scalar(ang, ang, below_pi, -below_pi, ALU.min, ALU.max).then_inc(angle_done, 1)
            dve.wait_ge(sin_done, 1)
            rope.then(dve.tensor_scalar(cs[:, :], ang, cst[:, SIGN:SIGN + 1], None, ALU.mult))
            split(chunk1(PAIR1))

            def softmax_first(i):
                link = Links(soft1_link, i * 5)
                dve.wait_ge(scores1, i + 2)
                for par in range(2):
                    half_ = tile(par, 1024)
                    ins = dve.scalar_tensor_tensor(prob1[:, half_], win[:, :], cst[:, col(i * 2 + (SLOPE + par))], sc[:, half_],
                                                   ALU.mult, ALU.add)
                link.then(ins)
                link.then(dve.tensor_reduce(mx, prob1[:, :].rearrange("p (n k) -> p n k", n=2 * TB), AX.X, ALU.max))
                sinks_ = [snk[:, col(i * 2 + par)] for par in range(2)]
                for par in range(2):
                    ins = dve.tensor_scalar(mx[:, tile(par, TB)], mx[:, tile(par, TB)], sinks_[par], None, ALU.max)
                link.then(ins)
                for par in range(2):
                    dve.tensor_scalar(es[:, tile(par, TB)], mx[:, tile(par, TB)], -1.0, sinks_[par], ALU.mult, ALU.add)
                dve.tensor_scalar(nm, mx, -1.0, None, ALU.mult).then_inc(shift1, 1)
                dve.wait_ge(exp1, i + 1)
                link.then(dve.tensor_tensor(ls, ls, es, ALU.add))
                link.then(dve.reciprocal(rl, ls))
                for n in range(2 * TB):
                    ins = dve.tensor_scalar(prob1[:, tile(n, 256)], prob1[:, tile(n, 256)], rl[:, n:n + 1], None, ALU.mult)
                ins.then_inc(probs1, 1)
                assert link.n == 5

            def y_first(i):
                zc = chunk1(PAIR1 + 1, i)
                dve.wait_ge(values1, i + 2)
                dve.wait_ge(evacuated[zc.slot], zc.uses + 1)
                for par in range(2):
                    rows_ = slice(HD * par, HD * par + HD)
                    ins = dve.scalar_tensor_tensor(g[rows_, tile(i)], ov[par][rows_, :], 0.5, sg[rows_, :], ALU.mult, ALU.mult)
                ins.then_inc(y1, 1)

            def turned_first(i):
                dve.wait_ge(turned1, i + 1)
                for b in range(2, TB):
                    dve.tensor_copy(pt1[:, tile(b)], bank(b)).then_inc(pt1_dve, 1)

            def q_lo(i):
                qc = chunk1(PAIR1, i)
                dve.wait_ge(q_hi_done, i + 1)
                for par, half_ in enumerate(HALVES):
                    ins = dve.scalar_tensor_tensor(q1[HALVES[1 - par], tile(par)], acc[qc.slot][half_, :], HD ** -0.5,
                                                   q1[half_, tile(par)].bitcast(F32), ALU.mult, ALU.subtract)
                ins.then_inc(evacuated[qc.slot], 1)

            def pair(i, first):
                zc = chunk1(PAIR1 + 1, i)
                split(zc)
                if not first:
                    turned_first(i - 1)
                q_lo(i)
                if not first:
                    y_first(i - 1)
                split(chunk1(PAIR1 + 2, i))
                softmax_first(i)
                dve.wait_ge(tanh1, i + 1)
                dve.scalar_tensor_tensor(sg, tz, 1.0, acc[zc.slot][:, :], ALU.add, ALU.mult).then_inc(evacuated[zc.slot], 1)

            def y_lo_tile(t, count):
                dve.wait_ge(y_hi_done, count)
                dve.tensor_tensor(h_lo[:, tile(t)], g[:, tile(t)], h_hi[:, tile(t)].bitcast(F32),
                                  ALU.subtract).then_inc(y_done, 1)

            dve.wait_ge(window_in, 32)
            dve.wait_ge(x_stored, 16)
            pair(0, True)
            with dve.Fori(1, PAIRS) as i:
                pair(i, False)
            turned_first(PAIRS - 1)

            def y_lo_tiles(before, nxt, last):
                with dve.Fori(0, KT // 2) as t:
                    y_lo_tile(t, before + t + 1)
                split(nxt)
                with dve.Fori(KT // 2, KT - 1) as t:
                    y_lo_tile(t, before + t + 1)
                last()
                y_lo_tile(KT - 1, before + KT)

            y_lo_tiles(0, chunk2(0, WO + 1), lambda: y_first(PAIRS - 1))

            def output_tile(l, t, nxt, memory):
                if nxt is not None:
                    split(nxt)
                if memory:
                    x = tile(t, MEM)
                    normed(m_n[:, x], area[:, x], gn[:, col(l * KT + t + MEMG)], r_mem[:, :]).then_inc(m_done, 1)

            def output(l, memory):
                split(chunk2(l, WO + 2))
                if memory:
                    dve.wait_ge(memory_in, l * 16 + 16)
                    output_tile(l, 0, None, memory)
                    output_tile(l, 1, None, memory)
                with dve.Fori(1, KT // 2 - (not memory)) as i:
                    for j in range(2):
                        output_tile(l, i * 2 + j, chunk2(l, WO + j + 1, i, 2), memory)
                if not memory:
                    split(chunk2(l, WO + KT - 1))

            dve.wait_ge(r_mem_done, 1)

            def new_x(t, l):
                normed(g[:, tile(t)], g[:, tile(t)], gn[:, col(l * KT + (t + POST))], bank(0)).then_inc(scaled, 1)
                if t % 2 == 0 or l is not LAYERS:
                    dve.wait_ge(scaled, l * KT + (t + 1))
                    if l is LAYERS:
                        dve.wait_ge(x_last_in[t // 4], 16)
                        x = x_last[:, tile(t)]
                    else:
                        slot, loads = loads_of(l, t // 2)
                        dve.wait_ge(residual_in[slot], loads * 16)
                        x = xr[:, tile(2 * slot + t % 2)]
                    dve.tensor_tensor(g[:, tile(t)], g[:, tile(t)], x, ALU.add).then_inc(x_new, 1)

            with dve.Fori(0, LAYERS) as l:
                output(l, True)
                for c in (chunk2(l, QL), chunk2(l, QL + 1)):
                    dve.wait_ge(evacuated[c.slot], c.uses)
                token_norm(norm_no(l, POSTN), l * 4 + 2, D)
                split(chunk2(l, QL + 1))
                dve.wait_ge(r_done, norm_no(l, POSTN) + 1)
                for t in range(KT):
                    new_x(t, l)
                token_norm(norm_no(l, PREN), l * 4 + 3, D)
                dve.wait_ge(r_done, norm_no(l, PREN) + 1)
                h_tiles(l * GN + (GL + PRE), bank(1), l * KT + KT, l * ODD + ODD)
                for j in range(1, QRT + 1):
                    split(chunk2(l, QL + j + 1))

                def latents(first, tiles, gain, r_b, before):
                    for n in range(tiles):
                        if before + n < 2:
                            dve.wait_ge((h_even, h_odd)[n], l * ODD + 2 * ODD)
                        else:
                            dve.wait_ge(lat_done, l * 6 + (before + n - 1))
                        normed(htmp[:, tile(n % 2)], g[:, tile(MLA + first + n)], gn[:, col(l * GN + (GL + gain + n))], r_b)\
                            .then_inc(lat_normed, 1)
                        dve.wait_ge(lat_hi_done, l * 6 + (before + n + 1))
                        x = tile(first + n)
                        dve.tensor_tensor(m_lo[:, x], htmp[:, tile(n % 2)], m_hi[:, x].bitcast(F32),
                                          ALU.subtract).then_inc(lat_done, 1)

                token_norm(norm_no(l, QN), l * 4 + 4, QRT * P)
                split(chunk2(l, KPE))
                split(chunk2(l, CONV))
                dve.wait_ge(r_done, norm_no(l, QN) + 1)
                for j in range(QRT):
                    c = chunk2(l, QL + j)
                    dve.wait_ge(evacuated[c.slot], c.uses + 1)
                latents(KVRT, QRT, QG, bank(0), 0)

                kc = chunk2(l, KPE)
                link = Links(kr_link, l * 3)
                dve.wait_ge(chunk_done, kc.n + 1)
                src = acc[kc.slot]
                link.then(dve.tensor_tensor(rot[0:64, :], src[0:64, :], cs[0:64, :], ALU.mult))
                link.then(dve.tensor_tensor(dg[0:64, :], src[64:128, :], cs[64:128, :], ALU.mult))
                link.then(dve.tensor_tensor(rot[0:64, :], rot[0:64, :], dg[0:64, :], ALU.add))
                dve.wait_ge(kr_hi_done, l + 1)
                for half_ in HALVES:
                    ins = dve.tensor_tensor(kr_lo[half_, :], rot[0:64, :], kr_hi[0:64, :].bitcast(F32), ALU.subtract)
                ins.then_inc(evacuated[kc.slot], 1)
                token_norm(norm_no(l, KVN), l * 4 + 5, KVRT * P)
                dve.memset(u[:, 0:1], 0.0)
                dve.memset(u[:, S + 1:S + 2], 0.0).then_inc(u_pad, 1)
                dve.wait_ge(u_pad, l + 1)
                dve.sem_inc(waited, 1)

                with dve.Fori(0, CT // 2) as i:
                    for j in range(2):
                        gc, xi, gb = (chunk2(l, CONV + 3 * j + n, i, 6) for n in range(3))
                        link = Links(conv_link, l * (3 * CT) + (i * 6 + 3 * j))
                        taps = [gn[:, col(l * GN + (i * 6 + (GL + TAP + 3 * j + n)))] for n in range(3)]
                        split(xi)
                        split(gb)
                        dve.wait_ge(chunk_done, xi.n + 1)
                        dve.wait_ge(evacuated[gc.slot], gc.uses + 1)
                        dve.tensor_tensor(u[:, 1:S + 1], acc[xi.slot][:, :], cg, ALU.mult).then_inc(evacuated[xi.slot], 1)
                        dve.wait_ge(evacuated[xi.slot], xi.uses + 1)
                        link.then(dve.tensor_scalar(cv, u[:, 0:S], taps[0], None, ALU.mult))
                        for n in (1, 2):
                            link.then(dve.scalar_tensor_tensor(cv, u[:, n:n + S], taps[n], cv, ALU.mult, ALU.add))
                        split(chunk2(l, CONV + 3 * j + 3, i, 6))
                        dve.wait_ge(chunk_done, gb.n + 1)
                        dve.tensor_tensor(g[:, tile(i * 2 + j)], acc[gb.slot][:, :], cv, ALU.mult)\
                            .then_inc(evacuated[gb.slot], 1)
                dve.wait_ge(r_done, norm_no(l, KVN) + 1)
                for j in range(KVRT):
                    c = chunk2(l, KVL + j)
                    dve.wait_ge(evacuated[c.slot], c.uses + 1)
                latents(0, KVRT, KVG, bank(1), QRT)

                banks = sc[:, :].rearrange("p (b n) -> p b n", b=TB)
                for c in range(MH):
                    no = l * MH + (c + 1)
                    link = Links(soft_m_link, l * (2 * MH) + 2 * c)

                    def mem_out(c):
                        dve.wait_ge(values_m, l * MH + (c + 1))
                        dve.tensor_copy(g[:, tile(CT + c)], ov[0][:, :]).then_inc(om_done, 1)

                    split(chunk2(l, QM + c + 1))
                    if c > 0:
                        mem_out(c - 1)
                    dve.wait_ge(scores_m, no)
                    link.then(dve.tensor_reduce(mx[:, 0:TB], banks[:, :, 0:MEM], AX.X, ALU.max))
                    dve.tensor_scalar(nm[:, 0:TB], mx[:, 0:TB], -MEM_SCALE, None, ALU.mult).then_inc(shift_m, 1)
                    dve.wait_ge(exp_m, no)
                    link.then(dve.reciprocal(rl[:, 0:TB], ls[:, 0:TB]))
                    for b in range(TB):
                        ins = dve.tensor_scalar(prob_m[:, tile(b, MEM)], prob_m[:, tile(b, MEM)], rl[:, b:b + 1], None, ALU.mult)
                    ins.then_inc(probs_m, 1)

                def y_head(no, t):
                    dve.wait_ge(values2, no + 1)
                    dve.scalar_tensor_tensor(g[:, tile(t)], ov[0][:, :], 0.5, sg, ALU.mult, ALU.mult).then_inc(y_a, 1)

                def rotate_pair(src, link):
                    for half_ in HALVES:
                        dve.tensor_tensor(rot[half_, :], src[half_, :], cs[0:64, :], ALU.mult)
                    for at in range(0, P, 32):
                        from_, sin_ = (at ^ 32), 64 + at % 64
                        ins = dve.tensor_tensor(dg[at:at + 32, :], src[from_:from_ + 32, :], cs[sin_:sin_ + 32, :], ALU.mult)
                    link.then(ins)
                    link.then(dve.tensor_tensor(rot[:, :], rot[:, :], dg[:, :], ALU.add))

                def head(i, j, first=False, last=False):
                    h = i * 2 + j
                    no = l * MLA + (i * 2 + (j + 1))
                    hc, ga, gb = (chunk2(l, HEAD + 3 * j + n, i, 6) for n in range(3))
                    link = Links(soft2_link, (no - 1) * 2)
                    split(ga)
                    dve.wait_ge(chunk_done, hc.n + 1)
                    if j == 0:
                        rotate_pair(bank(0), Links(rot_link, l * MLA + i * 2))
                    dve.wait_ge(qk_hi_done, no)
                    dve.tensor_tensor(kn_lo[:, :], ov[1][:, :], kn_hi[:, :].bitcast(F32), ALU.subtract)
                    dve.tensor_tensor(qn_lo[:, :], acc[hc.slot][:, :], qn_hi[:, :].bitcast(F32), ALU.subtract)\
                        .then_inc(evacuated[hc.slot], 1)
                    dve.wait_ge(qr_hi_done, no)
                    dve.tensor_tensor(qr[HALVES[1 - j], :], rot[HALVES[j], :], qr[HALVES[j], :].bitcast(F32), ALU.subtract)\
                        .then_inc(qk_done, 1)
                    split(gb)
                    if first:
                        mem_out(MH - 1)
                    else:
                        y_head(no - 1, h + (MLA - 1))
                    dve.wait_ge(y_a, no)
                    dve.wait_ge(tanh2, no * 2 - 1)
                    dve.scalar_tensor_tensor(sg, tz, 1.0, acc[ga.slot][:, :], ALU.add, ALU.mult).then_inc(evacuated[ga.slot], 1)
                    if not last:
                        split(chunk2(l, HEAD + 3 * j + 3, i, 6), HW[1 - j])
                    dve.wait_ge(scores2, no)
                    link.then(dve.tensor_reduce(mx[:, 0:TB], banks, AX.X, ALU.max))
                    dve.tensor_scalar(nm[:, 0:TB], mx[:, 0:TB], -MLA_SCALE, None, ALU.mult).then_inc(shift2, 1)
                    dve.wait_ge(exp2, no)
                    link.then(dve.reciprocal(rl[:, 0:TB], ls[:, 0:TB]))
                    for b in range(TB):
                        pr = prob2[:, tile(b)]
                        ins = dve.tensor_scalar(pr, pr, rl[:, b:b + 1], None, ALU.mult)
                    ins.then_inc(probs2, 1)
                    dve.wait_ge(tanh2, no * 2)
                    dve.scalar_tensor_tensor(dg[:, :], tz, 1.0, acc[gb.slot][:, :], ALU.add, ALU.mult).then_inc(evacuated[gb.slot], 1)
                    dve.wait_ge(evacuated[gb.slot], gb.uses + 1)
                    x = tile(h)
                    dve.scalar_tensor_tensor(g[:, x], g[:, x], 0.5, dg[:, :], ALU.mult, ALU.mult).then_inc(y_b, 1)
                    dve.wait_ge(turned2, no)
                    for b in range(2, TB):
                        dve.tensor_copy(prob2[:, :].rearrange("p (k q) -> p k q", k=TB)[:, :, tile(b, P)],
                                        bank(b).rearrange("p (k q) -> p k q", k=TB)).then_inc(pt2_dve, 1)

                head(0, 0, first=True)
                head(0, 1)
                with dve.Fori(1, MLA // 2 - 1) as i:
                    head(i, 0)
                    head(i, 1)
                head(MLA // 2 - 1, 0)
                head(MLA // 2 - 1, 1, last=True)
                split(chunk2(l, N2 + WO))
                y_lo_tiles(l * KT + KT, chunk2(l, N2 + WO + 1), lambda: y_head(l * MLA + MLA, KT - 1))

            output(LAYERS, False)
            for c in (chunk2(LAYERS, KT), chunk2(LAYERS, KT + 1)):
                dve.wait_ge(evacuated[c.slot], c.uses)
            token_norm(norm_no(LAYERS, POSTN), LAYERS * 4 + 2, D)
            dve.wait_ge(r_done, norm_no(LAYERS, POSTN) + 1)
            for t in range(KT):
                new_x(t, LAYERS)


def kernel(**inputs):
    import numpy as np
    import concourse.bacc as bacc
    from concourse import mybir
    from concourse.bass_utils import run_bass_kernel_spmd

    P, D, S, MEM, KT = 128, 2048, 512, 256, 16
    a = {k: np.asarray(x) for k, x in inputs.items()}

    def turned(x):
        t, f = x.shape
        return np.ascontiguousarray(x.T.reshape(f // P, P, t).transpose(1, 0, 2).reshape(P, -1))

    def chunk(w):
        k, c = w.shape
        return w.reshape(k // P, P, c).transpose(1, 0, 2).reshape(P, -1)

    def wide(w, tiles):
        k, c = w.shape
        return list(w.reshape(-1, tiles, P, c).transpose(0, 2, 1, 3).reshape(-1, P, tiles * c))

    def per_partition(x):
        return x.reshape(-1, P).T

    def swapped(w):
        return np.concatenate([w, w[:, 32:], w[:, :32]], axis=1)

    wi = a["w_in_a"][0]
    tiles = []
    for i in range(16):
        tiles += [wi[:, P * i:P * (i + 1)], wi[:, 2560 + P * i:2560 + P * (i + 1)]]
    keys = [chunk(wi[:, 2048 + P * c:2048 + P * (c + 1)]) for c in range(2)]
    w1 = np.stack(keys + wide(wi[:, 2304:2560], 8) + [chunk(t) for t in tiles], axis=1)

    wm = []
    w2 = [chunk(a["w_out_a"][0][:, P * c:P * (c + 1)]) for c in range(16)]
    for l in range(2):
        wi, uq, ukv = a["w_in_2"][l], a["w_uq_2"][l], a["w_ukv_2"][l]
        col = lambda w, at: w[:, at:at + P]
        wm += [chunk(col(a["w_mk_2"][l], P * c)) for c in range(4)] + wide(a["w_mv_2"][l], 4)
        tiles = [col(wi, P * c) for c in range(6)] + [swapped(wi[:, 768:832])]
        for c in range(4):
            tiles += [col(wi, 1344 + P * c), col(wi, 1856 + P * c), col(wi, 832 + P * c)]
        tiles += [col(wi, 2368 + P * c) for c in range(4)]
        out = [chunk(t) for t in tiles]
        for h in range(8):
            q = uq[:, 192 * h:192 * (h + 1)]
            nxt = uq[:, 192 * (h + 1) + 128:192 * (h + 2)]
            q = chunk(np.concatenate([q, nxt], axis=1) if h % 2 == 0 else q[:, :128])
            parts = [q, chunk(ukv[:, 256 * h:256 * h + P])]
            if h % 2 == 0:
                parts.append(chunk(np.concatenate([ukv[:, 256 * n + P:256 * (n + 1)] for n in (h, h + 1)], axis=1)))
            parts.append(np.zeros((P, KT * P - sum(x.shape[1] for x in parts)), q.dtype))
            out.append(np.concatenate(parts, axis=1))
            out += [chunk(col(wi, 2880 + P * h)), chunk(col(wi, 2880 + P * (8 + h)))]
        wo = np.concatenate([a["w_o_2"][l][1024:], a["w_o_2"][l][:1024]])
        w2 += out + [chunk(col(wo, P * c)) for c in range(16)]
    w2, wm = np.stack(w2, axis=1), np.stack(wm, axis=1)

    gains = [per_partition(a["g_pre"][0]), per_partition(a["g_post"][0])]
    gains += [per_partition(a["post_norm_g_2"][l]) for l in range(2)]
    gains += [per_partition(a["mem_norm_g_2"][l]) for l in range(2)]
    for l in range(2):
        gains += [per_partition(a[n][l]) for n in ("pre_norm_g_2", "q_norm_g_2", "kv_norm_g_2")]
        gains.append(a["conv_w_2"][l].reshape(3, 4, P).transpose(2, 1, 0).reshape(P, 12))

    row = np.arange(P)
    freq = (1.0 / (np.float32(10000.0) ** (np.arange(0, 64, 2, dtype=np.float32) / np.float32(64)))).astype(np.float32)
    slopes = (2.0 ** (-8.0 * np.arange(1, 33, dtype=np.float32) / 32)).astype(np.float32)
    consts = np.concatenate([
        np.eye(P, dtype=np.float32), np.ones((P, P), np.float32), np.broadcast_to(slopes, (P, 32)),
        freq[row % 32][:, None], np.where(row < 64, np.float32(np.pi / 2), np.float32(0))[:, None].astype(np.float32),
        np.where((row >= 64) & (row < 96), -1.0, 1.0)[:, None].astype(np.float32)], axis=1)
    dist = (row[:, None] + P - np.arange(2 * P)[None, :]).astype(np.float32)
    seen = (dist >= 0) & (dist < P)
    window = np.concatenate([np.where(seen & (np.arange(2 * P) >= P)[None, :], -dist, np.float32(-1e30))]
                            + [np.where(seen, -dist, np.float32(-1e30))] * 3, axis=1).astype(np.float32)

    arrays = {
        "xT": turned(a["x"][0]), "memT": turned(a["mem_2"][0]),
        "mem": np.ascontiguousarray(a["mem_2"][0].reshape(2, P, D).transpose(1, 0, 2)),
        "pos": a["positions_2"][0], "gains": np.concatenate(gains, axis=1), "sinks": a["sinks_a"][0],
        "consts": consts, "window": window, "w1": w1, "w2": w2, "wm": wm,
    }
    nc = bacc.Bacc("TRN2", target_bir_lowering=False, num_devices=1)
    send, aps = {}, []
    for name, x in arrays.items():
        send[name + "_dram"] = np.ascontiguousarray(x)
        aps.append(nc.dram_tensor(name + "_dram", x.shape, mybir.dt.from_np(x.dtype), kind="ExternalInput").ap())
    out = nc.dram_tensor("out_dram", (P, KT * S), mybir.dt.float32, kind="ExternalOutput").ap()
    build(nc, *aps, out)
    r = run_bass_kernel_spmd(nc, [send], core_ids=[0])
    y = np.asarray(r.results[0]["out_dram"]).reshape(P, KT, S)
    return np.ascontiguousarray(y.transpose(2, 1, 0).reshape(1, S, D))
```
